# Optimizing a Trainium2 kernel written in Bass

```python
import math
import jax, jax.numpy as jnp
from jax import lax
import numpy as np
import jax
import jax.numpy as jnp

D_MODEL = 1024
BATCH = 1
SEQ = 512
DEPTH = 2

N_MIXERS = 2
HEAD_DIM = 64
ATTN_HEADS = D_MODEL // HEAD_DIM
ATTN_WIDTH = ATTN_HEADS * HEAD_DIM
DILATED_GROUPS = ((128, 1), (512, 4), (2048, 16))
N_GROUPS_A = len(DILATED_GROUPS)
ATTN_IN_COLS = 3 * N_GROUPS_A * ATTN_WIDTH + ATTN_WIDTH
REL_BUCKETS = 32
REL_MAX_DIST = 2048
SSM_WIDTH = D_MODEL
SSM_GROUP = 16
SSM_N_GROUPS = SSM_WIDTH // SSM_GROUP
SSM_STATE = 64
N_ATTN_LAYERS = (DEPTH + 1) // 2
N_SSM_LAYERS = DEPTH // 2
EPS = 1e-6
NEG = -1e30


def rms_norm(x, g):
    xf = x.astype(jnp.float32)
    y = xf * lax.rsqrt(jnp.mean(xf * xf, axis=-1, keepdims=True) + EPS) * g.astype(jnp.float32)
    return y.astype(x.dtype)

def t5_bucket(dist):
    max_exact = REL_BUCKETS // 2
    n = jnp.maximum(dist, 1).astype(jnp.float32)
    large = max_exact + (jnp.log(n / max_exact) / math.log(REL_MAX_DIST / max_exact)
                         * (REL_BUCKETS - max_exact)).astype(jnp.int32)
    large = jnp.minimum(large, REL_BUCKETS - 1)
    return jnp.where(dist < max_exact, dist, large)

def dilated_group_attention(q, k, v, rel_bias, window, dilation):
    B, S, H, E = q.shape
    steps = window // dilation
    blk = steps
    L = S // dilation
    nb = -(-L // blk)
    Lp = nb * blk

    def to_sub(t):
        t = t.reshape(B, L, dilation, H, E)
        return jnp.pad(t, ((0, 0), (0, Lp - L), (0, 0), (0, 0), (0, 0)))

    qs = to_sub(q).reshape(B, nb, blk, dilation, H, E)
    front = ((0, 0), (blk, 0), (0, 0), (0, 0), (0, 0))
    ks = jnp.pad(to_sub(k), front).reshape(B, nb + 1, blk, dilation, H, E)
    vs = jnp.pad(to_sub(v), front).reshape(B, nb + 1, blk, dilation, H, E)
    kw = jnp.concatenate([ks[:, :-1], ks[:, 1:]], axis=2)
    vw = jnp.concatenate([vs[:, :-1], vs[:, 1:]], axis=2)

    i = jnp.arange(blk)[:, None]
    j = jnp.arange(2 * blk)[None, :]
    back = blk + i - j
    band = (back >= 0) & (back <= steps)
    valid = band[None] & ((jnp.arange(nb)[:, None, None] > 0) | (j[None] >= blk))
    bias = rel_bias[t5_bucket(jnp.maximum(back, 0) * dilation)]
    bias = jnp.transpose(bias, (2, 0, 1)).astype(jnp.float32)

    scale = HEAD_DIM ** -0.5
    logits = jnp.einsum('bnqrhe,bnkrhe->bnrhqk', qs, kw,
                        preferred_element_type=jnp.float32) * scale + bias
    logits = jnp.where(valid[None, :, None, None], logits, NEG)
    lse = jax.nn.logsumexp(logits, axis=-1)
    p = jnp.exp(logits - lse[..., None])
    o = jnp.einsum('bnrhqk,bnkrhe->bnqrhe', p.astype(v.dtype), vw)
    o = o.reshape(B, Lp, dilation, H, E)[:, :L].reshape(B, S, H, E)
    lse = jnp.transpose(lse, (0, 1, 4, 2, 3)).reshape(B, Lp, dilation, H)[:, :L].reshape(B, S, H)
    return o, lse

def dilated_attention_mixer(h, w_in, w_out, rel_bias):
    B, S, _ = h.shape
    proj = h @ w_in
    n_qkv = 3 * N_GROUPS_A * ATTN_WIDTH
    qkv = proj[..., :n_qkv].reshape(B, S, 3, N_GROUPS_A, ATTN_HEADS, HEAD_DIM)
    z = proj[..., n_qkv:]
    outs, lses = [], []
    for g, (window, dilation) in enumerate(DILATED_GROUPS):
        o, l = dilated_group_attention(qkv[:, :, 0, g], qkv[:, :, 1, g], qkv[:, :, 2, g],
                                       rel_bias, window, dilation)
        outs.append(o)
        lses.append(l)
    wts = jax.nn.softmax(jnp.stack(lses), axis=0)
    o = jnp.sum(wts[..., None] * jnp.stack(outs).astype(jnp.float32), axis=0)
    o = o.reshape(B, S, ATTN_WIDTH).astype(h.dtype)
    return (o * jax.nn.silu(z)) @ w_out

def s5_scan(u, a_re, a_im, log_dt, b_re, b_im, c_re, c_im, d_skip):
    B, S, _ = u.shape
    f = jnp.float32
    uf = u.astype(f).reshape(B, S, SSM_N_GROUPS, SSM_GROUP)
    A = lax.complex(a_re.astype(f), a_im.astype(f))
    dt = jnp.exp(log_dt.astype(f))[:, None]
    a_bar = jnp.exp(A * dt)
    Bm = lax.complex(b_re.astype(f), b_im.astype(f))
    b_bar = ((a_bar - 1.0) / A)[..., None] * Bm
    bu = jnp.einsum('bsgc,gpc->bsgp', uf.astype(jnp.complex64), b_bar)
    a_elems = jnp.broadcast_to(a_bar, bu.shape)

    def combine(left, right):
        return (right[0] * left[0], right[0] * left[1] + right[1])

    _, states = lax.associative_scan(combine, (a_elems, bu), axis=1)
    Cm = lax.complex(c_re.astype(f), c_im.astype(f))
    y = jnp.einsum('bsgp,gcp->bsgc', states, Cm).real
    y = y + d_skip.astype(f).reshape(SSM_N_GROUPS, SSM_GROUP) * uf
    return y.reshape(B, S, SSM_WIDTH).astype(u.dtype)

def s5_mixer(h, w_in, a_re, a_im, log_dt, b_re, b_im, c_re, c_im, d_skip, w_glu, b_glu, w_out):
    proj = h @ w_in
    u, z = proj[..., :SSM_WIDTH], proj[..., SSM_WIDTH:]
    y = s5_scan(u, a_re, a_im, log_dt, b_re, b_im, c_re, c_im, d_skip)
    g = jax.nn.gelu(y)
    y = g * jax.nn.sigmoid(g @ w_glu + b_glu)
    return (y * jax.nn.silu(z)) @ w_out

def first_inputs(seed: int = 0) -> dict:
    key = jax.random.key(seed)
    ks = jax.random.split(key, 24)
    nrm = jax.random.normal
    f = jnp.float32
    NA, NS, D = N_ATTN_LAYERS, N_SSM_LAYERS, D_MODEL
    G, P, C, E = SSM_N_GROUPS, SSM_STATE, SSM_GROUP, SSM_WIDTH
    x = nrm(ks[0], (BATCH, SEQ, D), f)
    rel_bias = 0.5 * nrm(ks[1], (REL_BUCKETS, ATTN_HEADS), f)
    attn_pre_norm = 1.0 + 0.05 * nrm(ks[2], (NA, D), f)
    attn_w_in = nrm(ks[3], (NA, D, ATTN_IN_COLS), f) * D ** -0.5
    attn_w_out = nrm(ks[4], (NA, ATTN_WIDTH, D), f) * ATTN_WIDTH ** -0.5
    attn_post_norm = 1.0 + 0.05 * nrm(ks[5], (NA, D), f)
    ssm_pre_norm = 1.0 + 0.05 * nrm(ks[6], (NS, D), f)
    ssm_w_in = nrm(ks[7], (NS, D, 2 * E), f) * D ** -0.5
    ssm_a_re = -0.5 + 0.01 * nrm(ks[8], (NS, G, P), f)
    ssm_a_im = math.pi * jnp.arange(P, dtype=f)[None, None, :] + 0.01 * nrm(ks[9], (NS, G, P), f)
    ssm_log_dt = jax.random.uniform(ks[10], (NS, G), f, math.log(1e-3), math.log(1e-1))
    ssm_b_re = nrm(ks[11], (NS, G, P, C), f) * (2 * C) ** -0.5
    ssm_b_im = nrm(ks[12], (NS, G, P, C), f) * (2 * C) ** -0.5
    ssm_c_re = nrm(ks[13], (NS, G, C, P), f) * (2 * P) ** -0.5
    ssm_c_im = nrm(ks[14], (NS, G, C, P), f) * (2 * P) ** -0.5
    ssm_d = nrm(ks[15], (NS, E), f)
    ssm_w_glu = nrm(ks[16], (NS, E, E), f) * E ** -0.5
    ssm_b_glu = 0.02 * nrm(ks[17], (NS, E), f)
    ssm_w_out = nrm(ks[18], (NS, E, D), f) * E ** -0.5
    ssm_post_norm = 1.0 + 0.05 * nrm(ks[19], (NS, D), f)
    return {"x": x, "rel_bias": rel_bias,
            "attn_pre_norm": attn_pre_norm, "attn_w_in": attn_w_in,
            "attn_w_out": attn_w_out, "attn_post_norm": attn_post_norm,
            "ssm_pre_norm": ssm_pre_norm, "ssm_w_in": ssm_w_in,
            "ssm_a_re": ssm_a_re, "ssm_a_im": ssm_a_im, "ssm_log_dt": ssm_log_dt,
            "ssm_b_re": ssm_b_re, "ssm_b_im": ssm_b_im,
            "ssm_c_re": ssm_c_re, "ssm_c_im": ssm_c_im, "ssm_d": ssm_d,
            "ssm_w_glu": ssm_w_glu, "ssm_b_glu": ssm_b_glu,
            "ssm_w_out": ssm_w_out, "ssm_post_norm": ssm_post_norm}

def first_block(x, rel_bias, attn_pre_norm, attn_w_in, attn_w_out, attn_post_norm,
              ssm_pre_norm, ssm_w_in, ssm_a_re, ssm_a_im, ssm_log_dt,
              ssm_b_re, ssm_b_im, ssm_c_re, ssm_c_im, ssm_d,
              ssm_w_glu, ssm_b_glu, ssm_w_out, ssm_post_norm):
    for i in range(DEPTH):
        j = i // N_MIXERS
        if i % N_MIXERS == 0:
            h = rms_norm(x, attn_pre_norm[j])
            h = dilated_attention_mixer(h, attn_w_in[j], attn_w_out[j], rel_bias)
            x = x + rms_norm(h, attn_post_norm[j])
        else:
            h = rms_norm(x, ssm_pre_norm[j])
            h = s5_mixer(h, ssm_w_in[j], ssm_a_re[j], ssm_a_im[j], ssm_log_dt[j],
                         ssm_b_re[j], ssm_b_im[j], ssm_c_re[j], ssm_c_im[j], ssm_d[j],
                         ssm_w_glu[j], ssm_b_glu[j], ssm_w_out[j])
            x = x + rms_norm(h, ssm_post_norm[j])
    return x


DEPTH_2 = 4

N_MIXERS_2 = 3
N_A = (DEPTH_2 + 2) // N_MIXERS_2
N_B = (DEPTH_2 + 1) // N_MIXERS_2
N_C = DEPTH_2 // N_MIXERS_2

DA_HEADS = 8
DA_HEAD_DIM = 64
DA_QK = 2 * DA_HEADS * DA_HEAD_DIM
DA_V = DA_HEADS * 2 * DA_HEAD_DIM
HG_EXPAND = 128
HG_HEADS = D_MODEL // HG_EXPAND
HG_KDIM = HG_EXPAND
HG_VDIM = D_MODEL // HG_HEADS
HG_FDIM = HG_HEADS * HG_KDIM
HG_CHUNK = 64
SW_Q_HEADS = 16
SW_KV_HEADS = 2
SW_HEAD_DIM = 64
SW_GROUP = SW_Q_HEADS // SW_KV_HEADS
SW_WINDOW = 128
SW_IN = SW_Q_HEADS * SW_HEAD_DIM + 2 * SW_KV_HEADS * SW_HEAD_DIM
N_BUCKETS = 32
MAX_DISTANCE = 128
N_BIAS_HEADS = 16
BLOCK = 128
D_FF = 4 * D_MODEL
PLE_DIM = 256
ALPHA = (2 * DEPTH_2) ** 0.25
BETA = (8 * DEPTH_2) ** -0.25
LN_EPS = 1e-5
RMS_EPS = 1e-6


def layer_norm(x, g, b):
    x32 = x.astype(jnp.float32)
    mu = jnp.mean(x32, axis=-1, keepdims=True)
    var = jnp.mean(jnp.square(x32 - mu), axis=-1, keepdims=True)
    y = (x32 - mu) * lax.rsqrt(var + LN_EPS) * g.astype(jnp.float32) + b.astype(jnp.float32)
    return y.astype(x.dtype)

def rms_norm_2(x, g):
    x32 = x.astype(jnp.float32)
    y = x32 * lax.rsqrt(jnp.mean(jnp.square(x32), axis=-1, keepdims=True) + RMS_EPS)
    return (y * g.astype(jnp.float32)).astype(x.dtype)

def t5_bucket_2(rel):
    n = jnp.maximum(rel, 0)
    max_exact = N_BUCKETS // 2
    nf = jnp.maximum(n, 1).astype(jnp.float32)
    large = max_exact + (jnp.log(nf / max_exact) / math.log(MAX_DISTANCE / max_exact)
                         * (N_BUCKETS - max_exact)).astype(jnp.int32)
    large = jnp.minimum(large, N_BUCKETS - 1)
    return jnp.where(n < max_exact, n, large)

def diff_attention(h, w_in, lam, subln, w_out, rel_bias, layer_idx):
    B, S, _ = h.shape
    H, d = DA_HEADS, DA_HEAD_DIM
    q, k, v = jnp.split(h @ w_in, [DA_QK, 2 * DA_QK], axis=-1)
    q = q.reshape(B, S, 2 * H, d).transpose(0, 2, 1, 3) * (d ** -0.5)
    k = k.reshape(B, S, 2 * H, d).transpose(0, 2, 1, 3)
    v = v.reshape(B, S, H, 2 * d).transpose(0, 2, 1, 3)
    lam_init = 0.8 - 0.6 * math.exp(-0.3 * layer_idx)
    lam32 = lam.astype(jnp.float32)
    lam_full = jnp.exp(jnp.sum(lam32[0] * lam32[1])) - jnp.exp(jnp.sum(lam32[2] * lam32[3])) + lam_init
    pos = jnp.arange(S, dtype=jnp.int32)
    outs = []
    for blk in range(S // BLOCK):
        qs = blk * BLOCK
        ke = qs + BLOCK
        s = jnp.einsum('bmqd,bmkd->bmqk', q[:, :, qs:ke], k[:, :, :ke]).astype(jnp.float32)
        rel = pos[qs:ke, None] - pos[None, :ke]
        bias = rel_bias[t5_bucket_2(rel)].astype(jnp.float32).transpose(2, 0, 1)
        s = jnp.where(rel >= 0, s + bias, -jnp.inf)
        a = jax.nn.softmax(s, axis=-1).reshape(B, H, 2, BLOCK, ke)
        a = a[:, :, 0] - lam_full * a[:, :, 1]
        outs.append(jnp.einsum('bhqk,bhkv->bhqv', a.astype(v.dtype), v[:, :, :ke]))
    o = jnp.concatenate(outs, axis=2)
    o = rms_norm_2(o, subln) * (1.0 - lam_init)
    o = o.transpose(0, 2, 1, 3).reshape(B, S, DA_V)
    return o @ w_out

def hgrn2(h, w_in, gnorm, w_out, lower_bound):
    B, S, _ = h.shape
    H, dk, dv, C = HG_HEADS, HG_KDIM, HG_VDIM, HG_CHUNK
    q, f, i, g = jnp.split(h @ w_in, 4, axis=-1)
    q = jax.nn.silu(q.astype(jnp.float32))
    lb = lower_bound.astype(jnp.float32)
    f = lb + (1.0 - lb) * jax.nn.sigmoid(f.astype(jnp.float32))
    logf = jnp.log(f)
    kin = 1.0 - f

    def to_chunks(t, dim):
        return t.reshape(B, S // C, C, H, dim).transpose(1, 0, 3, 2, 4)

    qc, kc, gc = to_chunks(q, dk), to_chunks(kin, dk), to_chunks(logf, dk)
    vc = to_chunks(i.astype(jnp.float32), dv)
    causal = jnp.tril(jnp.ones((C, C), dtype=bool))

    def step(state, inp):
        q_, k_, v_, g_ = inp
        G = jnp.cumsum(g_, axis=2)
        G_last = G[:, :, -1:, :]
        o_inter = jnp.einsum('bhtk,bhkv->bhtv', q_ * jnp.exp(G), state)
        diff = G[:, :, :, None, :] - G[:, :, None, :, :]
        decay = jnp.exp(jnp.where(causal[:, :, None], diff, -jnp.inf))
        A = jnp.einsum('bhtk,bhsk,bhtsk->bhts', q_, k_, decay)
        o = o_inter + jnp.einsum('bhts,bhsv->bhtv', A, v_)
        new_state = (jnp.exp(G_last[:, :, 0, :])[..., None] * state
                     + jnp.einsum('bhsk,bhsv->bhkv', k_ * jnp.exp(G_last - G), v_))
        return new_state, o

    s0 = jnp.zeros((B, H, dk, dv), jnp.float32)
    _, o = lax.scan(step, s0, (qc, kc, vc, gc))
    o = o.transpose(1, 0, 3, 2, 4).reshape(B, S, H, dv)
    o = rms_norm_2(o, gnorm) * jax.nn.silu(g.astype(jnp.float32).reshape(B, S, H, dv))
    o = o.reshape(B, S, H * dv).astype(h.dtype)
    return o @ w_out

def swa_sink_attention(h, w_in, sinks, w_out, rel_bias):
    B, S, _ = h.shape
    Hq, Hk, G, d, W = SW_Q_HEADS, SW_KV_HEADS, SW_GROUP, SW_HEAD_DIM, BLOCK
    NB = S // W
    q, k, v = jnp.split(h @ w_in, [Hq * d, Hq * d + Hk * d], axis=-1)
    q = q.reshape(B, NB, W, Hk, G, d) * (d ** -0.5)
    k = k.reshape(B, NB, W, Hk, d)
    v = v.reshape(B, NB, W, Hk, d)

    def prev_block(t):
        return jnp.concatenate([jnp.zeros_like(t[:, :1]), t[:, :-1]], axis=1)

    kb = jnp.concatenate([prev_block(k), k], axis=2)
    vb = jnp.concatenate([prev_block(v), v], axis=2)
    s = jnp.einsum('bnqhgd,bnkhd->bnhgqk', q, kb).astype(jnp.float32)
    qi = jnp.arange(W, dtype=jnp.int32)[:, None]
    kj = jnp.arange(2 * W, dtype=jnp.int32)[None, :]
    rel = qi + W - kj
    bias = rel_bias[t5_bucket_2(rel)].astype(jnp.float32).transpose(2, 0, 1).reshape(Hk, G, W, 2 * W)
    in_window = (rel >= 0) & (rel < SW_WINDOW)
    key_valid = (jnp.arange(NB, dtype=jnp.int32)[:, None, None] * W + kj[None] - W) >= 0
    mask = in_window[None] & key_valid
    s = jnp.where(mask[None, :, None, None], s + bias, -jnp.inf)
    sink = sinks.astype(jnp.float32).reshape(Hk, G)[None, None, :, :, None, None]
    m = jnp.maximum(jnp.max(s, axis=-1, keepdims=True), sink)
    e = jnp.exp(s - m)
    a = e / (jnp.sum(e, axis=-1, keepdims=True) + jnp.exp(sink - m))
    o = jnp.einsum('bnhgqk,bnkhd->bnqhgd', a.astype(vb.dtype), vb).reshape(B, S, Hq * d)
    return o @ w_out

def second_inputs(seed: int = 0) -> dict:
    key = jax.random.key(seed)
    ks = jax.random.split(key, 24)
    f32 = jnp.float32
    D = D_MODEL

    def nrm(k, shape, scale):
        return jax.random.normal(k, shape, f32) * scale

    return {
        "x": nrm(ks[0], (BATCH, SEQ, D), 1.0),
        "p": nrm(ks[1], (DEPTH_2, BATCH, SEQ, PLE_DIM), 1.0),
        "rel_bias": nrm(ks[2], (N_BUCKETS, N_BIAS_HEADS), 0.5),
        "hg_lower_bound": nrm(ks[3], (DEPTH_2, HG_FDIM), 0.1),
        "da_w_in": nrm(ks[4], (N_A, D, 2 * DA_QK + DA_V), D ** -0.5),
        "da_lambda": nrm(ks[5], (N_A, 4, DA_HEAD_DIM), 0.1),
        "da_subln": 1.0 + nrm(ks[6], (N_A, 2 * DA_HEAD_DIM), 0.02),
        "da_w_out": nrm(ks[7], (N_A, DA_V, D), DA_V ** -0.5 * BETA),
        "hg_w_in": nrm(ks[8], (N_B, D, 2 * HG_FDIM + 2 * D), D ** -0.5),
        "hg_gnorm": 1.0 + nrm(ks[9], (N_B, HG_VDIM), 0.02),
        "hg_w_out": nrm(ks[10], (N_B, D, D), D ** -0.5 * BETA),
        "sw_w_in": nrm(ks[11], (N_C, D, SW_IN), D ** -0.5),
        "sw_sinks": nrm(ks[12], (N_C, SW_Q_HEADS), 0.5),
        "sw_w_out": nrm(ks[13], (N_C, SW_Q_HEADS * SW_HEAD_DIM, D), (SW_Q_HEADS * SW_HEAD_DIM) ** -0.5 * BETA),
        "ln_g": 1.0 + nrm(ks[14], (DEPTH_2, 2, D), 0.02),
        "ln_b": nrm(ks[15], (DEPTH_2, 2, D), 0.02),
        "w_up": nrm(ks[16], (DEPTH_2, D, D_FF), D ** -0.5),
        "w_down": nrm(ks[17], (DEPTH_2, D_FF, D), D_FF ** -0.5 * BETA),
        "w_ple": nrm(ks[18], (DEPTH_2, PLE_DIM, D), PLE_DIM ** -0.5 * 0.5),
        "w_ple_gate": nrm(ks[19], (DEPTH_2, D, D), D ** -0.5),
    }

def second_block(x, p, rel_bias, hg_lower_bound, da_w_in, da_lambda, da_subln, da_w_out,
              hg_w_in, hg_gnorm, hg_w_out, sw_w_in, sw_sinks, sw_w_out,
              ln_g, ln_b, w_up, w_down, w_ple, w_ple_gate):
    lb_sm = jax.nn.softmax(hg_lower_bound.astype(jnp.float32), axis=0)
    lb_all = jnp.cumsum(lb_sm, axis=0) - lb_sm[0]
    h = x
    for i in range(DEPTH_2):
        kind, j = i % N_MIXERS_2, i // N_MIXERS_2
        if kind == 0:
            y = diff_attention(h, da_w_in[j], da_lambda[j], da_subln[j], da_w_out[j], rel_bias, i)
        elif kind == 1:
            y = hgrn2(h, hg_w_in[j], hg_gnorm[j], hg_w_out[j], lb_all[i])
        else:
            y = swa_sink_attention(h, sw_w_in[j], sw_sinks[j], sw_w_out[j], rel_bias)
        h = layer_norm(ALPHA * h + y, ln_g[i, 0], ln_b[i, 0])
        u = jnp.square(jax.nn.relu(h @ w_up[i])) @ w_down[i]
        h = layer_norm(ALPHA * h + u, ln_g[i, 1], ln_b[i, 1])
        h = h + jax.nn.sigmoid(h @ w_ple_gate[i]) * (p[i] @ w_ple[i])
    return h


def setup_inputs(seed=0):
    out = dict(first_inputs(seed))
    for name, value in second_inputs(seed + 1).items():
        if name != "x":
            out[name + "_2"] = value
    return out


def reference(
    x, rel_bias, attn_pre_norm, attn_w_in, attn_w_out, attn_post_norm, ssm_pre_norm, ssm_w_in,
    ssm_a_re, ssm_a_im, ssm_log_dt, ssm_b_re, ssm_b_im, ssm_c_re, ssm_c_im, ssm_d, ssm_w_glu,
    ssm_b_glu, ssm_w_out, ssm_post_norm, p_2, rel_bias_2, hg_lower_bound_2, da_w_in_2,
    da_lambda_2, da_subln_2, da_w_out_2, hg_w_in_2, hg_gnorm_2, hg_w_out_2, sw_w_in_2,
    sw_sinks_2, sw_w_out_2, ln_g_2, ln_b_2, w_up_2, w_down_2, w_ple_2, w_ple_gate_2,
):
    x = first_block(
        x, rel_bias, attn_pre_norm, attn_w_in, attn_w_out, attn_post_norm, ssm_pre_norm,
        ssm_w_in, ssm_a_re, ssm_a_im, ssm_log_dt, ssm_b_re, ssm_b_im, ssm_c_re, ssm_c_im, ssm_d,
        ssm_w_glu, ssm_b_glu, ssm_w_out, ssm_post_norm,
    )
    return second_block(
        x, p_2, rel_bias_2, hg_lower_bound_2, da_w_in_2, da_lambda_2, da_subln_2, da_w_out_2,
        hg_w_in_2, hg_gnorm_2, hg_w_out_2, sw_w_in_2, sw_sinks_2, sw_w_out_2, ln_g_2, ln_b_2,
        w_up_2, w_down_2, w_ple_2, w_ple_gate_2,
    )


_drawn_inputs = setup_inputs


def setup_inputs(seed=0):
    import zlib

    import numpy as np

    out = dict(_drawn_inputs(seed))
    spreads = {}
    factors = {'ssm_a_re': 8.0,
     'ssm_b_glu': 8.0,
     'hg_lower_bound_2': 8.0,
     'da_subln_2': 8.0,
     'hg_gnorm_2': 8.0,
     'sw_sinks_2': 8.0}
    for name, (base, spread) in spreads.items():
        noise = np.random.default_rng([zlib.crc32(name.encode()), seed]).standard_normal(out[name].shape)
        drawn = base * np.exp(spread * noise) if base else spread * noise
        out[name] = jnp.asarray(drawn.astype(out[name].dtype))
    for name, factor in factors.items():
        out[name] = (out[name] * factor).astype(out[name].dtype)
    return out
```

```python
import math
from contextlib import ExitStack

import numpy as np
import concourse.bass as bass
from concourse import mybir

F32 = mybir.dt.float32
F32R = mybir.dt.float32r
I32 = mybir.dt.int32
ALU = mybir.AluOpType
ACT = mybir.ActivationFunctionType
AX = mybir.AxisListType

STAGES = ("attn", "ssm", "layer0", "layer1", "layer2", "layer3")

P = 128
S = 512
D = 1024
TT = S // P
KT = D // P
CHUNK = 2048
RAW = 2
SPLIT = 2
CREDIT = 8
NEG = -1e30
N_LAYERS = 4
ALPHA = (2 * N_LAYERS) ** 0.25
HEADS = 16
RMS_EPS = 1e-6
LN_EPS = 1e-5
SSM_T = 8
SSM_N = S // SSM_T
SSM_PAIRS = 32
SSM_C = 16
HG_LEVELS = 7
SW_ORDER = [h for j in range(4) for h in (2 * j, 2 * j + 1, 8 + 2 * j, 9 + 2 * j)]


def f_chunks(w):
    n = w.shape[1] // 256
    return w.reshape(KT, P, n, 256).transpose(2, 1, 0, 3).reshape(n, P, CHUNK)


def t_chunks(w):
    k, n = w.shape
    return w.reshape(k // 512, 4, P, n // 512, 512).transpose(3, 0, 2, 1, 4).reshape(-1, P, CHUNK)


def attn_chunks(w):
    qkv = w[:, :9216].reshape(D, 3, 3, 8, P)
    z = w[:, 9216:].reshape(D, 8, P)
    out = []
    for i in range(4):
        cols = []
        for p in (2 * i, 2 * i + 1):
            qk = [[qkv[:, 0, g, p], qkv[:, 1, g, p]] for g in range(3)]
            cols += [qkv[:, 2, 0, p], qkv[:, 2, 1, p]] + qk[0]
            cols += [z[:, p], z[:, p + 1]] if p == 2 * i else []
            cols += qk[1]
            cols += [qkv[:, 2, 2, p], qkv[:, 2, 2, p + 1]] if p == 2 * i else []
            cols += qk[2]
        out.append(f_chunks(np.concatenate(cols, axis=1)))
    return np.concatenate(out)


def da_chunks(w):
    q, k, v = (w[:, 1024 * j:1024 * (j + 1)].reshape(D, 8, P) for j in range(3))
    out = []
    for i in range(4):
        a, b = 2 * i, 2 * i + 1
        out.append(f_chunks(np.concatenate([q[:, a], k[:, a], q[:, b], k[:, b], v[:, a], v[:, b]], axis=1)))
    return np.concatenate(out)


def sw_chunks(w):
    q, k, v = w[:, :1024].reshape(D, 16, 64), w[:, 1024:1152], w[:, 1152:]
    cols = [k[:, :64], k[:, :64], k[:, 64:], k[:, 64:], v, v, q[:, SW_ORDER].reshape(D, 1024)]
    return f_chunks(np.concatenate(cols, axis=1))


def layer_rest_chunks(wo, up, down, gate, ple):
    parts = [t_chunks(wo)]
    for q in range(4):
        parts += [f_chunks(up[:, 1024 * q:1024 * (q + 1)]), t_chunks(down[1024 * q:1024 * (q + 1)])]
    parts += [t_chunks(gate), ple.reshape(2, P, D).transpose(1, 0, 2).reshape(1, P, CHUNK)]
    return np.concatenate(parts)


def pack_weights(i):
    g = lambda n: np.asarray(i[n])
    parts = []
    if "attn" in STAGES:
        parts += [attn_chunks(g("attn_w_in")[0]), t_chunks(g("attn_w_out")[0])]
    if "ssm" in STAGES:
        parts += [f_chunks(g("ssm_w_in")[0]), f_chunks(g("ssm_w_glu")[0]), t_chunks(g("ssm_w_out")[0])]
    for layer in range(N_LAYERS):
        if f"layer{layer}" not in STAGES:
            continue
        kind, j = layer % 3, layer // 3
        if kind == 0:
            parts.append(da_chunks(g("da_w_in_2")[j]))
            wo = g("da_w_out_2")[j]
        elif kind == 1:
            w = g("hg_w_in_2")[j]
            parts += [f_chunks(w[:, :2048]), t_chunks(w[:, 2048:])]
            wo = g("hg_w_out_2")[j]
        else:
            parts.append(sw_chunks(g("sw_w_in_2")[j]))
            wo = g("sw_w_out_2")[j].reshape(16, 64, D)[SW_ORDER].reshape(D, D)
        parts.append(layer_rest_chunks(wo, g("w_up_2")[layer], g("w_down_2")[layer], g("w_ple_gate_2")[layer], g("w_ple_2")[layer]))
    return np.ascontiguousarray(np.concatenate(parts))


def bucket(dist, max_dist):
    n = max(dist, 1)
    if dist < 16:
        return dist
    return min(16 + int(math.log(n / 16) / math.log(max_dist / 16) * 16), 31)


def one_hot(width, back_of, valid, max_dist):
    m = np.zeros((33, width), np.float32)
    for y in range(width):
        back = back_of(y)
        if valid(back):
            m[bucket(back, max_dist), y] = 1.0
        else:
            m[32, y] = NEG
    return m


W1, W2 = 256, 128
L1, L2 = W1 + P - 1, W2 + P - 1
LA = L1 + 2 * L2
WD, WS = 512, 256
LD_, LS = WD + P - 1, WS + P - 1
LB = LD_ + LS


def bias_constants():
    a = [one_hot(L1, lambda y: P + P - 1 - y, lambda b: 0 <= b <= P, 2048),
         one_hot(L2, lambda y: 4 * (P - 1 - y), lambda b: b >= 0, 2048),
         one_hot(L2, lambda y: 4 * (P - 1 - y), lambda b: b >= 0 and b % 16 == 0, 2048)]
    b = [one_hot(LD_, lambda y: 3 * P + P - 1 - y, lambda b: b >= 0, 128),
         one_hot(LS, lambda y: P + P - 1 - y, lambda b: 0 <= b < P, 128)]
    return np.concatenate(a, axis=1), np.concatenate(b, axis=1)


def hg_masks():
    m = np.zeros((P, HG_LEVELS + 1, P), np.int32)
    for lev in range(HG_LEVELS):
        c = P >> (lev + 1)
        for s in range(P):
            if (s // c) % 2 == 0:
                t0 = (s // c + 1) * c
                m[s, lev, t0:t0 + c] = 1
    m[np.arange(P), HG_LEVELS, np.arange(P)] = 1
    return m


def head_select():
    m = np.zeros((HEADS, 8, P), np.float32)
    for h in range(HEADS):
        m[h, h // 2, 64 * (h % 2):64 * (h % 2) + 64] = 1.0
    return m


class Signal:

    def __init__(self, handle, base=0):
        self.h, self.base = handle, base


class InOrder:

    def __init__(self, eng, sig):
        self.eng, self.sig, self.start, self.k, self.per = eng, sig, 0, 0, None

    def __call__(self, ins):
        self.k += 1
        ins.then_inc(self.sig.h, 1)
        self.eng.wait_ge(self.sig.h, self.sig.base + self.start + self.k)

    def enter(self, i, per):
        self.before, self.per, self.k0 = self.start + self.k, per, self.k
        self.start, self.k = self.before + i * per, 0

    def leave(self, n):
        assert self.k == self.per, f"links per pass: {self.k}, not {self.per}"
        self.start, self.k = self.before + n * self.per, 0

    def done(self):
        self.sig.base += self.start + self.k


def build(nc, t, out):
    ctx = ExitStack()
    with ctx:
        taken = {}

        def sb(name, shape, dt=F32, c=ctx):
            taken[name] = taken.get(name, 0) + 1
            return c.enter_context(nc.sbuf_tensor(name if taken[name] == 1 else f"{name}_{taken[name]}", shape, dt))

        def signal(name, base=0):
            s = Signal(ctx.enter_context(nc.semaphore(name)), base)
            if base:
                credited.append(s)
            return s

        credited = []
        NCH = t["weights"].shape[0]
        X = sb("X", [P, TT, D])
        XTh = sb("XTh", [P, KT, S], F32R)
        XTl = sb("XTl", [P, KT, S], F32R)
        Y = sb("Y", [P, TT, D])
        YF = Y[:, :, :].rearrange("p a b -> p (a b)").rearrange("p (k s) -> p k s", k=KT)
        raw = [sb(f"raw{i}", [P, CHUNK]) for i in range(RAW)]
        wh = [sb(f"wh{i}", [P, CHUNK], F32R) for i in range(SPLIT)]
        wl = [sb(f"wl{i}", [P, CHUNK], F32R) for i in range(SPLIT)]
        ident = sb("ident", [P, P])
        zero = sb("zero", [P, 1])
        mhalf = sb("mhalf", [P, 1])
        col = sb("col", [P, 64])
        st = sb("st", [P, 96])
        PS = [ctx.enter_context(nc.psum_tensor(f"bank{i}", [P, 512], F32)) for i in range(8)]

        raw_in = [signal(f"raw_in{i}") for i in range(RAW)]
        w_split = signal("w_split")
        w_high = signal("w_high")
        w_used = signal("w_used", CREDIT)
        tile_done = signal("tile_done")
        tile_free = signal("tile_free", CREDIT)
        tile2_done = signal("tile2_done")
        tile2_free = signal("tile2_free", CREDIT)
        a_b = signal("act_to_dve")
        b_a = signal("dve_to_act")
        b_p = signal("dve_to_pe")
        b_g = signal("dve_to_pool")
        g_b = signal("pool_to_dve")
        a_p = signal("act_to_pe")
        p_a = signal("pe_to_act")
        p_b = signal("pe_to_dve")
        loaded = signal("loaded")
        stored = signal("stored")
        dve_order, act_order, pool_order = signal("dve_order"), signal("act_order"), signal("pool_order")
        split_free = signal("split_free", CREDIT)
        sigs = dict(sc_done=signal("scores_done"), sc_free=signal("scores_free", CREDIT), sbias=signal("biased"),
                    pexp=signal("exp_done"), pnorm=signal("probs_done"), tr=signal("probs_transposed", CREDIT),
                    pt=signal("probsT_copied", CREDIT), pv=signal("pv_done", CREDIT), oev=signal("pv_free", CREDIT),
                    bias_in=signal("bias_in"), bias_used=signal("bias_used", CREDIT), proj=signal("proj_done"),
                    pev=signal("proj_free", CREDIT))

        bias_a = nc.dram_tensor("bias_a", (HEADS, P, 512), F32, kind="Internal").ap()
        bias_d = nc.dram_tensor("bias_d", (HEADS, P, WD), F32, kind="Internal").ap()
        bias_s = nc.dram_tensor("bias_s", (HEADS, P, WS), F32, kind="Internal").ap()

        pos = [0]

        def load_chunk(sp, c, slot):
            sp.wait_ge(w_split.h, c - RAW + 1)
            sp.dma_start(raw[slot][:, :], t["weights"][bass.ds(c, 1)].rearrange("a p n -> p (a n)")).then_inc(raw_in[slot].h, 16)

        def split_chunk(pool, c, r, s):
            pool.wait_ge(w_used.h, CREDIT + c - SPLIT + 1)
            pool.wait_ge(raw_in[r].h, 16 * ((c - r) // RAW + 1) if isinstance(c, int) else (c - r) * (16 // RAW) + 16)
            pool.tensor_tensor(wh[s][:, :], raw[r][:, :], zero[:, :].to_broadcast([P, CHUNK]), ALU.add).then_inc(w_high.h, 1)
            pool.wait_ge(w_high.h, c + 1)
            pool.tensor_tensor(wl[s][:, :], raw[r][:, :], wh[s][:, :].bitcast(F32), ALU.subtract).then_inc(w_split.h, 1)

        def stream(eng, first, last, unit, one):
            last = min(last, NCH)
            n = (last - first) // unit
            if n >= 2:
                with eng.Fori(0, n) as i:
                    for j in range(unit):
                        one(i * unit + (first + j), first + j)
                first += n * unit
            for c in range(first, last):
                one(c, c)

        def sp_stream(sp, n):
            a = pos[0] + SPLIT + RAW
            stream(sp, a, a + n, RAW, lambda c, k: load_chunk(sp, c, k % RAW))

        def pool_stream(pool, n):
            a = pos[0] + SPLIT
            stream(pool, a, a + n, 2, lambda c, k: split_chunk(pool, c, k % RAW, k % SPLIT))

        def arrived(pe, c):
            pe.wait_ge(w_split.h, c + 1)

        def three(psum, hi_pairs, first, last):
            (sh, sl), (mh, ml) = hi_pairs
            nc.tensor.matmul(psum, sh, mh, start=first, stop=False)
            nc.tensor.matmul(psum, sl, mh, start=False, stop=False)
            return nc.tensor.matmul(psum, sh, ml, start=False, stop=last)

        def f_tile(psum, slot, m, xh=XTh, xl=XTl):
            for k in range(KT):
                c = slice(256 * k + P * m, 256 * k + P * m + P)
                last = three(psum, ((wh[slot][:, c], wl[slot][:, c]), (xh[:, k, :], xl[:, k, :])), k == 0, k == KT - 1)
            return last

        def v_tile(psum, slot, c0, n, tok):
            for k in range(KT):
                c = slice(256 * k + c0, 256 * k + c0 + n)
                last = three(psum, ((tok(XTh, k), tok(XTl, k)), (wh[slot][:, c], wl[slot][:, c])), k == 0, k == KT - 1)
            return last

        def t_tile(psum, slot, kks, xs, tok, first, last, width=512, c0=0, step=512):
            xh, xl = xs
            for n, (kk, k) in enumerate(kks):
                c = slice(step * kk + c0, step * kk + c0 + width)
                r = three(psum, ((tok(xh, k), tok(xl, k)), (wh[slot][:, c], wl[slot][:, c])),
                          first and n == 0, last and n == len(kks) - 1)
            return r

        def natural(tt):
            return lambda x, k: x[:, k, P * tt:P * tt + P]

        def setup():
            with ExitStack() as c:
                oh_a = sb("oh_a", [33, LA], F32, c)
                oh_b = sb("oh_b", [33, LB], F32, c)
                rb = sb("rb", [33, 2 * HEADS], F32, c)
                ta = sb("ta", [HEADS, LA], F32, c)
                tb = sb("tb", [HEADS, LB], F32, c)
                made = signal("made")
                tables = signal("tables")
                with nc.Block() as block:
                    @block.sync
                    def _(sp):
                        for k in range(min(RAW, NCH)):
                            sp.dma_start(raw[k][:, :], t["weights"][k]).then_inc(raw_in[k].h, 16)
                        for k in range(RAW, min(RAW + SPLIT, NCH)):
                            load_chunk(sp, k, k % RAW)

                    @block.gpsimd
                    def _(pool):
                        link = InOrder(pool, pool_order)
                        link(pool.memset(zero[:, :], 0.0))
                        link(pool.memset(mhalf[:, :], -0.5))
                        link(pool.memset(ident[:, :], 0.0))
                        pool.memset(rb[32:33, :], 1.0).then_inc(made.h, 1)
                        pool.wait_ge(made.h, 1)
                        pool.affine_select(out=ident[:, :], in_=ident[:, :], compare_op=ALU.not_equal, fill=1.0,
                                           base=0, pattern=[[-1, P]], channel_multiplier=1).then_inc(made.h, 1)
                        pool.wait_ge(made.h, 2)
                        link.done()
                        for s in credited:
                            pool.sem_inc(s.h, CREDIT)
                        for k in range(min(SPLIT, NCH)):
                            pool.wait_ge(raw_in[k % RAW].h, 16 * (k // RAW + 1))
                            pool.tensor_tensor(wh[k][:, :], raw[k % RAW][:, :], zero[:, :].to_broadcast([P, CHUNK]), ALU.add).then_inc(w_high.h, 1)
                            pool.wait_ge(w_high.h, k + 1)
                            pool.tensor_tensor(wl[k][:, :], raw[k % RAW][:, :], wh[k][:, :].bitcast(F32), ALU.subtract).then_inc(w_split.h, 1)

                    @block.scalar
                    def _(act):
                        for d, s in ((oh_a[:, :], t["onehot_a"]), (oh_b[:, :], t["onehot_b"]),
                                     (rb[0:32, 0:HEADS], t["rel_bias"]), (rb[0:32, HEADS:], t["rel_bias_2"]),
                                     (X[:, :, :], t["x"].rearrange("b (t p) d -> p (b t) d", p=P)),
                                     (col[:, 0:KT], t["attn_pre_norm"]), (col[:, KT:2 * KT], t["ssm_pre_norm"]),
                                     (col[:, 16:18], t["da_subln_2"]), (col[:, 18:19], t["hg_gnorm_2"])):
                            act.dma_start(d, s).then_inc(loaded.h, 16)
                        act.wait_ge(tables.h, 4)

                        def toeplitz(dst, table, off, w):
                            x = table[:, off:off + w]
                            src = bass.AP(x.tensor, x.offset + P - 1, [list(x.ap[0]), [-1, P], [1, w]])
                            act.dma_start(dst, src).then_inc(stored.h, 16)
                        toeplitz(bias_a[:, :, 0:W1], ta, 0, W1)
                        toeplitz(bias_a[:, :, W1:384], ta, L1, W2)
                        toeplitz(bias_a[:, :, 384:512], ta, L1 + L2, W2)
                        toeplitz(bias_d, tb, 0, WD)
                        toeplitz(bias_s, tb, LD_, WS)
                        act.wait_ge(stored.h, 16 * 5)
                        act.wait_ge(loaded.h, 16 * 9)

                    @block.tensor
                    def _(pe):
                        pe.wait_ge(loaded.h, 16 * 9)
                        pe.wait_ge(made.h, 2)
                        for n, (o, lo, hi, r) in enumerate(((oh_a, 0, 512, 0), (oh_a, 512, LA, 0), (oh_b, 0, 512, 1), (oh_b, 512, LB, 1))):
                            nc.tensor.matmul(PS[n][0:HEADS, 0:hi - lo], rb[:, HEADS * r:HEADS * r + HEADS], o[:, lo:hi],
                                             start=True, stop=True).then_inc(p_b.h, 1)

                    @block.vector
                    def _(dve):
                        for n, (o, lo, hi) in enumerate(((ta, 0, 512), (ta, 512, LA), (tb, 0, 512), (tb, 512, LB))):
                            dve.wait_ge(p_b.h, n + 1)
                            nc.vector.tensor_copy(o[:, lo:hi], PS[n][0:HEADS, 0:hi - lo]).then_inc(tables.h, 1)
                stored.base += 16 * 5
                loaded.base += 16 * 9
                p_b.base += 4

        def norm_phase(kind, gain=None, vecs=(), extra=None, transposed=True, last=False):
            with ExitStack() as c:
                N = sb("N", [P, TT, D], F32, c) if kind in ("pre", "heads", "rms_add") else None
                bc = [sb(f"bc{i}", [P, D], F32, c) for i in range(2)]
                tmp = [sb(f"tmp{i}", [P, 512], F32, c) for i in range(2)]
                src = {"pre": N, "plain": X, "ln": X, "rms_add": X, "heads": N}[kind]
                ready, sums = b_p, a_b
                n_vec = len(vecs)
                with nc.Block() as block:
                    @block.sync
                    def _(sp):
                        for n, v in enumerate(vecs):
                            sp.dma_start(bc[n][:, :], v.partition_broadcast(P)).then_inc(loaded.h, 16)
                        if last:
                            for tt in range(TT):
                                sp.wait_ge(b_p.h, b_p.base + tt + 1)
                                sp.dma_start(out[0, P * tt:P * tt + P, :], X[:, tt, :]).then_inc(stored.h, 16)
                            sp.wait_ge(stored.h, stored.base + 16 * TT)

                    @block.gpsimd
                    def _(pool):
                        p = nc.gpsimd
                        link = InOrder(pool, pool_order)

                        def rsqrt(x, scale, eps):
                            link(p.tensor_scalar(x, x, scale, eps, ALU.mult, ALU.add))
                            return p.tensor_tensor(x, x, mhalf[:, :].to_broadcast([P, x.shape[1]]), ALU.pow)
                        for tt in range(TT if kind != "plain" else 0):
                            if kind in ("pre", "rms_add"):
                                pool.wait_ge(sums.h, sums.base + tt + 1)
                                rsqrt(st[:, tt:tt + 1], 1.0, RMS_EPS).then_inc(g_b.h, 1)
                            elif kind == "ln":
                                pool.wait_ge(b_g.h, b_g.base + tt + 1)
                                rsqrt(st[:, 33:34], 1.0, LN_EPS).then_inc(g_b.h, 1)
                            else:
                                pool.wait_ge(b_g.h, b_g.base + tt + 1)
                                link(rsqrt(st[:, 40:48], 1.0 / P, RMS_EPS))
                                p.tensor_scalar(st[:, 40:48], st[:, 40:48], extra["post"], None, ALU.mult).then_inc(g_b.h, 1)
                        link.done()

                    @block.scalar
                    def _(act):
                        if kind in ("pre", "rms_add"):
                            for tt in range(TT):
                                z = X if kind == "pre" else Y
                                nc.scalar.activation(N[:, tt, :], z[:, tt, :], ACT.Square, scale=D ** -0.5,
                                                     accum_out=st[:, tt:tt + 1]).then_inc(sums.h, 1)
                        elif kind == "heads":
                            for tt in range(TT):
                                nc.scalar.activation(N[:, tt, :], Y[:, tt, :], ACT.Square).then_inc(sums.h, 1)
                        if transposed:
                            for n in range(2 * TT):
                                tt, half = n // 2, n % 2
                                if gain is None:
                                    act.wait_ge(p_a.h, p_a.base + n + 1)
                                    s = PS[n % 4][:, :]
                                else:
                                    act.wait_ge(b_a.h, b_a.base + n + 1)
                                    s = tmp[n % 2][:, :]
                                nc.scalar.activation(XTh[:, 4 * half:4 * half + 4, P * tt:P * tt + P],
                                                     s.rearrange("p (k c) -> p k c", k=4), ACT.Copy).then_inc(a_p.h, 1)

                    @block.vector
                    def _(dve):
                        link = InOrder(dve, dve_order)
                        v = nc.vector

                        def low(n):
                            tt, half = n // 2, n % 2
                            if gain is None:
                                s = PS[n % 4][:, :]
                            else:
                                dve.wait_ge(p_a.h, p_a.base + n + 1)
                                s = tmp[n % 2][:, :]
                                g = gain[:, 4 * half:4 * half + 4] if gain.shape[1] > 1 else gain
                                g = g.unsqueeze(2).to_broadcast([P, 4, P]) if gain.shape[1] > 1 else g.unsqueeze(2).to_broadcast([P, 4, P])
                                v.tensor_tensor(s.rearrange("p (k c) -> p k c", k=4),
                                                PS[n % 4][:, :].rearrange("p (k c) -> p k c", k=4), g, ALU.mult).then_inc(b_a.h, 1)
                            dve.wait_ge(a_p.h, a_p.base + n + 1)
                            v.tensor_tensor(XTl[:, 4 * half:4 * half + 4, P * tt:P * tt + P],
                                            s.rearrange("p (k c) -> p k c", k=4),
                                            XTh[:, 4 * half:4 * half + 4, P * tt:P * tt + P].bitcast(F32),
                                            ALU.subtract).then_inc(tile2_free.h, 1)

                        if n_vec:
                            dve.wait_ge(loaded.h, loaded.base + 16 * n_vec)
                        for tt in range(TT):
                            if kind == "pre":
                                dve.wait_ge(g_b.h, g_b.base + tt + 1)
                                r = st[:, tt:tt + 1]
                                v.tensor_scalar(N[:, tt, :], X[:, tt, :], r, None, ALU.mult).then_inc(ready.h, 1)
                            elif kind == "plain":
                                dve.sem_inc(ready.h, 1)
                            elif kind == "rms_add":
                                dve.wait_ge(g_b.h, g_b.base + tt + 1)
                                r = st[:, tt:tt + 1]
                                link(v.scalar_tensor_tensor(N[:, tt, :], Y[:, tt, :], r, bc[0][:, :], ALU.mult, ALU.mult))
                                v.tensor_tensor(X[:, tt, :], X[:, tt, :], N[:, tt, :], ALU.add).then_inc(ready.h, 1)
                            elif kind == "ln":
                                bs, ag = st[:, 16:28], st[:, 32:34]
                                for h in range(2):
                                    link(v.bn_stats(bs[:, 6 * h:6 * h + 6], Y[:, tt, 512 * h:512 * h + 512]))
                                v.bn_aggr(ag, bs).then_inc(b_g.h, 1)
                                dve.wait_ge(g_b.h, g_b.base + tt + 1)
                                link(v.tensor_scalar(Y[:, tt, :], Y[:, tt, :], ag[:, 0:1], ag[:, 1:2], ALU.subtract, ALU.mult))
                                link(v.tensor_tensor(Y[:, tt, :], Y[:, tt, :], bc[0][:, :], ALU.mult))
                                v.tensor_tensor(X[:, tt, :], Y[:, tt, :], bc[1][:, :], ALU.add).then_inc(ready.h, 1)
                            else:
                                dve.wait_ge(sums.h, sums.base + tt + 1)
                                sq = N[:, tt, :].rearrange("p (h e) -> p h e", h=8)
                                v.tensor_reduce(st[:, 40:48], sq, AX.X, ALU.add).then_inc(b_g.h, 1)
                                dve.wait_ge(g_b.h, g_b.base + tt + 1)
                                link(v.tensor_tensor(sq, Y[:, tt, :].rearrange("p (h e) -> p h e", h=8),
                                                     st[:, 40:48].unsqueeze(2).to_broadcast([P, 8, P]), ALU.mult))
                                if "gate" in extra:
                                    link(v.tensor_tensor(N[:, tt, :], N[:, tt, :], extra["gate"][:, tt, :], ALU.mult))
                                dve.sem_inc(ready.h, 1)
                            if transposed and tt >= 1:
                                low(2 * tt - 2)
                                low(2 * tt - 1)
                        if transposed:
                            low(2 * TT - 2)
                            low(2 * TT - 1)
                        link.done()

                    if transposed:
                        @block.tensor
                        def _(pe):
                            for n in range(2 * TT):
                                tt, half = n // 2, n % 2
                                pe.wait_ge(ready.h, ready.base + tt + 1)
                                if n >= 4:
                                    pe.wait_ge(tile2_free.h, tile2_free.base + n - 3)
                                for k in range(4):
                                    r = nc.tensor.transpose(PS[n % 4][:, P * k:P * k + P],
                                                            src[:, tt, 512 * half + P * k:512 * half + P * k + P], ident[:, :])
                                r.then_inc(p_a.h, 1)
                ready.base += TT
                if kind != "plain":
                    g_b.base += TT
                if kind in ("ln", "heads"):
                    b_g.base += TT
                if kind in ("pre", "rms_add", "heads"):
                    sums.base += TT
                loaded.base += 16 * n_vec
                if transposed:
                    p_a.base += 2 * TT
                    a_p.base += 2 * TT
                    tile2_free.base += 2 * TT
                    if gain is not None:
                        b_a.base += 2 * TT
                if last:
                    stored.base += 16 * TT

        def t_banks(n):
            return PS[n % 8]

        def t_linear(pe, c0, xs, tok):
            for j in range(4):
                half, kh = j // 2, j % 2
                arrived(pe, c0 + j)
                for tt in range(TT):
                    r = t_tile(PS[4 * half + tt][:, :], (c0 + j) % SPLIT, [(kk, 4 * kh + kk) for kk in range(4)],
                               xs, tok(tt), kh == 0, kh == 1)
                    if tt == TT - 1:
                        r.then_inc(w_used.h, 1)
                    elif kh == 1:
                        r.then_inc(tile_done.h, 1)

        def wait_t(eng, c0, half, tt):
            if tt == TT - 1:
                eng.wait_ge(w_used.h, CREDIT + c0 + 2 * half + 2)
            else:
                eng.wait_ge(tile_done.h, tile_done.base + 3 * half + tt + 1)

        def out_phase(alpha, tok=natural):
            c0 = pos[0]
            with nc.Block() as block:
                @block.sync
                def _(sp):
                    sp_stream(sp, 4)

                @block.gpsimd
                def _(pool):
                    pool_stream(pool, 4)

                @block.tensor
                def _(pe):
                    t_linear(pe, c0, (XTh, XTl), tok)

                @block.vector
                def _(dve):
                    for half in range(2):
                        for tt in range(TT):
                            wait_t(dve, c0, half, tt)
                            y, x = (z[:, tt, 512 * half:512 * half + 512] for z in (Y, X))
                            if alpha is None:
                                nc.vector.tensor_copy(y, PS[4 * half + tt][:, :])
                            else:
                                nc.vector.scalar_tensor_tensor(y, x, alpha, PS[4 * half + tt][:, :], ALU.mult, ALU.add)
            tile_done.base += 6
            pos[0] += 4

        def ffn_phase():
            c0 = pos[0]
            with ExitStack() as c:
                HTh = sb("HTh", [P, KT, S], F32R, c)
                HTl = sb("HTl", [P, KT, S], F32R, c)
                R = [sb(f"R{i}", [P, S], F32, c) for i in range(2)]
                Q = [sb(f"Q{i}", [P, S], F32, c) for i in range(2)]
                up_free, down_free = tile_free, tile2_free
                relu_done, sq_done, high_done, low_done = up_free, b_a, a_b, b_p
                with nc.Block() as block:
                    @block.sync
                    def _(sp):
                        sp_stream(sp, 32)

                    @block.gpsimd
                    def _(pool):
                        pool_stream(pool, 32)

                    @block.tensor
                    def _(pe):
                        with pe.Fori(0, 4) as q:
                            for j in range(4):
                                arrived(pe, q * 8 + (c0 + j))
                                for m in range(2):
                                    u = 2 * j + m
                                    pe.wait_ge(up_free.h, q * 8 + (up_free.base + u - 3))
                                    r = f_tile(PS[u % 4][:, :], (c0 + j) % SPLIT, m)
                                    r.then_inc((tile_done if m == 0 else w_used).h, 1)
                            for j in range(4):
                                half, kh = j // 2, j % 2
                                arrived(pe, q * 8 + (c0 + 4 + j))
                                pe.wait_ge(low_done.h, q * 8 + (low_done.base + 4 * kh + 4))
                                for tt in range(TT):
                                    if kh == 0:
                                        pe.wait_ge(down_free.h, q * 8 + (down_free.base + 4 * half + tt - 3))
                                    r = t_tile(PS[4 + tt][:, :], (c0 + j) % SPLIT, [(kk, 4 * kh + kk) for kk in range(4)],
                                               (HTh, HTl), natural(tt), kh == 0, kh == 1)
                                    if tt == TT - 1:
                                        r.then_inc(w_used.h, 1)
                                    elif kh == 1:
                                        r.then_inc(tile2_done.h, 1)

                    @block.scalar
                    def _(act):
                        with act.Fori(0, 4) as q:
                            for u in range(8):
                                if u % 2 == 0:
                                    act.wait_ge(tile_done.h, q * 4 + (tile_done.base + u // 2 + 1))
                                else:
                                    act.wait_ge(w_used.h, q * 8 + (CREDIT + c0 + u // 2 + 1))
                                nc.scalar.activation(R[u % 2][:, :], PS[u % 4][:, :], ACT.Relu).then_inc(relu_done.h, 1)
                                act.wait_ge(sq_done.h, q * 8 + (sq_done.base + u + 1))
                                nc.scalar.activation(HTh[:, u, :], Q[u % 2][:, :], ACT.Copy).then_inc(high_done.h, 1)

                    @block.vector
                    def _(dve):
                        v = nc.vector
                        link = InOrder(dve, dve_order)
                        for tt in range(TT):
                            link(v.tensor_scalar(Y[:, tt, :], X[:, tt, :], ALPHA, None, ALU.mult))
                        with dve.Fori(0, 4) as q:
                            for u in range(8):
                                dve.wait_ge(relu_done.h, q * 8 + (relu_done.base + u + 1))
                                v.tensor_tensor(Q[u % 2][:, :], R[u % 2][:, :], R[u % 2][:, :], ALU.mult).then_inc(sq_done.h, 1)
                                dve.wait_ge(high_done.h, q * 8 + (high_done.base + u + 1))
                                v.tensor_tensor(HTl[:, u, :], Q[u % 2][:, :], HTh[:, u, :].bitcast(F32), ALU.subtract).then_inc(low_done.h, 1)
                            for half in range(2):
                                for tt in range(TT):
                                    if tt == TT - 1:
                                        dve.wait_ge(w_used.h, q * 8 + (CREDIT + c0 + 4 + 2 * half + 2))
                                    else:
                                        dve.wait_ge(tile2_done.h, q * 6 + (tile2_done.base + 3 * half + tt + 1))
                                    y = Y[:, tt, 512 * half:512 * half + 512]
                                    v.tensor_tensor(y, y, PS[4 + tt][:, :], ALU.add).then_inc(down_free.h, 1)
                        link.done()
                up_free.base += 32
                down_free.base += 32
                tile_done.base += 16
                tile2_done.base += 24
                sq_done.base += 32
                high_done.base += 32
                low_done.base += 32
                pos[0] += 32

        def ple_phase(layer):
            c0 = pos[0]
            with ExitStack() as c:
                pT = sb("pT", [P, 2, S], F32, c)
                pTh = sb("pTh", [P, 2, S], F32R, c)
                pTl = sb("pTl", [P, 2, S], F32R, c)
                with nc.Block() as block:
                    @block.sync
                    def _(sp):
                        sp.dma_start(pT[:, :, :], t["p_2"][layer].rearrange("(k p) s -> p k s", p=P)).then_inc(loaded.h, 16)
                        sp_stream(sp, 5)

                    @block.gpsimd
                    def _(pool):
                        pool_stream(pool, 5)

                    @block.tensor
                    def _(pe):
                        t_linear(pe, c0, (XTh, XTl), natural)
                        arrived(pe, c0 + 4)
                        pe.wait_ge(b_p.h, b_p.base + 1)
                        for half in range(2):
                            for tt in range(TT):
                                n = 4 * half + tt
                                pe.wait_ge(tile2_free.h, tile2_free.base + n + 1)
                                r = t_tile(PS[n][:, :], (c0 + 4) % SPLIT, [(0, 0), (1, 1)], (pTh, pTl), natural(tt), True, True,
                                           c0=512 * half, step=1024)
                                r.then_inc((w_used if n == 7 else tile2_done).h, 1)

                    @block.scalar
                    def _(act):
                        act.wait_ge(loaded.h, loaded.base + 16)
                        nc.scalar.activation(pTh[:, :, :], pT[:, :, :], ACT.Copy).then_inc(a_b.h, 1)
                        for half in range(2):
                            for tt in range(TT):
                                wait_t(act, c0, half, tt)
                                nc.scalar.activation(Y[:, tt, 512 * half:512 * half + 512], PS[4 * half + tt][:, :],
                                                     ACT.Sigmoid).then_inc(tile2_free.h, 1)

                    @block.vector
                    def _(dve):
                        v = nc.vector
                        link = InOrder(dve, dve_order)
                        dve.wait_ge(loaded.h, loaded.base + 16)
                        dve.wait_ge(a_b.h, a_b.base + 1)
                        v.tensor_tensor(pTl[:, :, :], pT[:, :, :], pTh[:, :, :].bitcast(F32), ALU.subtract).then_inc(b_p.h, 1)
                        for half in range(2):
                            for tt in range(TT):
                                n = 4 * half + tt
                                dve.wait_ge(tile2_free.h, tile2_free.base + n + 1)
                                if n == 7:
                                    dve.wait_ge(w_used.h, CREDIT + c0 + 5)
                                else:
                                    dve.wait_ge(tile2_done.h, tile2_done.base + n + 1)
                                y, x = (z[:, tt, 512 * half:512 * half + 512] for z in (Y, X))
                                link(v.tensor_tensor(y, y, PS[n][:, :], ALU.mult))
                                v.tensor_tensor(x, x, y, ALU.add)
                        link.done()
            tile_done.base += 6
            tile2_done.base += 7
            tile2_free.base += 8
            loaded.base += 16
            a_b.base += 1
            b_p.base += 1
            pos[0] += 5

        def pe_jobs(n, scores, transposes, values, fill=lambda j: None):
            scores(0)
            scores(1)
            fill(-1)
            for j in range(n):
                transposes(j)
                if j + 2 < n:
                    scores(j + 2)
                fill(j)
                values(j)

        def dve_jobs(n, biased, normalise):
            for j in range(n + 1):
                if j < n:
                    biased(j)
                if j >= 1:
                    normalise(j - 1)

        def act_jobs(n, exps, copy_probs, copy_out, drain=lambda j: None):
            for j in range(n + 2):
                if j < n:
                    exps(j)
                if j >= 2:
                    copy_out(j - 2)
                if 1 <= j <= n:
                    copy_probs(j - 1)
                drain(j - 1)

        SC_DONE, SC_FREE, BIASED, EXPED, PNORM, TR, PTC, PV, OEV = (
            sigs[k] for k in ("sc_done", "sc_free", "sbias", "pexp", "pnorm", "tr", "pt", "pv", "oev"))
        BIAS_IN, BIAS_USED, PROJ, PEV = (sigs[k] for k in ("bias_in", "bias_used", "proj", "pev"))


        def diff_attention(layer, j):
            c0 = pos[0]
            lam_init = 0.8 - 0.6 * math.exp(-0.3 * layer)
            with ExitStack() as c:
                RUNS, RUN = 4, 8
                QT = sb("QT", [P, 2, 2, S], F32, c)
                KTT = sb("KTT", [P, 2, 2, S], F32, c)
                V = sb("V", [P, 2, TT, 256], F32, c)
                B = sb("B", [P, 4, WD], F32, c)
                SC = sb("SC", [P, 2, 2, 512], F32, c)
                PT = sb("PT", [P, 2, 512], F32, c)
                sa = sb("sa", [P, 2, 8], F32, c)
                lam = sb("lam", [P, 4 * 64 + 8], F32, c)
                TBANK, OBANK = 6, 7
                CH = (0, 0, 1, 1, 2, 2, 2, 2)
                STEP = (-1, 0, 1, 3, 4, 4, 5, 6)
                CHUNK_END = (1, 3, 7)
                OTHERS = tuple(n for n in range(8) if n not in CHUNK_END)
                with nc.Block() as block:
                    @block.sync
                    def _(sp):
                        sp_stream(sp, 12)

                    @block.gpsimd
                    def _(pool):
                        pool_stream(pool, 12)

                    @block.tensor
                    def _(pe):
                        def project(r, n):
                            ch = c0 + 3 * r + CH[n]
                            if n in (0, 2, 4):
                                arrived(pe, ch)
                            pe.wait_ge(PEV.h, PEV.base + RUN * r + n - 1)
                            if n < 4:
                                x = f_tile(PS[n % 2][:, :], ch % SPLIT, n % 2)
                            else:
                                x = v_tile(PS[n % 2][:, 0:256], ch % SPLIT, 0, 256, natural(n - 4))
                            x.then_inc((w_used if n in CHUNK_END else PROJ).h, 1)

                        def run(r):
                            def wait(s, k):
                                pe.wait_ge(s.h, s.base + RUN * r + k)

                            def scores(n):
                                hh, b = n // 4, n % 4
                                wait(SC_FREE, n - 1)
                                for m in range(2):
                                    x = nc.tensor.matmul(PS[2 + 2 * (n % 2) + m][:, 0:P * (b + 1)],
                                                         QT[64 * m:64 * m + 64, r % 2, hh, P * b:P * b + P],
                                                         KTT[64 * m:64 * m + 64, r % 2, hh, 0:P * (b + 1)], start=True, stop=True)
                                x.then_inc(SC_DONE.h, 1)

                            def transposes(n):
                                wait(PNORM, n + 1)
                                wait(PTC, n)
                                for k in range(n % 4 + 1):
                                    x = nc.tensor.transpose(PS[TBANK][:, P * k:P * k + P], SC[:, n % 2, 0, P * k:P * k + P], ident[:, :])
                                x.then_inc(TR.h, 1)

                            def fill(j):
                                for n in range(RUN):
                                    if STEP[n] == j and r + 1 < RUNS:
                                        project(r + 1, n)

                            def values(n):
                                wait(PTC, n + 1)
                                wait(OEV, n)
                                hh, b = n // 4, n % 4
                                for k in range(b + 1):
                                    x = nc.tensor.matmul(PS[OBANK][:, 0:P], PT[:, n % 2, P * k:P * k + P],
                                                         V[:, r % 2, k, P * hh:P * hh + P], start=(k == 0), stop=(k == b))
                                x.then_inc(PV.h, 1)
                            wait(PEV, RUN)
                            pe_jobs(RUN, scores, transposes, values, fill)
                        for n in range(RUN):
                            project(0, n)
                        for r in range(RUNS):
                            run(r)

                    @block.scalar
                    def _(act):
                        a = nc.scalar

                        def load_bias(r):
                            act.dma_start(B[:, :, :], bias_d[4 * r:4 * r + 4].rearrange("h p w -> p h w")).then_inc(BIAS_IN.h, 16)

                        def take(r, n):
                            if n in CHUNK_END:
                                act.wait_ge(w_used.h, CREDIT + c0 + 3 * r + CH[n] + 1)
                            else:
                                act.wait_ge(PROJ.h, PROJ.base + len(OTHERS) * r + OTHERS.index(n) + 1)
                            if n < 4:
                                dst, scale = ((QT, 0.125), (KTT, 1.0))[n % 2]
                                a.activation(dst[:, r % 2, n // 2, :], PS[n % 2][:, :], ACT.Copy, scale=scale).then_inc(PEV.h, 1)
                            else:
                                a.activation(V[:, r % 2, n - 4, :], PS[n % 2][:, 0:256], ACT.Copy).then_inc(PEV.h, 1)

                        def run(r):
                            def wait(s, k):
                                act.wait_ge(s.h, s.base + RUN * r + k)

                            def exps(n):
                                wait(BIASED, n + 1)
                                w = P * (n % 4 + 1)
                                for m in range(2):
                                    x = a.activation(SC[:, n % 2, m, 0:w], SC[:, n % 2, m, 0:w], ACT.Exp,
                                                     bias=sa[:, n % 2, 2 + m:3 + m], accum_out=sa[:, n % 2, 4 + m:5 + m])
                                x.then_inc(EXPED.h, 1)

                            def copy_probs(n):
                                wait(TR, n + 1)
                                wait(PV, n - 1)
                                w = P * (n % 4 + 1)
                                a.activation(PT[:, n % 2, 0:w], PS[TBANK][:, 0:w], ACT.Copy).then_inc(PTC.h, 1)

                            def copy_out(n):
                                wait(PV, n + 1)
                                h = 2 * r + n // 4
                                a.activation(Y[:, n % 4, P * h:P * h + P], PS[OBANK][:, 0:P], ACT.Copy).then_inc(OEV.h, 1)

                            def drain(j):
                                if r + 1 < RUNS:
                                    if j == RUN - 2:
                                        act.wait_ge(BIAS_USED.h, BIAS_USED.base + r + 1)
                                        load_bias(r + 1)
                                    for n in range(RUN):
                                        if STEP[n] == j:
                                            take(r + 1, n)
                            act_jobs(RUN, exps, copy_probs, copy_out, drain)
                        load_bias(0)
                        act.dma_start(lam[:, 0:256], t["da_lambda_2"][j].rearrange("a e -> (a e)").partition_broadcast(P)).then_inc(loaded.h, 16)
                        act.wait_ge(b_a.h, b_a.base + 1)
                        a.activation(lam[:, 258:260], lam[:, 256:258], ACT.Exp).then_inc(a_b.h, 1)
                        for n in range(RUN):
                            take(0, n)
                        for r in range(RUNS):
                            run(r)

                    @block.vector
                    def _(dve):
                        v = nc.vector
                        link = InOrder(dve, dve_order)
                        dve.wait_ge(loaded.h, loaded.base + 16)
                        l4 = lam[:, 0:256].rearrange("p (a b e) -> p a b e", a=2, b=2)
                        link(v.tensor_tensor(l4[:, :, 0, :], l4[:, :, 0, :], l4[:, :, 1, :], ALU.mult))
                        v.tensor_reduce(lam[:, 256:258], l4[:, :, 0, :], AX.X, ALU.add).then_inc(b_a.h, 1)
                        dve.wait_ge(a_b.h, a_b.base + 1)
                        link(v.tensor_tensor(lam[:, 260:261], lam[:, 259:260], lam[:, 258:259], ALU.subtract))
                        link(v.tensor_scalar(lam[:, 261:262], lam[:, 260:261], -lam_init, None, ALU.add))
                        with dve.Fori(0, 2) as i:
                            link.enter(i, 16 * 5 + 2)
                            for hp in range(2):
                                def wait(s, k, per=16):
                                    dve.wait_ge(s.h, i * per + (s.base + k))

                                def biased(n):
                                    hh, b = n // 4, n % 4
                                    w = P * (b + 1)
                                    wait(SC_DONE, 8 * hp + n + 1)
                                    wait(TR, 8 * hp + n - 1)
                                    if n == 0:
                                        wait(BIAS_IN, 16 * (hp + 1), per=32)
                                    link(v.tensor_tensor(SC[:, n % 2, 0, 0:w], PS[2 + 2 * (n % 2)][:, 0:w], B[:, 2 * hh, WD - w:WD], ALU.add))
                                    v.tensor_tensor(SC[:, n % 2, 1, 0:w], PS[3 + 2 * (n % 2)][:, 0:w], B[:, 2 * hh + 1, WD - w:WD], ALU.add).then_inc(SC_FREE.h, 1)
                                    wait(SC_FREE, 8 * hp + n + 1)
                                    link(v.tensor_reduce(sa[:, n % 2, 0:2], SC[:, n % 2, :, 0:w], AX.X, ALU.max))
                                    if n == 7:
                                        link(v.tensor_scalar(sa[:, n % 2, 2:4], sa[:, n % 2, 0:2], -1.0, None, ALU.mult))
                                        dve.sem_inc(BIAS_USED.h, 1)
                                        dve.sem_inc(BIASED.h, 1)
                                    else:
                                        v.tensor_scalar(sa[:, n % 2, 2:4], sa[:, n % 2, 0:2], -1.0, None, ALU.mult).then_inc(BIASED.h, 1)

                                def normalise(n):
                                    w = P * (n % 4 + 1)
                                    wait(EXPED, 8 * hp + n + 1)
                                    link(v.reciprocal(sa[:, n % 2, 6:8], sa[:, n % 2, 4:6]))
                                    link(v.tensor_tensor(sa[:, n % 2, 7:8], sa[:, n % 2, 7:8], lam[:, 261:262], ALU.mult))
                                    link(v.tensor_scalar(SC[:, n % 2, 1, 0:w], SC[:, n % 2, 1, 0:w], sa[:, n % 2, 7:8], None, ALU.mult))
                                    v.scalar_tensor_tensor(SC[:, n % 2, 0, 0:w], SC[:, n % 2, 0, 0:w], sa[:, n % 2, 6:7],
                                                           SC[:, n % 2, 1, 0:w], ALU.mult, ALU.add).then_inc(PNORM.h, 1)
                                dve_jobs(8, biased, normalise)
                        link.leave(2)
                        link.done()
                for s in (SC_DONE, SC_FREE, BIASED, EXPED, PNORM, TR, PTC, PV, OEV, PEV):
                    s.base += 32
                PROJ.base += 20
                BIAS_IN.base += 64
                BIAS_USED.base += 4
                loaded.base += 16
                a_b.base += 1
                b_a.base += 1
                pos[0] += 12
            norm_phase("heads", gain=col[:, 16 + j:17 + j], extra={"post": 1.0 - lam_init})

        def final_store():
            with nc.Block() as block:
                @block.sync
                def _(sp):
                    sp.dma_start(out.rearrange("b (t p) d -> p (b t) d", p=P), X[:, :, :]).then_inc(stored.h, 16)
                    sp.wait_ge(stored.h, stored.base + 16)
        class Job:

            def __init__(self, e, scores, bias, rows, values, stat, ntiles):
                self.e, self.scores, self.bias, self.rows, self.values = e, scores, bias, rows, values
                self.stat, self.ntiles = stat, ntiles
                self.nstat = sum(r[1] for r in rows)

        def window_jobs(e, q, k, v, bias):
            prev_diag, diag = bias[:, 0:W1], bias[:, P:W1]
            return [Job(e, [(q(0), k(0, 1), 0, P), (q(1), k(0, 2), P, 2 * P)],
                        [(0, 1, P, diag), (P, 1, 2 * P, prev_diag)], [(0, 1, P), (P, 1, 2 * P)],
                        [[(v(0), 0)], [(v(0), 1), (v(1), 2)]], 0, 3),
                    Job(e, [(q(2), k(1, 2), 0, 2 * P), (q(3), k(2, 2), 2 * P, 2 * P)],
                        [(0, 2, 2 * P, prev_diag)], [(0, 2, 2 * P)],
                        [[(v(1), 0), (v(2), 1)], [(v(2), 2), (v(3), 3)]], 2, 4)]

        def residue_job(e, q, k, v, bias, stat):
            return Job(e, [(q(r), k(r), P * r, P) for r in range(4)], [(0, 4, P, bias)], [(0, 4, P)],
                       [[(v(r), r)] for r in range(4)], stat, 4)

        def bands(ap, first, n, w):
            return ap[:, first:first + n * w].rearrange("p (n w) -> p n w", n=n)

        class RowAttention:

            def __init__(self, jobs, SC, PT, stats, sink=None):
                self.jobs, self.SC, self.PT, self.stats, self.sink = jobs, SC, PT, stats, sink

            def stat(self, j, kind):
                x = self.jobs[j]
                return self.stats[:, x.e, kind, x.stat:x.stat + x.nstat]

            def pe(self, at, fill=lambda j: None):
                J, SC, PT = self.jobs, self.SC, self.PT

                def scores(n):
                    at(SC_FREE, n - 1)
                    for q, k, c, w in J[n].scores:
                        r = nc.tensor.matmul(PS[2 + n % 2][:, c:c + w], q, k, start=True, stop=True)
                    r.then_inc(SC_DONE.h, 1)

                def transposes(n):
                    at(PNORM, n + 1)
                    at(PTC, n - 1)
                    for k in range(J[n].ntiles):
                        r = nc.tensor.transpose(PS[4 + n % 2][:, P * k:P * k + P], SC[:, n % 2, P * k:P * k + P], ident[:, :])
                    r.then_inc(TR.h, 1)

                def values(n):
                    at(PTC, n + 1)
                    at(OEV, n - 1)
                    lo = 64 * J[n].e
                    for q, terms in enumerate(J[n].values):
                        for m, (v, tile) in enumerate(terms):
                            r = nc.tensor.matmul(PS[6 + n % 2][lo:lo + 64, P * q:P * q + P], v, PT[:, n % 2, P * tile:P * tile + P],
                                                 start=(m == 0), stop=(m == len(terms) - 1))
                    r.then_inc(PV.h, 1)
                pe_jobs(len(J), scores, transposes, values, fill)

            def dve(self, at, link, bias_wait, bias_done, head_done):
                v, J, SC = nc.vector, self.jobs, self.SC

                def biased(n):
                    x = J[n]
                    at(SC_DONE, n + 1)
                    at(TR, n - 1)
                    if n == 0:
                        bias_wait()
                    for i, (c, m, w, b) in enumerate(x.bias):
                        o, s = bands(SC[:, n % 2, :], c, m, w), bands(PS[2 + n % 2][:, :], c, m, w)
                        r = v.tensor_tensor(o, s, b.unsqueeze(1).to_broadcast([P, m, w]), ALU.add)
                        if i < len(x.bias) - 1:
                            link(r)
                    r.then_inc(SC_FREE.h, 1)
                    at(SC_FREE, n + 1)
                    if n == len(J) - 1:
                        bias_done()
                    k = 0
                    for c, m, w in x.rows:
                        link(v.tensor_reduce(self.stat(n, 0)[:, k:k + m], bands(SC[:, n % 2, :], c, m, w), AX.X, ALU.max))
                        k += m
                    if self.sink is not None:
                        link(v.tensor_scalar(self.stat(n, 0), self.stat(n, 0), self.sink(x), None, ALU.max))
                    v.tensor_scalar(self.stat(n, 1), self.stat(n, 0), -1.0, None, ALU.mult).then_inc(BIASED.h, 1)

                def normalise(n):
                    x = J[n]
                    at(EXPED, n + 1)
                    link(v.reciprocal(self.stat(n, 3), self.stat(n, 2)))
                    k = 0
                    for i, (c, m, w) in enumerate(x.rows):
                        s = bands(SC[:, n % 2, :], c, m, w)
                        r = v.tensor_tensor(s, s, self.stat(n, 3)[:, k:k + m].unsqueeze(2).to_broadcast([P, m, w]), ALU.mult)
                        if i < len(x.rows) - 1:
                            link(r)
                        k += m
                    r.then_inc(PNORM.h, 1)
                    head_done(n)
                dve_jobs(len(J), biased, normalise)

            def dve_links(self):
                return sum(len(x.bias) - 1 + len(x.rows) + (self.sink is not None) + 1 + len(x.rows) - 1 for x in self.jobs)

            def act(self, at, copy_to, link=None, drain=lambda j: None):
                a, J, SC, PT = nc.scalar, self.jobs, self.SC, self.PT

                def exps(n):
                    x = J[n]
                    at(BIASED, n + 1)
                    k = 0
                    for c, m, w in x.rows:
                        for i in range(m):
                            s = SC[:, n % 2, c + i * w:c + i * w + w]
                            r = a.activation(s, s, ACT.Exp, bias=self.stat(n, 1)[:, k:k + 1], accum_out=self.stat(n, 2)[:, k:k + 1])
                            k += 1
                    if self.sink is not None:
                        link(r)
                        sk, den = sink_tmp[:, 0:k], sink_tmp[:, 4:4 + k]
                        link(a.activation(sk, self.stat(n, 1), ACT.Exp, bias=self.sink(x)))
                        for i in range(k):
                            r = a.activation(self.stat(n, 2)[:, i:i + 1], self.stat(n, 2)[:, i:i + 1], ACT.Identity, bias=sk[:, i:i + 1])
                    r.then_inc(EXPED.h, 1)

                def copy_probs(n):
                    at(TR, n + 1)
                    at(PV, n - 1)
                    w = P * J[n].ntiles
                    a.activation(PT[:, n % 2, 0:w], PS[4 + n % 2][:, 0:w], ACT.Copy).then_inc(PTC.h, 1)

                def copy_out(n):
                    at(PV, n + 1)
                    lo = 64 * J[n].e
                    copy_to(n, PS[6 + n % 2][lo:lo + 64, 0:P * len(J[n].values)]).then_inc(OEV.h, 1)
                act_jobs(len(J), exps, copy_probs, copy_out, drain)

        sink_tmp = sb("sink_tmp", [P, 8])

        def dilated_attention():
            c0 = pos[0]
            with ExitStack() as c:
                O3 = sb("O3", [P, 3, 8, S], F32, c)
                MX = sb("MX", [P, HEADS, 12], F32, c)
                SM = sb("SM", [P, HEADS, 12], F32, c)
                with ExitStack() as c2:
                    QK = sb("QK", [P, 6, S], F32, c2)
                    V = sb("V", [P, TT, 2, 3, P], F32, c2)
                    V2 = sb("V2", [P, TT, P], F32, c2)
                    B = sb("B", [P, 2, 512], F32, c2)
                    SC = sb("SC", [P, 2, 512], F32, c2)
                    PT = sb("PT", [P, 2, 512], F32, c2)
                    stats = sb("stats", [P, 2, 4, 12], F32, c2)

                    def g0(ap, t0):
                        return ap[:, P * t0:P * t0 + P]

                    def g1(ap, r):
                        return ap[:, r::4]

                    def jobs(half):
                        by_group = [[], [], []]
                        for e in range(2):
                            lo = 64 * e
                            qk = lambda n: QK[lo:lo + 64, n, :]
                            vv = lambda g: (lambda r: V[:, r, half, g, lo:lo + 64])
                            by_group[0] += window_jobs(e, (lambda b, q=qk(0): g0(q, b)),
                                                       (lambda b, n, k=qk(1): k[:, P * b:P * b + n * P]), vv(0), B[:, e, 0:W1])
                            by_group[1].append(residue_job(e, (lambda r, q=qk(2): g1(q, r)), (lambda r, k=qk(3): g1(k, r)), vv(1), B[:, e, W1:384], 4))
                            by_group[2].append(residue_job(e, (lambda r, q=qk(4): g1(q, r)), (lambda r, k=qk(5): g1(k, r)), vv(2), B[:, e, 384:512], 8))
                        for g in range(3):
                            for n, x in enumerate(by_group[g]):
                                x.group, x.part = g, n % 2
                        return by_group[0] + by_group[1] + by_group[2]

                    att = [RowAttention(jobs(h), SC, PT, stats) for h in range(2)]
                    def qk_pair(g, ch, steps):
                        return [("qk", 2 * g, ch, 0, steps[0]), ("qk", 2 * g + 1, ch, 1, steps[1])]

                    def v_tiles(kind, ch, steps):
                        return [(kind, tt, ch, 0, steps[tt]) for tt in range(TT)]
                    first = (v_tiles("v01", 0, (-1, -1, 0, 0)) + qk_pair(0, 1, (1, 1)) + [("z", 0, 2, 0, 2), ("z", 1, 2, 1, 3)]
                             + qk_pair(1, 3, (3, 4)) + v_tiles("v2", 4, (4, 5, 5, 6)) + qk_pair(2, 5, (6, 7)))
                    second = (v_tiles("v01", 6, (-1, -1, 0, 0)) + qk_pair(0, 7, (1, 2)) + qk_pair(1, 8, (3, 4)) + qk_pair(2, 9, (5, 7)))
                    tiles = [first, second]
                    PASSES, RUN = 4, 8
                    n_tiles = len(first) + len(second)

                    def ends(half, n):
                        return n == len(tiles[half]) - 1 or tiles[half][n + 1][2] != tiles[half][n][2]
                    n_proj = sum(not ends(h, n) for h in range(2) for n in range(len(tiles[h])))

                    def proj_before(half, n):
                        return sum(not ends(h, m) for h in range(half + 1) for m in range(len(tiles[h])) if h < half or m <= n)

                    def project(pe, i, di, half, n):
                        kind, x, ch, m, _ = tiles[half][n]
                        k = n + len(first) * half
                        if n == 0 or tiles[half][n - 1][2] != ch:
                            pe.wait_ge(w_split.h, i * 10 + (10 * di + c0 + ch + 1))
                        pe.wait_ge(PEV.h, i * n_tiles + (n_tiles * di + PEV.base + k - 1))
                        bank, slot = PS[k % 2], (c0 + ch) % SPLIT
                        if kind in ("qk", "z"):
                            r = f_tile(bank[:, :], slot, m)
                        elif kind == "v01":
                            v_tile(bank[:, 0:P], slot, 0, P, lambda X_, kk: g0(X_[:, kk, :], x))
                            r = v_tile(bank[:, P:2 * P], slot, P, P, lambda X_, kk: g1(X_[:, kk, :], x))
                        else:
                            r = v_tile(bank[:, 0:256], slot, 0, 256, lambda X_, kk: g1(X_[:, kk, :], x))
                        r.then_inc((w_used if ends(half, n) else PROJ).h, 1)

                    def take(act, i, di, half, n, at=None):
                        a = nc.scalar
                        kind, x, ch, _, _ = tiles[half][n]
                        if ends(half, n):
                            act.wait_ge(w_used.h, i * 10 + (10 * di + CREDIT + c0 + ch + 1))
                        else:
                            act.wait_ge(PROJ.h, i * n_proj + (n_proj * di + PROJ.base + proj_before(half, n)))
                        bank = PS[(n + len(first) * half) % 2]
                        if kind == "qk":
                            if at is not None:
                                at(SC_DONE, 4 + 2 * (x // 2))
                            a.activation(QK[:, x, :], bank[:, :], ACT.Copy, scale=(0.125, 1.0)[x % 2]).then_inc(PEV.h, 1)
                        elif kind == "z":
                            a.activation(YF[:, bass.ds(i * 2 + (2 * di + x), 1), :].rearrange("p a s -> p (a s)"), bank[:, :], ACT.Copy).then_inc(PEV.h, 1)
                        elif kind == "v01":
                            a.activation(V[:, x, half, 0:2, :], bank[:, 0:256].rearrange("p (g e) -> p g e", g=2), ACT.Copy).then_inc(PEV.h, 1)
                        else:
                            a.activation(V[:, x, 0, 2, :], bank[:, 0:P], ACT.Copy)
                            a.activation(V2[:, x, :], bank[:, P:2 * P], ACT.Copy).then_inc(PEV.h, 1)

                    def next_half(half, last):
                        return None if last and half == 1 else (half, 1 - half)

                    def at_step(half, j):
                        return [n for n, x in enumerate(tiles[half]) if x[4] == j]
                    with nc.Block() as block:
                        @block.sync
                        def _(sp):
                            sp_stream(sp, 40)

                        @block.gpsimd
                        def _(pool):
                            pool_stream(pool, 40)

                        @block.tensor
                        def _(pe):
                            def one_pass(i, last):
                                for half in range(2):
                                    def at(s, k):
                                        pe.wait_ge(s.h, i * (2 * RUN) + (s.base + RUN * half + k))

                                    def fill(j):
                                        to = next_half(half, last)
                                        for n in (at_step(to[1], j) if to else ()):
                                            project(pe, i, to[0], to[1], n)
                                    pe.wait_ge(PEV.h, i * n_tiles + (PEV.base + len(first) + len(second) * half))
                                    att[half].pe(at, fill)
                            for n in range(len(first)):
                                project(pe, 0, 0, 0, n)
                            with pe.Fori(0, PASSES - 1) as i:
                                one_pass(i, False)
                            one_pass(PASSES - 1, True)

                        @block.scalar
                        def _(act):
                            a = nc.scalar

                            def load_bias(i, di, half):
                                act.dma_start(B[:, :, :], bias_a[bass.ds(i * 4 + (4 * di + 2 * half), 2)].rearrange("h p w -> p h w")).then_inc(BIAS_IN.h, 16)

                            def one_pass(i, last):
                                for half in range(2):
                                    def at(s, k):
                                        act.wait_ge(s.h, i * (2 * RUN) + (s.base + RUN * half + k))

                                    def copy_to(n, psum):
                                        j = att[half].jobs[n]
                                        lo = 64 * j.e
                                        o = O3[lo:lo + 64, j.group, bass.ds(i * 2 + half, 1), :].rearrange("p a s -> p (a s)")
                                        if j.group == 0:
                                            return a.activation(o[:, 256 * j.part:256 * j.part + 256], psum, ACT.Copy)
                                        return a.activation(o.rearrange("p (l r) -> p r l", r=4), psum.rearrange("p (r l) -> p r l", r=4), ACT.Copy)

                                    def drain(j):
                                        to = next_half(half, last)
                                        if to and j == RUN - 2:
                                            act.wait_ge(BIAS_USED.h, i * 2 + (BIAS_USED.base + half + 1))
                                            load_bias(i, to[0], to[1])
                                        for n in (at_step(to[1], j) if to else ()):
                                            take(act, i, to[0], to[1], n, at)
                                    if half == 1:
                                        act.wait_ge(PEV.h, i * n_tiles + (PEV.base + len(first)))
                                        a.activation(V[:, :, 1, 2, :], V2[:, :, :], ACT.Copy)
                                    att[half].act(at, copy_to, drain=drain)
                            load_bias(0, 0, 0)
                            for n in range(len(first)):
                                take(act, 0, 0, 0, n)
                            with act.Fori(0, PASSES - 1) as i:
                                one_pass(i, False)
                            one_pass(PASSES - 1, True)

                        @block.vector
                        def _(dve):
                            link = InOrder(dve, dve_order)
                            with dve.Fori(0, PASSES) as i:
                                link.enter(i, sum(x.dve_links() for x in att))
                                for half in range(2):
                                    def at(s, k):
                                        dve.wait_ge(s.h, i * (2 * RUN) + (s.base + RUN * half + k))

                                    def head_done(n):
                                        if n >= RUN - 2:
                                            e = n - (RUN - 2)
                                            for dst, kind in ((MX, 0), (SM, 2)):
                                                nc.vector.tensor_copy(dst[:, bass.ds(i * 4 + (2 * half + e), 1), :].rearrange("p a s -> p (a s)"),
                                                                      stats[:, e, kind, :])
                                    att[half].dve(at, link, lambda: dve.wait_ge(BIAS_IN.h, i * 32 + (BIAS_IN.base + 16 * (half + 1))),
                                                  lambda: dve.sem_inc(BIAS_USED.h, 1), head_done)
                                link.leave(PASSES)
                            link.done()
                    for s in (SC_DONE, SC_FREE, BIASED, EXPED, PNORM, TR, PTC, PV, OEV):
                        s.base += 64
                    PEV.base += 4 * n_tiles
                    PROJ.base += 4 * n_proj
                    BIAS_IN.base += 128
                    BIAS_USED.base += 8
                    pos[0] += 40
                combine_groups(O3, MX, SM)

        def combine_groups(O3, MX, SM):
            with ExitStack() as c:
                LR = sb("LR", [HEADS, 3, S], F32, c)
                M = sb("M", [HEADS, S], F32, c)
                sel = sb("sel", [HEADS, 8, P], F32, c)
                acc = sb("acc", [P, 2, S], F32, c)
                sg = sb("sg", [P, 2, S], F32, c)
                with nc.Block() as block:
                    @block.sync
                    def _(sp):
                        sp.dma_start(sel[:, :, :], t["head_select"]).then_inc(loaded.h, 16)

                    @block.scalar
                    def _(act):
                        a = nc.scalar
                        a.activation(SM[:, :, :], SM[:, :, :], ACT.Ln).then_inc(a_b.h, 1)
                        act.wait_ge(b_a.h, b_a.base + 1)
                        a.activation(LR[:, :, :], LR[:, :, :], ACT.Exp).then_inc(a_b.h, 1)
                        for p in range(8):
                            if p >= 2:
                                act.wait_ge(tile2_free.h, tile2_free.base + p - 1)
                            a.activation(sg[:, p % 2, :], YF[:, p, :], ACT.Sigmoid).then_inc(a_b.h, 1)
                            act.wait_ge(b_a.h, b_a.base + 2 + p)
                            a.activation(XTh[:, p, :], acc[:, 0, :], ACT.Copy).then_inc(a_p.h, 1)

                    @block.tensor
                    def _(pe):
                        pe.wait_ge(b_p.h, b_p.base + 1)
                        for s in range(12):
                            r = nc.tensor.transpose(PS[s // 4][0:HEADS, P * (s % 4):P * (s % 4) + P], SM[:, :, s], ident[:, :])
                        r.then_inc(p_b.h, 1)
                        pe.wait_ge(b_p.h, b_p.base + 2)
                        pe.wait_ge(loaded.h, loaded.base + 16)
                        for p in range(8):
                            if p >= 2:
                                pe.wait_ge(tile2_free.h, tile2_free.base + p - 1)
                            for g in range(3):
                                r = nc.tensor.matmul(PS[4 * (p % 2) + g][:, :], sel[:, p, :], LR[:, g, :], start=True, stop=True)
                            r.then_inc(p_b.h, 1)

                    @block.vector
                    def _(dve):
                        v = nc.vector
                        link = InOrder(dve, dve_order)
                        dve.wait_ge(a_b.h, a_b.base + 1)
                        v.tensor_tensor(SM[:, :, :], SM[:, :, :], MX[:, :, :], ALU.add).then_inc(b_p.h, 1)
                        dve.wait_ge(p_b.h, p_b.base + 1)
                        link(v.tensor_copy(LR[:, 0, :], PS[0][0:HEADS, :]))
                        for g, r in ((1, 4), (2, 4)):
                            link(v.tensor_copy(LR[:, g, :].rearrange("p (l r) -> p r l", r=r),
                                               PS[g][0:HEADS, :].rearrange("p (r l) -> p r l", r=r)))
                        link(v.tensor_tensor(M[:, :], LR[:, 0, :], LR[:, 1, :], ALU.max))
                        link(v.tensor_tensor(M[:, :], M[:, :], LR[:, 2, :], ALU.max))
                        v.tensor_tensor(LR[:, :, :], LR[:, :, :], M[:, :].unsqueeze(1).to_broadcast([HEADS, 3, S]), ALU.subtract).then_inc(b_a.h, 1)
                        dve.wait_ge(a_b.h, a_b.base + 2)
                        link(v.tensor_tensor(M[:, :], LR[:, 0, :], LR[:, 1, :], ALU.add))
                        link(v.tensor_tensor(M[:, :], M[:, :], LR[:, 2, :], ALU.add))
                        link(v.reciprocal(M[:, :], M[:, :]))
                        v.tensor_tensor(LR[:, :, :], LR[:, :, :], M[:, :].unsqueeze(1).to_broadcast([HEADS, 3, S]), ALU.mult).then_inc(b_p.h, 1)
                        for p in range(8):
                            dve.wait_ge(p_b.h, p_b.base + 2 + p)
                            if p >= 1:
                                dve.wait_ge(a_p.h, a_p.base + p)
                            link(v.tensor_tensor(acc[:, 0, :], O3[:, 0, p, :], PS[4 * (p % 2)][:, :], ALU.mult))
                            for g in (1, 2):
                                link(v.tensor_tensor(acc[:, 1, :], O3[:, g, p, :], PS[4 * (p % 2) + g][:, :], ALU.mult))
                                link(v.tensor_tensor(acc[:, 0, :], acc[:, 0, :], acc[:, 1, :], ALU.add))
                            link(v.tensor_tensor(acc[:, 0, :], acc[:, 0, :], YF[:, p, :], ALU.mult))
                            dve.wait_ge(a_b.h, a_b.base + 3 + p)
                            v.tensor_tensor(acc[:, 0, :], acc[:, 0, :], sg[:, p % 2, :], ALU.mult).then_inc(b_a.h, 1)
                            dve.wait_ge(a_p.h, a_p.base + p + 1)
                            v.tensor_tensor(XTl[:, p, :], acc[:, 0, :], XTh[:, p, :].bitcast(F32), ALU.subtract).then_inc(tile2_free.h, 1)
                            dve.wait_ge(tile2_free.h, tile2_free.base + p + 1)
                        link.done()
                loaded.base += 16
                a_b.base += 10
                b_a.base += 9
                p_b.base += 9
                b_p.base += 2
                a_p.base += 8
                tile2_free.base += 8

        def sliding_attention():
            c0 = pos[0]
            with ExitStack() as c:
                Q = sb("Q", [P, 2, S], F32, c)
                KK = sb("KK", [P, 2, S], F32, c)
                V = sb("V", [P, TT, P], F32, c)
                B = sb("B", [P, 4, WS], F32, c)
                SC = sb("SC", [P, 2, 512], F32, c)
                PT = sb("PT", [P, 2, 512], F32, c)
                stats = sb("stats", [P, 2, 4, 12], F32, c)
                sinks = sb("sinks", [P, HEADS], F32, c)
                sk = sb("sk", [P, 4], F32, c)

                js = []
                for kv in range(2):
                    for e in range(2):
                        lo = 64 * e
                        w = window_jobs(e, (lambda b, q=Q[lo:lo + 64, kv, :]: q[:, P * b:P * b + P]),
                                        (lambda b, n, k=KK[lo:lo + 64, kv, :]: k[:, P * b:P * b + n * P]),
                                        (lambda r, kv=kv: V[:, r, 64 * kv:64 * kv + 64]), B[:, 2 * kv + e, :])
                        for x in w:
                            x.head = 2 * kv + e
                        js += w
                att = RowAttention(js, SC, PT, stats, sink=lambda x: sk[:, x.head:x.head + 1])
                RUNS, RUN = 4, 8
                STEP = (1, 5)
                with nc.Block() as block:
                    @block.sync
                    def _(sp):
                        sp_stream(sp, 6)

                    @block.gpsimd
                    def _(pool):
                        pool_stream(pool, 6)

                    @block.tensor
                    def _(pe):
                        for n in range(6):
                            if n in (0, 2):
                                arrived(pe, c0 + n // 2)
                            pe.wait_ge(PEV.h, PEV.base + n - 1)
                            if n < 2:
                                r = f_tile(PS[n % 2][:, :], c0 % SPLIT, n)
                            else:
                                r = v_tile(PS[n % 2][:, 0:P], (c0 + 1) % SPLIT, 0, P, natural(n - 2))
                            r.then_inc((w_used if n in (1, 5) else PROJ).h, 1)

                        def project(r, m):
                            if m == 0:
                                arrived(pe, c0 + 2 + r)
                            pe.wait_ge(PEV.h, PEV.base + 6 + 2 * r + m - 1)
                            x = f_tile(PS[m][:, :], (c0 + r) % SPLIT, m)
                            x.then_inc((w_used if m else PROJ).h, 1)
                        project(0, 0)
                        project(0, 1)
                        for r in range(RUNS):
                            def at(s, k):
                                pe.wait_ge(s.h, s.base + RUN * r + k)

                            def fill(j):
                                if j in STEP and r + 1 < RUNS:
                                    project(r + 1, STEP.index(j))
                            pe.wait_ge(PEV.h, PEV.base + 6 + 2 * r + 2)
                            att.pe(at, fill)

                    @block.scalar
                    def _(act):
                        a = nc.scalar
                        link = InOrder(act, act_order)

                        def load_bias(r):
                            for kv in range(2):
                                h = 2 * r + 8 * kv
                                act.dma_start(B[:, 2 * kv:2 * kv + 2, :], bias_s[h:h + 2].rearrange("h p w -> p h w")).then_inc(BIAS_IN.h, 16)

                        def take(r, m):
                            if m:
                                act.wait_ge(w_used.h, CREDIT + c0 + 2 + r + 1)
                            else:
                                act.wait_ge(PROJ.h, PROJ.base + 4 + r + 1)
                            if r:
                                act.wait_ge(SC_DONE.h, SC_DONE.base + RUN * (r - 1) + 4 + 4 * m)
                            a.activation(Q[:, m, :], PS[m][:, :], ACT.Copy, scale=0.125).then_inc(PEV.h, 1)
                        act.dma_start(sinks[:, :], t["sw_sinks_2"][0].partition_broadcast(P)).then_inc(loaded.h, 16)
                        load_bias(0)
                        for n in range(6):
                            if n in (1, 5):
                                act.wait_ge(w_used.h, CREDIT + c0 + (1 if n == 1 else 2))
                            else:
                                act.wait_ge(PROJ.h, PROJ.base + {0: 1, 2: 2, 3: 3, 4: 4}[n])
                            if n < 2:
                                a.activation(KK[:, n, :], PS[n % 2][:, :], ACT.Copy).then_inc(PEV.h, 1)
                            else:
                                a.activation(V[:, n - 2, :], PS[n % 2][:, 0:P], ACT.Copy).then_inc(PEV.h, 1)
                        take(0, 0)
                        take(0, 1)
                        for r in range(RUNS):
                            def at(s, k):
                                act.wait_ge(s.h, s.base + RUN * r + k)

                            def copy_to(n, psum):
                                x = att.jobs[n]
                                lo = 64 * x.e
                                return a.activation(YF[lo:lo + 64, 2 * r + x.head // 2, 256 * (n % 2):256 * (n % 2) + 256], psum, ACT.Copy)

                            def drain(j):
                                if r + 1 < RUNS:
                                    if j == RUN - 2:
                                        act.wait_ge(BIAS_USED.h, BIAS_USED.base + r + 1)
                                        load_bias(r + 1)
                                    if j in STEP:
                                        take(r + 1, STEP.index(j))
                            att.act(at, copy_to, link, drain)
                        link.done()

                    @block.vector
                    def _(dve):
                        link = InOrder(dve, dve_order)
                        dve.wait_ge(loaded.h, loaded.base + 16)
                        with dve.Fori(0, RUNS) as i:
                            link.enter(i, att.dve_links() + 1)

                            def at(s, k):
                                dve.wait_ge(s.h, i * RUN + (s.base + k))

                            def bias_wait():
                                dve.wait_ge(BIAS_IN.h, i * 32 + (BIAS_IN.base + 32))
                            at(SC_DONE, 1)
                            link(nc.vector.tensor_copy(sk[:, :], sinks[:, bass.ds(i * 4, 4)]))
                            att.dve(at, link, bias_wait, lambda: dve.sem_inc(BIAS_USED.h, 1), lambda n: None)
                            link.leave(RUNS)
                        link.done()
                for s in (SC_DONE, SC_FREE, BIASED, EXPED, PNORM, TR, PTC, PV, OEV):
                    s.base += 32
                PEV.base += 14
                PROJ.base += 8
                BIAS_IN.base += 128
                BIAS_USED.base += 4
                loaded.base += 16
                pos[0] += 6
            split_features(lambda k: YF[:, k, :])

        def split_features(src, gate=None):
            with nc.Block() as block:
                @block.scalar
                def _(act):
                    for k in range(KT):
                        nc.scalar.activation(XTh[:, k, :], src(k), ACT.Copy).then_inc(a_b.h, 1)

                @block.vector
                def _(dve):
                    for k in range(KT):
                        dve.wait_ge(a_b.h, a_b.base + k + 1)
                        nc.vector.tensor_tensor(XTl[:, k, :], src(k), XTh[:, k, :].bitcast(F32), ALU.subtract)
            a_b.base += KT
        U8 = mybir.dt.uint8
        hg_lv = dict(pd=signal("hg_diff"), ae=signal("hg_exp"), dw=signal("hg_weighted"), wf=signal("hg_slot_free", CREDIT),
                     lf=signal("hg_level_free", CREDIT), kht=signal("hg_khat_copied", CREDIT), tk=signal("hg_khat_transposed"),
                     ud=signal("hg_update_done"), sr=signal("hg_states_ready", CREDIT), oe=signal("hg_out_free", CREDIT), dt=signal("dve_tick"), pt=signal("pool_tick"))

        def hgrn(layer, j):
            c0 = pos[0]
            with ExitStack() as c:
                G = sb("G", [P, TT, D], F32, c)
                with ExitStack() as c2:
                    QF = sb("QF", [P, KT, S], F32, c2)
                    KIN = sb("KIN", [P, KT, S], F32, c2)
                    LF = sb("LF", [P, KT, S], F32, c2)
                    IV = sb("IV", [P, TT, D], F32, c2)
                    masks = sb("masks", [P, HG_LEVELS + 1, P], U8, c2)
                    with ExitStack() as c3:
                        masks32 = sb("masks32", [P, HG_LEVELS + 1, P], I32, c3)
                        lbt = sb("lbt", [P, 4, 8], F32, c3)
                        lb = sb("lb", [P, 3, 8], F32, c3)
                        ones = sb("ones", [P, S], F32, c3)
                        SG = sb("SG", [P, 2, S], F32, c3)
                        with nc.Block() as block:
                            @block.sync
                            def _(sp):
                                sp.dma_start(lbt[:, :, :], t["hg_lower_bound_2"]).then_inc(loaded.h, 16)
                                sp.dma_start(masks32[:, :, :], t["hg_masks"]).then_inc(loaded.h, 16)
                                sp_stream(sp, 16)

                            @block.gpsimd
                            def _(pool):
                                pool_stream(pool, 16)

                            @block.tensor
                            def _(pe):
                                with pe.Fori(0, 4) as i:
                                    for n in range(4):
                                        if n % 2 == 0:
                                            pe.wait_ge(w_split.h, i * 2 + (c0 + n // 2 + 1))
                                        pe.wait_ge(tile_free.h, i * 4 + (tile_free.base + n - 3))
                                        r = f_tile(PS[n][:, :], (c0 + n // 2) % SPLIT, n % 2)
                                        r.then_inc((w_used if n % 2 else tile_done).h, 1)
                                with pe.Fori(0, 4) as i:
                                    for kh in range(2):
                                        pe.wait_ge(w_split.h, i * 2 + (c0 + 8 + kh + 1))
                                        for tt in range(TT):
                                            if kh == 0:
                                                pe.wait_ge(tile2_free.h, i * 4 + (tile2_free.base + tt - 3))
                                            r = t_tile(PS[4 + tt][:, :], (c0 + kh) % SPLIT, [(kk, 4 * kh + kk) for kk in range(4)],
                                                       (XTh, XTl), natural(tt), kh == 0, kh == 1)
                                            if tt == TT - 1:
                                                r.then_inc(w_used.h, 1)
                                            elif kh == 1:
                                                r.then_inc(tile2_done.h, 1)

                            def wait_f(eng, n):
                                if n % 2:
                                    eng.wait_ge(w_used.h, CREDIT + c0 + n // 2 + 1)
                                else:
                                    eng.wait_ge(tile_done.h, tile_done.base + n // 2 + 1)

                            def wait_g(eng, n):
                                if n % 4 == 3:
                                    eng.wait_ge(w_used.h, CREDIT + c0 + 8 + 2 * (n // 4) + 2)
                                else:
                                    eng.wait_ge(tile2_done.h, tile2_done.base + 3 * (n // 4) + n % 4 + 1)

                            @block.scalar
                            def _(act):
                                a = nc.scalar
                                act.wait_ge(b_a.h, b_a.base + 1)
                                a.activation(lbt[:, :, :], lbt[:, :, :], ACT.Exp).then_inc(a_b.h, 1)
                                for n in range(16):
                                    wait_f(act, n)
                                    if n >= 2:
                                        act.wait_ge(tile_free.h, tile_free.base + n - 1)
                                    a.activation(SG[:, n % 2, :], PS[n % 4][:, :], ACT.Sigmoid).then_inc(a_b.h, 1)
                                for n in range(8, 16):
                                    wait_g(act, n)
                                    a.activation(G[:, n % 4, 512 * (n // 4 - 2):512 * (n // 4 - 1)], PS[4 + n % 4][:, :], ACT.Sigmoid).then_inc(a_b.h, 1)
                                act.wait_ge(tile2_free.h, tile2_free.base + 16)
                                for h in range(8):
                                    a.activation(LF[:, h, :], LF[:, h, :], ACT.Ln).then_inc(a_b.h, 1)

                            @block.vector
                            def _(dve):
                                v = nc.vector
                                link = InOrder(dve, dve_order)
                                link(v.memset(ones[:, :], 1.0))
                                link(v.memset(ones[:, 0:S:P], 0.0))
                                dve.wait_ge(loaded.h, loaded.base + 32)
                                link(v.tensor_copy(masks[:, :, :], masks32[:, :, :]))
                                m, s, one_less = (lb[:, k, :] for k in range(3))
                                link(v.tensor_tensor(m, lbt[:, 0, :], lbt[:, 1, :], ALU.max))
                                link(v.tensor_tensor(m, m, lbt[:, 2, :], ALU.max))
                                link(v.tensor_tensor(m, m, lbt[:, 3, :], ALU.max))
                                v.tensor_tensor(lbt[:, :, :], lbt[:, :, :], m.unsqueeze(1).to_broadcast([P, 4, 8]), ALU.subtract).then_inc(b_a.h, 1)
                                dve.wait_ge(a_b.h, a_b.base + 1)
                                link(v.tensor_tensor(s, lbt[:, 0, :], lbt[:, 1, :], ALU.add))
                                link(v.tensor_tensor(s, s, lbt[:, 2, :], ALU.add))
                                link(v.tensor_tensor(s, s, lbt[:, 3, :], ALU.add))
                                link(v.reciprocal(s, s))
                                link(v.tensor_tensor(lbt[:, :, :], lbt[:, :, :], s.unsqueeze(1).to_broadcast([P, 4, 8]), ALU.mult))
                                link(v.tensor_copy(m, lbt[:, 0, :]))
                                for k in range(1, layer + 1):
                                    link(v.tensor_tensor(m, m, lbt[:, k, :], ALU.add))
                                link(v.tensor_tensor(m, m, lbt[:, 0, :], ALU.subtract))
                                link(v.tensor_scalar(one_less, m, -1.0, 1.0, ALU.mult, ALU.add))
                                for n in range(16):
                                    wait_f(dve, n)
                                    dve.wait_ge(a_b.h, a_b.base + 2 + n)
                                    if n < 8:
                                        v.tensor_tensor(QF[:, n, :], PS[n % 4][:, :], SG[:, n % 2, :], ALU.mult).then_inc(tile_free.h, 1)
                                    else:
                                        h = n - 8
                                        link(v.tensor_scalar(LF[:, h, :], SG[:, n % 2, :], one_less[:, h:h + 1], m[:, h:h + 1], ALU.mult, ALU.add))
                                        v.tensor_scalar(KIN[:, h, :], LF[:, h, :], -1.0, 1.0, ALU.mult, ALU.add).then_inc(tile_free.h, 1)
                                for n in range(16):
                                    wait_g(dve, n)
                                    tt, half = n % 4, n // 4
                                    if n < 8:
                                        v.tensor_copy(IV[:, tt, 512 * half:512 * half + 512], PS[4 + tt][:, :]).then_inc(tile2_free.h, 1)
                                    else:
                                        dve.wait_ge(a_b.h, a_b.base + 10 + n)
                                        g = G[:, tt, 512 * (half - 2):512 * (half - 1)]
                                        v.tensor_tensor(g, g, PS[4 + tt][:, :], ALU.mult).then_inc(tile2_free.h, 1)
                                for h in range(8):
                                    dve.wait_ge(a_b.h, a_b.base + 26 + h)
                                    v.tensor_tensor_scan(LF[:, h, :], ones[:, :], LF[:, h, :], 0.0, ALU.mult, ALU.add)
                                link.done()
                        loaded.base += 32
                        b_a.base += 1
                        a_b.base += 33
                        tile_free.base += 16
                        tile2_free.base += 16
                        tile_done.base += 8
                        tile2_done.base += 12
                        pos[0] += 16
                    hgrn_heads(QF, KIN, LF, IV, masks)
                norm_phase("heads", gain=col[:, 18:19], extra={"post": 1.0, "gate": G})

        def hgrn_heads(QF, KIN, LF, IV, masks):
            PD, AE, DW, WF, LVF, KHC, TK, UD, SR, OE, DVE_TICK, POOL_TICK = (
                hg_lv[k] for k in ("pd", "ae", "dw", "wf", "lf", "kht", "tk", "ud", "sr", "oe", "dt", "pt"))
            with ExitStack() as c:
                W = sb("W", [P, 4, S], F32, c)
                AT = sb("AT", [P, TT, P], F32, c)
                KHT = sb("KHT", [P, 3, P], F32, c)
                ST = sb("ST", [P, 3, P], F32, c)
                EL = sb("EL", [P, 4], F32, c)
                SL = 10

                def head(ap, i, b):
                    return ap[:, bass.ds(i * 2 + b, 1), :].rearrange("p a s -> p (a s)")

                def w(b, n):
                    return W[:, (SL * b + n) % 4, :]

                def blocks(ap, lev):
                    return ap.rearrange("p (n c) -> p n c", c=P >> lev)

                def at(eng, s, i, per, k):
                    eng.wait_ge(s.h, i * (2 * per) + (s.base + k))
                with nc.Block() as block:
                    @block.gpsimd
                    def _(pool):
                        with pool.Fori(0, 4) as i:
                            for b in range(2):
                                g = head(LF, i, b)
                                for n in [0] + list(range(2, 9)):
                                    at(pool, WF, i, SL, SL * b + n - 3)
                                    pool.sem_inc(POOL_TICK.h, 1)
                                    if n == 0:
                                        g3 = g.rearrange("p (n c) -> p n c", c=P)
                                        x, y = g3[:, :, P - 1:P].to_broadcast([P, TT, P]), g3
                                        o = w(b, n).rearrange("p (n c) -> p n c", c=P)
                                    else:
                                        lev = n - 2
                                        g3, half = blocks(g, lev), P >> (lev + 1)
                                        x, y = g3, g3[:, :, half - 1:half].to_broadcast([P, S // (2 * half), 2 * half])
                                        o = blocks(w(b, n), lev)
                                    pool.tensor_tensor(o, x, y, ALU.subtract).then_inc(PD.h, 1)

                    @block.scalar
                    def _(act):
                        a = nc.scalar

                        def out(i, b):
                            at(act, WF, i, SL, SL * (b + 1))
                            a.activation(Y[:, :, bass.ds(i * 256 + P * b, P)], PS[6 + b][:, :].rearrange("p (n v) -> p n v", n=TT),
                                         ACT.Copy).then_inc(OE.h, 1)
                        with act.Fori(0, 4) as i:
                            for b in range(2):
                                for n in range(SL):
                                    if n in (1, 9):
                                        at(act, WF, i, SL, SL * b + n - 3)
                                    else:
                                        at(act, PD, i, 8, 8 * b + (1 if n == 0 else n))
                                    x = w(b, n)
                                    if n == 1:
                                        r = a.activation(x, head(KIN, i, b), ACT.Copy)
                                    elif n == 9:
                                        r = a.activation(x, head(LF, i, b), ACT.Exp)
                                    elif n == 0:
                                        r = a.activation(x, x, ACT.Exp)
                                    else:
                                        x3, half = blocks(x, n - 2), P >> (n - 1)
                                        a.activation(x3[:, :, 0:half], x3[:, :, 0:half], ACT.Exp, scale=-1.0)
                                        r = a.activation(x3[:, :, half:], x3[:, :, half:], ACT.Exp)
                                    r.then_inc(AE.h, 1)
                                    if n == 3:
                                        at(act, TK, i, 1, b + 1)
                                        a.activation(KHT[:, :, :], PS[4][:, 0:3 * P].rearrange("p (n k) -> p n k", n=3), ACT.Copy).then_inc(KHC.h, 1)
                                    if n == 5 and b == 1:
                                        out(i, 0)
                            out(i, 1)

                    @block.tensor
                    def _(pe):
                        with pe.Fori(0, 4) as i:
                            for b in range(2):
                                iv = lambda cc: IV[:, cc, bass.ds(i * 256 + P * b, P)]
                                for n in range(SL):
                                    x = w(b, n)
                                    if n == 0:
                                        at(pe, DW, i, 9, 9 * b + 1)
                                        at(pe, KHC, i, 1, b)
                                        for cc in range(3):
                                            r = nc.tensor.transpose(PS[4][:, P * cc:P * cc + P], x[:, P * cc:P * cc + P], ident[:, :])
                                        r.then_inc(TK.h, 1)
                                        continue
                                    if n < 9:
                                        if n == 1:
                                            at(pe, AE, i, SL, SL * b + 2)
                                        else:
                                            at(pe, DW, i, 9, 9 * b + n)
                                        k = n - 1
                                        at(pe, LVF, i, 8, 8 * b + k - 3)
                                        for cc in range(TT):
                                            cs = slice(P * cc, P * cc + P)
                                            rhs = QF[:, bass.ds(i * 2 + b, 1), cs].rearrange("p a s -> p (a s)") if n == 1 else x[:, cs]
                                            r = nc.tensor.matmul(PS[k % 4][:, cs], x[:, cs], rhs, start=True, stop=True)
                                        r.then_inc(WF.h, 2 if n == 1 else 1)
                                    if n == 5:
                                        at(pe, KHC, i, 1, b + 1)
                                        at(pe, SR, i, 1, b)
                                        for cc in range(3):
                                            r = nc.tensor.matmul(PS[5][:, P * cc:P * cc + P], KHT[:, cc, :], iv(cc), start=True, stop=True)
                                        r.then_inc(UD.h, 1)
                                    if n == 9:
                                        at(pe, DW, i, 9, 9 * b + 9)
                                        at(pe, SR, i, 1, b + 1)
                                        at(pe, OE, i, 1, b - 1)
                                        for cc in range(TT):
                                            cs = slice(P * cc, P * cc + P)
                                            r = nc.tensor.matmul(PS[6 + b][:, cs], AT[:, cc, :], iv(cc), start=True, stop=cc == 0)
                                            if cc:
                                                r = nc.tensor.matmul(PS[6 + b][:, cs], x[:, cs], ST[:, cc - 1, :], start=False, stop=True)
                                        r.then_inc(WF.h, 1)

                    @block.vector
                    def _(dve):
                        v = nc.vector
                        link = InOrder(dve, dve_order)
                        link(v.memset(AT[:, :, :], 0.0))
                        with dve.Fori(0, 4) as i:
                            link.enter(i, 2 * (1 + 7 + 2))
                            for b in range(2):
                                def merge(k):
                                    at(dve, WF, i, SL, SL * b + k + 2)
                                    dve.sem_inc(DVE_TICK.h, 1)
                                    lev = HG_LEVELS if k == 0 else k - 1
                                    v.copy_predicated(AT[:, :, :], masks[:, lev:lev + 1, :].to_broadcast([P, TT, P]),
                                                      PS[k % 4][:, :].rearrange("p (n t) -> p n t", n=TT)).then_inc(LVF.h, 1)
                                    at(dve, LVF, i, 8, 8 * b + k + 1)
                                for n in range(SL):
                                    x = w(b, n)
                                    if n != 1:
                                        at(dve, AE, i, SL, SL * b + n + 1)
                                    if n == 0:
                                        v.tensor_tensor(x, x, head(KIN, i, b), ALU.mult).then_inc(DW.h, 1)
                                    elif n == 9:
                                        link(v.tensor_copy(EL[:, :], x[:, P - 1::P]))
                                        v.tensor_tensor(x, x, head(QF, i, b), ALU.mult).then_inc(DW.h, 1)
                                    elif n >= 2:
                                        x3, half = blocks(x, n - 2), P >> (n - 1)
                                        kin, q = blocks(head(KIN, i, b), n - 2), blocks(head(QF, i, b), n - 2)
                                        link(v.tensor_tensor(x3[:, :, 0:half], x3[:, :, 0:half], kin[:, :, 0:half], ALU.mult))
                                        v.tensor_tensor(x3[:, :, half:], x3[:, :, half:], q[:, :, half:], ALU.mult).then_inc(DW.h, 1)
                                        merge(n - 2)
                                merge(7)
                                at(dve, UD, i, 1, b + 1)
                                link(v.tensor_copy(ST[:, 0, :], PS[5][:, 0:P]))
                                for cc in (1, 2):
                                    r = v.scalar_tensor_tensor(ST[:, cc, :], ST[:, cc - 1, :], EL[:, cc:cc + 1], PS[5][:, P * cc:P * cc + P], ALU.mult, ALU.add)
                                    if cc == 1:
                                        link(r)
                                r.then_inc(SR.h, 1)
                            link.leave(4)
                        link.done()
                for s, n in ((PD, 64), (AE, 80), (DW, 72), (WF, 80), (LVF, 64), (KHC, 8), (TK, 8), (UD, 8), (SR, 8), (OE, 8)):
                    s.base += n
        ssm_in = nc.dram_tensor("ssm_in", (P, SSM_PAIRS, 2, P), F32, kind="Internal").ap()
        ssm_out = nc.dram_tensor("ssm_out", (P, SSM_PAIRS, 4, P), F32, kind="Internal").ap()
        lag_kernel = nc.dram_tensor("lag_kernel", (SSM_C, 2 * SSM_PAIRS, 15 * SSM_C), F32, kind="Internal").ap()
        u_dram = nc.dram_tensor("u_dram", (D, S), F32, kind="Internal").ap()
        y_dram = nc.dram_tensor("y_dram", (D, S), F32, kind="Internal").ap()
        QP = 8
        sg_names = dict(ready=signal("ssm_ready"), w2t=signal("ssm_transposed"), w2c=signal("ssm_transposed_copied", CREDIT),
                        hd=signal("ssm_lags_done"), hc=signal("ssm_lags_copied", CREDIT), st_=signal("ssm_stored", CREDIT),
                        st2=signal("ssm_stored_lags", CREDIT), st3=signal("ssm_stored_out", CREDIT),
                        vin=signal("ssm_inputs_done"), vfree=signal("ssm_inputs_free", CREDIT), sprev=signal("ssm_states"),
                        yd=signal("ssm_y_done", CREDIT), yf=signal("ssm_y_free", CREDIT),
                        tick=signal("pe_tick"), uin=signal("ssm_u_in"), ld0=signal("ssm_loaded_even"), ld1=signal("ssm_loaded_odd"))

        def ssm_mixer():
            with ExitStack() as c:
                E = sb("E", [P, 2, SSM_PAIRS, SSM_N], F32, c)
                RD = sb("RD", [P, SSM_PAIRS, SSM_N], F32, c)
                ssm_prepare(E, RD)
                norm_phase("pre", gain=col[:, KT:2 * KT])
                ssm_project()
                with ExitStack() as c2:
                    ssm_core(E, RD, c2)
            ssm_gate()
            split_features(lambda k: YF[:, k, :])

        def ssm_prepare(E, RD):
            PI2 = 2 * math.pi
            C1 = 6.28125
            C2 = float(np.float32(PI2 - C1))
            C3 = PI2 - C1 - C2
            MAGIC = 1.5 * 2 ** 23
            R, W2T_, W2C, HD, HC, ST1, ST2, ST3 = (sg_names[k] for k in ("ready", "w2t", "w2c", "hd", "hc", "st_", "st2", "st3"))
            with ExitStack() as c:
                A = sb("A", [P, 3, SSM_PAIRS], F32, c)
                BB = sb("BB", [P, 2, SSM_PAIRS, SSM_C], F32, c)
                CC = sb("CC", [P, 2, SSM_PAIRS, SSM_C], F32, c)
                s_ = sb("s_", [P, 16, SSM_PAIRS], F32, c)
                PW = sb("PW", [P, 2, 9, SSM_PAIRS], F32, c)
                PR = sb("PR", [P, 2, 8, SSM_PAIRS], F32, c)
                BQ = sb("BQ", [P, 2, QP, SSM_C], F32, c)
                CA = sb("CA", [P, 2, QP, 9, SSM_C], F32, c)
                W2 = sb("W2", [P, 2, QP, 8, SSM_C], F32, c)
                W2T = sb("W2T", [P, QP, 2, P], F32, c)
                T = sb("T", [P, 2, QP * 9 * SSM_C], F32, c)
                HS = sb("HS", [SSM_C, 2 * QP, 15 * SSM_C], F32, c)
                dcol = sb("dcol", [SSM_C, 2 * SSM_PAIRS], F32, c)
                eye = sb("eye", [SSM_C, SSM_C], F32, c)
                skip = sb("skip", [SSM_C, 2 * SSM_PAIRS, SSM_C], F32, c)
                n_loads = 9
                with nc.Block() as block:
                    @block.sync
                    def _(sp):
                        for d, x in ((A[:, 0, :], "ssm_a_re"), (A[:, 1, :], "ssm_a_im"), (A[:, 2, :], "ssm_log_dt"),
                                     (BB[:, 0], "ssm_b_re"), (BB[:, 1], "ssm_b_im"), (CC[:, 0], "ssm_c_re"), (CC[:, 1], "ssm_c_im"),
                                     (dcol[:, :], "ssm_d_rows"), (eye[:, :], "eye16")):
                            sp.dma_start(d, t[x]).then_inc(loaded.h, 16)
                        with sp.Fori(0, 4) as q:
                            sp.wait_ge(R.h, q + (R.base + 1))
                            for x in range(2):
                                sp.dma_start(ssm_out[:, bass.ds(q * QP, QP), 2 + x, :].rearrange("p a (n c) -> p a n c", c=SSM_C),
                                             CA[:, x, :, 1:9, :]).then_inc(ST1.h, 16)
                            sp.wait_ge(W2C.h, q * 4 + (W2C.base + 4))
                            sp.dma_start(ssm_in[:, bass.ds(q * QP, QP)], W2T[:, :, :, :]).then_inc(ST3.h, 16)
                            sp.wait_ge(HC.h, q + (HC.base + 1))
                            sp.dma_start(lag_kernel[:, bass.ds(q * 2 * QP, 2 * QP), :], HS[:, :, :]).then_inc(ST2.h, 16)
                        sp.wait_ge(ST2.h, ST2.base + 64)
                        for st_ in range(SSM_T):
                            src = lag_kernel[:, :, SSM_C * (7 - st_):SSM_C * (7 - st_) + P].rearrange("c (a g) n -> c a g n", g=2)
                            for g in range(2):
                                sp.dma_start(ssm_out[SSM_C * st_:SSM_C * st_ + SSM_C, :, g, :], src[:, :, g, :]).then_inc(stored.h, 16)
                        sp.wait_ge(stored.h, stored.base + 16 * 16)
                        sp.wait_ge(ST1.h, ST1.base + 128)
                        sp.wait_ge(ST3.h, ST3.base + 64)

                    @block.scalar
                    def _(act):
                        a = nc.scalar
                        act.wait_ge(loaded.h, loaded.base + 16 * n_loads)
                        a.activation(s_[:, 0, :], A[:, 2, :], ACT.Exp).then_inc(a_b.h, 1)
                        act.wait_ge(b_a.h, b_a.base + 1)
                        a.activation(s_[:, 3, :], s_[:, 1, :], ACT.Exp)
                        a.activation(s_[:, 4, :], s_[:, 1, :], ACT.Exp, scale=float(SSM_T)).then_inc(a_b.h, 1)
                        act.wait_ge(b_a.h, b_a.base + 2)
                        a.activation(s_[:, 6, :], s_[:, 5, :], ACT.Sin)
                        a.activation(s_[:, 7, :], s_[:, 5, :], ACT.Sin, scale=0.5).then_inc(a_b.h, 1)
                        with act.Fori(0, 4) as q:
                            for n in range(4):
                                act.wait_ge(W2T_.h, q * 4 + (W2T_.base + n + 1))
                                if n == 0:
                                    act.wait_ge(ST3.h, q * 16 + ST3.base)
                                a.activation(W2T[:, 2 * n:2 * n + 2, :, :].rearrange("p a b c -> p (a b c)"), PS[n][:, :], ACT.Copy).then_inc(W2C.h, 1)

                    @block.tensor
                    def _(pe):
                        with pe.Fori(0, 4) as q:
                            pe.wait_ge(R.h, q + (R.base + 1))
                            pe.wait_ge(W2C.h, q * 4 + W2C.base)
                            for n in range(4):
                                for x in range(4):
                                    r = nc.tensor.transpose(PS[n][:, P * x:P * x + P], W2[:, x % 2, 2 * n + x // 2].rearrange("p n c -> p (n c)"), ident[:, :])
                                r.then_inc(W2T_.h, 1)
                            pe.wait_ge(HC.h, q + HC.base)
                            pe.sem_inc(sg_names["tick"].h, 1)
                            for g in range(2 * QP):
                                lo, pr = 64 * (g % 2), g // 2
                                for x in range(2):
                                    r = nc.tensor.matmul(PS[4 + 2 * (g % 2) + pr // 4][0:SSM_C, P * (pr % 4):P * (pr % 4) + P], BQ[lo:lo + 64, x, pr, :],
                                                         CA[lo:lo + 64, x, pr, 0:8, :].rearrange("p n c -> p (n c)"), start=x == 0, stop=x == 1)
                            r.then_inc(HD.h, 1)

                    @block.vector
                    def _(dve):
                        v = nc.vector
                        link = InOrder(dve, dve_order)

                        def mul(o, x, y):
                            link(v.tensor_tensor(o, x, y, ALU.mult))

                        def cmul(o, x, y, t1, t2, negate_im=False):
                            mul(t1, x[0], y[0])
                            mul(t2, x[1], y[1])
                            link(v.tensor_tensor(o[0], t1, t2, ALU.subtract))
                            mul(t1, x[0], y[1])
                            mul(t2, x[1], y[0])
                            if negate_im:
                                link(v.tensor_scalar(t1, t1, -1.0, None, ALU.mult))
                            link(v.tensor_tensor(o[1], t1, t2, ALU.subtract if negate_im else ALU.add))
                        sm = lambda k: s_[:, k, :]
                        dve.wait_ge(loaded.h, loaded.base + 16 * n_loads)
                        link(v.memset(HS[:, :, 0:7 * SSM_C], 0.0))
                        link(v.tensor_tensor(skip[:, :, :], eye[:, :].unsqueeze(1).to_broadcast([SSM_C, 2 * SSM_PAIRS, SSM_C]),
                                             dcol[:, :].unsqueeze(2).to_broadcast([SSM_C, 2 * SSM_PAIRS, SSM_C]), ALU.mult))
                        dve.wait_ge(a_b.h, a_b.base + 1)
                        v.tensor_tensor(sm(1), A[:, 0, :], sm(0), ALU.mult).then_inc(b_a.h, 1)
                        mul(sm(2), A[:, 1, :], sm(0))
                        link(v.tensor_scalar(sm(8), sm(2), 1.0 / PI2, None, ALU.mult))
                        link(v.tensor_scalar(sm(8), sm(8), MAGIC, None, ALU.add))
                        link(v.tensor_scalar(sm(8), sm(8), -MAGIC, None, ALU.add))
                        link(v.scalar_tensor_tensor(sm(2), sm(8), -C1, sm(2), ALU.mult, ALU.add))
                        link(v.scalar_tensor_tensor(sm(2), sm(8), -C2, sm(2), ALU.mult, ALU.add))
                        link(v.scalar_tensor_tensor(sm(2), sm(8), -C3, sm(2), ALU.mult, ALU.add))
                        v.tensor_scalar(sm(5), sm(2), math.pi, -math.pi, ALU.min, ALU.max).then_inc(b_a.h, 1)
                        dve.wait_ge(a_b.h, a_b.base + 3)
                        mul(sm(8), sm(7), sm(7))
                        link(v.tensor_scalar(sm(9), sm(8), -2.0, 1.0, ALU.mult, ALU.add))
                        pw = lambda n, m=1: (PW[:, 0, n:n + m, :], PW[:, 1, n:n + m, :])
                        link(v.memset(PW[:, 0, 0:1, :], 1.0))
                        link(v.memset(PW[:, 1, 0:1, :], 0.0))
                        mul(PW[:, 0, 1, :], sm(3), sm(9))
                        mul(PW[:, 1, 1, :], sm(3), sm(6))
                        tw = lambda m: tuple(T[:, x, 0:m * SSM_PAIRS].rearrange("p (n a) -> p n a", n=m) for x in range(2))
                        for m in (1, 2, 4):
                            top = tuple(x.to_broadcast([P, m, SSM_PAIRS]) for x in pw(m))
                            cmul(pw(m + 1, m), pw(1, m), top, *tw(m))
                        for n in range(8):
                            link(v.tensor_copy(PR[:, :, n, :], PW[:, :, 7 - n, :]))
                        link(v.tensor_scalar(sm(10), PW[:, 0, 1, :], -1.0, None, ALU.add))
                        mul(sm(11), A[:, 0, :], A[:, 0, :])
                        mul(sm(12), A[:, 1, :], A[:, 1, :])
                        link(v.tensor_tensor(sm(11), sm(11), sm(12), ALU.add))
                        link(v.reciprocal(sm(11), sm(11)))
                        mul(sm(12), sm(10), A[:, 0, :])
                        mul(sm(13), PW[:, 1, 1, :], A[:, 1, :])
                        link(v.tensor_tensor(sm(12), sm(12), sm(13), ALU.add))
                        mul(sm(12), sm(12), sm(11))
                        mul(sm(13), PW[:, 1, 1, :], A[:, 0, :])
                        mul(sm(14), sm(10), A[:, 1, :])
                        link(v.tensor_tensor(sm(13), sm(13), sm(14), ALU.subtract))
                        mul(sm(13), sm(13), sm(11))
                        with dve.Fori(0, 4) as q:
                            link.enter(q, 6 + 7 + 6 + 5)
                            pr = bass.ds(q * QP, QP)
                            dve.wait_ge(ST1.h, q * 32 + ST1.base)
                            dve.wait_ge(HC.h, q + HC.base)
                            bb = [BB[:, x, pr, :] for x in range(2)]
                            ff = [s_[:, 12 + x, pr].unsqueeze(2).to_broadcast([P, QP, SSM_C]) for x in range(2)]
                            tb = [T[:, x, 0:QP * SSM_C].rearrange("p (a c) -> p a c", c=SSM_C) for x in range(2)]
                            cmul((BQ[:, 0], BQ[:, 1]), ff, bb, *tb)
                            sh = [P, QP, 9, SSM_C]
                            aa = [PW[:, x, :, pr].rearrange("p n a -> p a n").unsqueeze(3).to_broadcast(sh) for x in range(2)]
                            cc = [CC[:, x, pr, :].unsqueeze(2).to_broadcast(sh) for x in range(2)]
                            t9 = [T[:, x, :].rearrange("p (a n c) -> p a n c", n=9, c=SSM_C) for x in range(2)]
                            cmul((CA[:, 0], CA[:, 1]), aa, cc, *t9, negate_im=True)
                            sh = [P, QP, 8, SSM_C]
                            aa = [PR[:, x, :, pr].rearrange("p n a -> p a n").unsqueeze(3).to_broadcast(sh) for x in range(2)]
                            cc = [BQ[:, x].unsqueeze(2).to_broadcast(sh) for x in range(2)]
                            t8 = [T[:, x, 0:QP * P].rearrange("p (a n c) -> p a n c", n=8, c=SSM_C) for x in range(2)]
                            cmul((W2[:, 0], W2[:, 1]), aa, cc, *t8)
                            dve.sem_inc(R.h, 1)
                            dve.wait_ge(HD.h, q + (HD.base + 1))
                            dve.wait_ge(ST2.h, q * 16 + ST2.base)
                            for n in range(4):
                                g0 = 8 * (n % 2) + n // 2
                                link(v.tensor_copy(HS[:, g0:g0 + 7:2, 7 * SSM_C:], PS[4 + n][0:SSM_C, :].rearrange("p (g n) -> p g n", g=4)))
                            lag0 = HS[:, :, 7 * SSM_C:8 * SSM_C]
                            link(v.tensor_tensor(lag0, lag0, skip[:, bass.ds(q * 2 * QP, 2 * QP), :], ALU.add))
                            dve.sem_inc(HC.h, 1)
                            link.leave(4)
                        u = [(sm(9), sm(6)), (sm(10), sm(11)), (sm(12), sm(13))]
                        t2 = (sm(14), sm(15))
                        cur = u[0]
                        for k in range(3):
                            nxt = u[1 + k % 2]
                            cmul(nxt, cur, cur, *t2)
                            cur = nxt
                        link(v.memset(E[:, 0, :, 0:1], 1.0))
                        link(v.memset(E[:, 1, :, 0:1], 0.0))
                        for k in range(6):
                            m = 1 << k
                            cu = tuple(x.unsqueeze(2).to_broadcast([P, SSM_PAIRS, m]) for x in cur)
                            tt_ = tuple(T[:, x, 0:SSM_PAIRS * m].rearrange("p (a n) -> p a n", n=m) for x in range(2)) if m <= 32 else None
                            cmul(tuple(E[:, x, :, m:2 * m] for x in range(2)), tuple(E[:, x, :, 0:m] for x in range(2)), cu, *tt_)
                            nxt = u[1 + (k + 1) % 2]
                            cmul(nxt, cur, cur, *t2)
                            cur = nxt
                        link(v.tensor_copy(RD[:, :, :], sm(4).unsqueeze(2).to_broadcast([P, SSM_PAIRS, SSM_N])))
                        link(v.memset(RD[:, :, 0:1], 0.0))
                        link.done()
                loaded.base += 16 * n_loads
                a_b.base += 3
                b_a.base += 2
                R.base += 4
                ST1.base += 128
                ST2.base += 64
                ST3.base += 64
                W2C.base += 16
                W2T_.base += 16
                HD.base += 4
                HC.base += 4
                stored.base += 256

        def ssm_project():
            c0 = pos[0]
            with ExitStack() as c:
                UF = sb("UF", [P, KT, SSM_T, SSM_N], F32, c)
                with nc.Block() as block:
                    @block.sync
                    def _(sp):
                        sp_stream(sp, 8)

                    @block.gpsimd
                    def _(pool):
                        pool_stream(pool, 8)

                    @block.tensor
                    def _(pe):
                        with pe.Fori(0, 4) as i:
                            for n in range(4):
                                if n % 2 == 0:
                                    pe.wait_ge(w_split.h, i * 2 + (c0 + n // 2 + 1))
                                pe.wait_ge(tile_free.h, i * 4 + (tile_free.base + n - 3))
                                r = f_tile(PS[n][:, :], (c0 + n // 2) % SPLIT, n % 2)
                                r.then_inc((w_used if n % 2 else tile_done).h, 1)

                    def wait_f(eng, n):
                        if n % 2:
                            eng.wait_ge(w_used.h, CREDIT + c0 + n // 2 + 1)
                        else:
                            eng.wait_ge(tile_done.h, tile_done.base + n // 2 + 1)

                    @block.scalar
                    def _(act):
                        for n in range(16):
                            wait_f(act, n)
                            if n < 8:
                                nc.scalar.activation(UF[:, n], PS[n % 4][:, :].rearrange("p (n s) -> p s n", s=SSM_T), ACT.Copy).then_inc(tile_free.h, 1)
                                if n == 7:
                                    act.wait_ge(tile_free.h, tile_free.base + 8)
                                    act.dma_start(u_dram.rearrange("(k p) s -> p k s", p=P), UF[:, :, :, :].rearrange("p k s n -> p k (s n)")).then_inc(stored.h, 16)
                            else:
                                nc.scalar.activation(YF[:, n - 8, :], PS[n % 4][:, :], ACT.Sigmoid).then_inc(a_b.h, 1)
                        act.wait_ge(stored.h, stored.base + 16)

                    @block.vector
                    def _(dve):
                        for n in range(8, 16):
                            dve.wait_ge(a_b.h, a_b.base + n - 7)
                            nc.vector.tensor_tensor(YF[:, n - 8, :], YF[:, n - 8, :], PS[n % 4][:, :], ALU.mult).then_inc(tile_free.h, 1)
            tile_free.base += 16
            tile_done.base += 8
            a_b.base += 8
            stored.base += 16
            pos[0] += 8

        def ssm_core(E, RD, c):
            VIN, VFREE, SPREV, YD, YFR = (sg_names[k] for k in ("vin", "vfree", "sprev", "yd", "yf"))
            LD = [sg_names["ld0"], sg_names["ld1"]]
            UIN = sg_names["uin"]
            FP = 4
            U = sb("U", [P, 2 * SSM_PAIRS, SSM_N], F32, c)
            UB = sb("UB", [P, 2, 2 * FP, SSM_N], F32, c)
            YG = sb("YG", [P, 2 * SSM_PAIRS, SSM_N], F32, c)
            MI = sb("MI", [P, 2, FP, 2, P], F32, c)
            MO = sb("MO", [P, 2, FP, 4, P], F32, c)
            SP_ = sb("SP_", [P, 2, 2, FP, SSM_N], F32, c)
            Z = sb("Z", [P, 2, FP, SSM_N], F32, c)
            T = sb("T2", [P, 2, FP, SSM_N], F32, c)
            with nc.Block() as block:
                @block.sync
                def _(sp):
                    for s in range(SSM_T):
                        sp.dma_start(U[SSM_C * s:SSM_C * s + SSM_C, :, :],
                                     u_dram.rearrange("(g c) (s n) -> s c g n", c=SSM_C, s=SSM_T)[s]).then_inc(loaded.h, 16)

                @block.scalar
                def _(act):
                    a = nc.scalar
                    act.wait_ge(loaded.h, loaded.base + 16 * SSM_T)

                    def evacuate(i, b):
                        yg = YG[:, :, :].rearrange("p (a g) n -> p a g n", g=2)
                        for g in range(2):
                            r = a.activation(yg[:, bass.ds(i * 8 + FP * b, FP), g, :], PS[4 + b + 2 * g][:, 0:256].rearrange("p (a n) -> p a n", a=FP), ACT.Copy)
                        r.then_inc(YFR.h, 1)
                    with act.Fori(0, 4) as i:
                        for b in range(2):
                            act.wait_ge(YD.h, i * 2 + (YD.base + b - 1))
                            pr = bass.ds(i * 8 + FP * b, FP)
                            act.dma_start(MI[:, b], ssm_in[:, pr]).then_inc(LD[b].h, 16)
                            act.dma_start(MO[:, b], ssm_out[:, pr]).then_inc(LD[b].h, 16)
                            a.activation(UB[:, b].rearrange("p g n -> p (g n)"),
                                         U[:, bass.ds(i * 16 + 8 * b, 8), :].rearrange("p g n -> p (g n)"), ACT.Copy).then_inc(UIN.h, 1)
                            if b == 1:
                                act.wait_ge(YD.h, i * 2 + (YD.base + 1))
                                evacuate(i, 0)
                        act.wait_ge(YD.h, i * 2 + (YD.base + 2))
                        evacuate(i, 1)
                    act.wait_ge(YFR.h, YFR.base + 8)
                    for s in range(SSM_T):
                        act.dma_start(y_dram.rearrange("(g c) (s n) -> s c g n", c=SSM_C, s=SSM_T)[s],
                                      YG[SSM_C * s:SSM_C * s + SSM_C, :, :]).then_inc(stored.h, 16)
                    act.wait_ge(stored.h, stored.base + 16 * SSM_T)

                @block.tensor
                def _(pe):
                    with pe.Fori(0, 4) as i:
                        for b in range(2):
                            pe.wait_ge(UIN.h, i * 2 + (UIN.base + b + 1))
                            pe.wait_ge(LD[b].h, i * 32 + (LD[b].base + 32))
                            pe.wait_ge(VFREE.h, i * 2 + (VFREE.base + b - 1))
                            for x in range(2):
                                for g in range(2 * FP):
                                    lo = 64 * (g % 2)
                                    r = nc.tensor.matmul(PS[b][lo:lo + 64, 256 * x + 64 * (g // 2):256 * x + 64 * (g // 2) + 64],
                                                         MI[:, b, g // 2, x, lo:lo + 64],
                                                         UB[:, b, g, :], start=True, stop=True)
                            r.then_inc(VIN.h, 1)
                        for b in range(2):
                            pe.wait_ge(SPREV.h, i * 2 + (SPREV.base + b + 1))
                            pe.wait_ge(YFR.h, i * 2 + (YFR.base + b - 1))
                            for g in range(2 * FP):
                                lo, o = 64 * (g % 2), PS[4 + b + 2 * (g % 2)][:, 64 * (g // 2):64 * (g // 2) + 64]
                                nc.tensor.matmul(o, MO[:, b, g // 2, g % 2, :], UB[:, b, g, :], start=True, stop=False)
                                for x in range(2):
                                    r = nc.tensor.matmul(o, MO[lo:lo + 64, b, g // 2, 2 + x, :], SP_[lo:lo + 64, b, x, g // 2, :], start=False, stop=x == 1)
                            r.then_inc(YD.h, 1)

                @block.vector
                def _(dve):
                    v = nc.vector
                    link = InOrder(dve, dve_order)
                    link(v.memset(SP_[:, :, :, :, 0:1].rearrange("p a b c d -> p (a b) (c d)"), 0.0))
                    with dve.Fori(0, 4) as i:
                        link.enter(i, 2 * 13)
                        for b in range(2):
                            pr = bass.ds(i * 8 + FP * b, FP)
                            er, ei = (E[:, x, pr, :] for x in range(2))
                            vr, vi = (PS[b][:, 256 * x:256 * x + 256].rearrange("p (a n) -> p a n", a=FP) for x in range(2))
                            t0, t1 = T[:, 0], T[:, 1]
                            dve.wait_ge(VIN.h, i * 2 + (VIN.base + b + 1))
                            link(v.tensor_tensor(t0, vr, er, ALU.mult))
                            link(v.tensor_tensor(t1, vi, ei, ALU.mult))
                            link(v.tensor_tensor(Z[:, 0], t0, t1, ALU.add))
                            link(v.tensor_tensor(t0, vi, er, ALU.mult))
                            v.tensor_tensor(t1, vr, ei, ALU.mult).then_inc(VFREE.h, 1)
                            dve.wait_ge(VFREE.h, i * 2 + (VFREE.base + b + 1))
                            link(v.tensor_tensor(Z[:, 1], t0, t1, ALU.subtract))
                            rd = RD[:, pr, :].rearrange("p a n -> p (a n)")
                            for x in range(2):
                                z = Z[:, x].rearrange("p a n -> p (a n)")
                                link(v.tensor_tensor_scan(z, rd, z, 0.0, ALU.mult, ALU.add))
                            n1 = slice(0, SSM_N - 1)
                            er, ei = (E[:, x, pr, n1] for x in range(2))
                            z0, z1, t0, t1 = Z[:, 0, :, n1], Z[:, 1, :, n1], T[:, 0, :, n1], T[:, 1, :, n1]
                            link(v.tensor_tensor(t0, z0, er, ALU.mult))
                            link(v.tensor_tensor(t1, z1, ei, ALU.mult))
                            dve.wait_ge(YD.h, i * 2 + (YD.base + b - 1))
                            link(v.tensor_tensor(SP_[:, b, 0, :, 1:], t0, t1, ALU.subtract))
                            link(v.tensor_tensor(t0, z0, ei, ALU.mult))
                            link(v.tensor_tensor(t1, z1, er, ALU.mult))
                            link(v.tensor_tensor(SP_[:, b, 1, :, 1:], t0, t1, ALU.add))
                            dve.sem_inc(SPREV.h, 1)
                        link.leave(4)
                    link.done()
            loaded.base += 16 * SSM_T
            stored.base += 16 * SSM_T
            for s in (VIN, VFREE, SPREV, YD, YFR, UIN):
                s.base += 8
            for s in LD:
                s.base += 128

        def ssm_gate():
            c0 = pos[0]
            with ExitStack() as c:
                GF = sb("GF", [P, KT, S], F32, c)
                SG = sb("SG", [P, 2, S], F32, c)
                bcol = sb("bcol", [P, KT], F32, c)
                with nc.Block() as block:
                    @block.sync
                    def _(sp):
                        sp.dma_start(GF[:, :, :], y_dram.rearrange("(k p) s -> p k s", p=P)).then_inc(loaded.h, 16)
                        sp.dma_start(bcol[:, :], t["ssm_b_glu"]).then_inc(loaded.h, 16)
                        sp_stream(sp, 4)

                    @block.gpsimd
                    def _(pool):
                        pool_stream(pool, 4)

                    @block.tensor
                    def _(pe):
                        for n in range(8):
                            if n % 2 == 0:
                                arrived(pe, c0 + n // 2)
                            if n == 0:
                                pe.wait_ge(b_p.h, b_p.base + 8)
                            pe.wait_ge(tile_free.h, tile_free.base + n - 3)
                            r = f_tile(PS[n % 4][:, :], (c0 + n // 2) % SPLIT, n % 2)
                            r.then_inc((w_used if n % 2 else tile_done).h, 1)

                    @block.scalar
                    def _(act):
                        a = nc.scalar
                        act.wait_ge(loaded.h, loaded.base + 32)
                        for n in range(8):
                            a.activation(GF[:, n, :], GF[:, n, :], ACT.Gelu_apprx_tanh).then_inc(a_b.h, 1)
                            act.wait_ge(a_b.h, a_b.base + 2 * n + 1)
                            a.activation(XTh[:, n, :], GF[:, n, :], ACT.Copy).then_inc(a_b.h, 1)
                        for n in range(8):
                            if n % 2:
                                act.wait_ge(w_used.h, CREDIT + c0 + n // 2 + 1)
                            else:
                                act.wait_ge(tile_done.h, tile_done.base + n // 2 + 1)
                            if n >= 2:
                                act.wait_ge(b_a.h, b_a.base + n - 1)
                            a.activation(SG[:, n % 2, :], PS[n % 4][:, :], ACT.Sigmoid, bias=bcol[:, n:n + 1]).then_inc(tile_free.h, 1)

                    @block.vector
                    def _(dve):
                        v = nc.vector
                        link = InOrder(dve, dve_order)
                        for n in range(8):
                            dve.wait_ge(a_b.h, a_b.base + 2 * n + 2)
                            v.tensor_tensor(XTl[:, n, :], GF[:, n, :], XTh[:, n, :].bitcast(F32), ALU.subtract).then_inc(b_p.h, 1)
                        for n in range(8):
                            dve.wait_ge(tile_free.h, tile_free.base + n + 1)
                            link(v.tensor_tensor(SG[:, n % 2, :], SG[:, n % 2, :], GF[:, n, :], ALU.mult))
                            y = YF[:, n, :].rearrange("p (n s) -> p n s", s=SSM_T)
                            v.tensor_tensor(y, y, SG[:, n % 2, :].rearrange("p (s n) -> p n s", s=SSM_T), ALU.mult).then_inc(b_a.h, 1)
                        link.done()
            loaded.base += 32
            a_b.base += 16
            b_a.base += 8
            b_p.base += 8
            tile_free.base += 8
            tile_done.base += 4
            pos[0] += 4
        setup()
        if "attn" in STAGES:
            norm_phase("pre", gain=col[:, 0:KT])
            dilated_attention()
            out_phase(None)
            norm_phase("rms_add", vecs=(t["attn_post_norm"][0],), transposed=False)
        if "ssm" in STAGES:
            ssm_mixer()
            out_phase(None)
            norm_phase("rms_add", vecs=(t["ssm_post_norm"][0],), transposed=False)
        for layer in range(N_LAYERS):
            if f"layer{layer}" not in STAGES:
                continue
            norm_phase("plain")
            kind, j = layer % 3, layer // 3
            if kind == 0:
                diff_attention(layer, j)
            elif kind == 1:
                hgrn(layer, j)
            else:
                sliding_attention()
            out_phase(ALPHA)
            norm_phase("ln", vecs=(t["ln_g_2"][layer, 0], t["ln_b_2"][layer, 0]))
            ffn_phase()
            norm_phase("ln", vecs=(t["ln_g_2"][layer, 1], t["ln_b_2"][layer, 1]))
            ple_phase(layer)
        assert pos[0] == NCH, (pos[0], NCH)
        final_store()


def column(v):
    return np.ascontiguousarray(np.asarray(v).reshape(-1, P).T)


def kernel(**inputs):
    import concourse.bacc as bacc
    from concourse.bass_utils import run_bass_kernel_spmd

    i = {k: np.asarray(v) for k, v in inputs.items()}
    onehot_a, onehot_b = bias_constants()
    arrays = {
        "x": i["x"], "weights": pack_weights(i), "onehot_a": onehot_a, "onehot_b": onehot_b,
        "rel_bias": i["rel_bias"], "rel_bias_2": i["rel_bias_2"],
        "attn_pre_norm": column(i["attn_pre_norm"]), "ssm_pre_norm": column(i["ssm_pre_norm"]),
        "da_subln_2": column(i["da_subln_2"]), "hg_gnorm_2": column(i["hg_gnorm_2"]),
        "attn_post_norm": i["attn_post_norm"], "ssm_post_norm": i["ssm_post_norm"],
        "ln_g_2": i["ln_g_2"], "ln_b_2": i["ln_b_2"],
        "head_select": head_select(),
        "p_2": np.ascontiguousarray(i["p_2"][:, 0].transpose(0, 2, 1)),
        "da_lambda_2": i["da_lambda_2"],
        "sw_sinks_2": np.ascontiguousarray(i["sw_sinks_2"][:, SW_ORDER]),
        "hg_lower_bound_2": np.ascontiguousarray(i["hg_lower_bound_2"].reshape(N_LAYERS, 8, P).transpose(2, 0, 1)),
        "hg_masks": hg_masks(),
        "ssm_a_re": np.ascontiguousarray(i["ssm_a_re"][0].reshape(32, 2, 64).transpose(1, 2, 0).reshape(P, 32)),
        "ssm_a_im": np.ascontiguousarray(i["ssm_a_im"][0].reshape(32, 2, 64).transpose(1, 2, 0).reshape(P, 32)),
        "ssm_log_dt": np.ascontiguousarray(np.repeat(i["ssm_log_dt"][0].reshape(32, 2).T, 64, axis=0)),
        "ssm_b_re": np.ascontiguousarray(i["ssm_b_re"][0].reshape(32, 2, 64, 16).transpose(1, 2, 0, 3).reshape(P, 32, 16)),
        "ssm_b_im": np.ascontiguousarray(i["ssm_b_im"][0].reshape(32, 2, 64, 16).transpose(1, 2, 0, 3).reshape(P, 32, 16)),
        "ssm_c_re": np.ascontiguousarray(i["ssm_c_re"][0].reshape(32, 2, 16, 64).transpose(1, 3, 0, 2).reshape(P, 32, 16)),
        "ssm_c_im": np.ascontiguousarray(i["ssm_c_im"][0].reshape(32, 2, 16, 64).transpose(1, 3, 0, 2).reshape(P, 32, 16)),
        "ssm_d_rows": np.ascontiguousarray(i["ssm_d"][0].reshape(64, SSM_C).T), "eye16": np.eye(SSM_C, dtype=np.float32),
        "ssm_b_glu": column(i["ssm_b_glu"]),
    }
    nc = bacc.Bacc("TRN2", target_bir_lowering=False, num_devices=1)
    t = {k: nc.dram_tensor("in_" + k, v.shape, mybir.dt.from_np(v.dtype), kind="ExternalInput").ap() for k, v in arrays.items()}
    out = nc.dram_tensor("out_0", (1, S, D), F32, kind="ExternalOutput").ap()
    build(nc, t, out)
    r = run_bass_kernel_spmd(nc, [{"in_" + k: v for k, v in arrays.items()}], core_ids=[0])
    return r.results[0]["out_0"]
```

```python
import math
from contextlib import ExitStack

import numpy as np
import concourse.bass as bass
from concourse import mybir

F32 = mybir.dt.float32
F32R = mybir.dt.float32r
I32 = mybir.dt.int32
ALU = mybir.AluOpType
ACT = mybir.ActivationFunctionType
AX = mybir.AxisListType

STAGES = ("attn", "ssm", "layer0", "layer1", "layer2", "layer3")

P = 128
S = 512
D = 1024
TT = S // P
KT = D // P
CHUNK = 2048
RAW = 2
SPLIT = 2
CREDIT = 8
NEG = -1e30
N_LAYERS = 4
ALPHA = (2 * N_LAYERS) ** 0.25
HEADS = 16
RMS_EPS = 1e-6
LN_EPS = 1e-5
SSM_T = 8
SSM_N = S // SSM_T
SSM_PAIRS = 32
SSM_C = 16
HG_LEVELS = 7
SW_ORDER = [h for j in range(4) for h in (2 * j, 2 * j + 1, 8 + 2 * j, 9 + 2 * j)]


def f_chunks(w):
    n = w.shape[1] // 256
    return w.reshape(KT, P, n, 256).transpose(2, 1, 0, 3).reshape(n, P, CHUNK)


def t_chunks(w):
    k, n = w.shape
    return w.reshape(k // 512, 4, P, n // 512, 512).transpose(3, 0, 2, 1, 4).reshape(-1, P, CHUNK)


def attn_chunks(w):
    qkv = w[:, :9216].reshape(D, 3, 3, 8, P)
    z = w[:, 9216:].reshape(D, 8, P)
    out = []
    for i in range(4):
        cols = []
        for p in (2 * i, 2 * i + 1):
            qk = [[qkv[:, 0, g, p], qkv[:, 1, g, p]] for g in range(3)]
            cols += [qkv[:, 2, 0, p], qkv[:, 2, 1, p]] + qk[0]
            cols += [z[:, p], z[:, p + 1]] if p == 2 * i else []
            cols += qk[1]
            cols += [qkv[:, 2, 2, p], qkv[:, 2, 2, p + 1]] if p == 2 * i else []
            cols += qk[2]
        out.append(f_chunks(np.concatenate(cols, axis=1)))
    return np.concatenate(out)


def da_chunks(w):
    q, k, v = (w[:, 1024 * j:1024 * (j + 1)].reshape(D, 8, P) for j in range(3))
    out = []
    for i in range(4):
        a, b = 2 * i, 2 * i + 1
        out.append(f_chunks(np.concatenate([q[:, a], k[:, a], q[:, b], k[:, b], v[:, a], v[:, b]], axis=1)))
    return np.concatenate(out)


def sw_chunks(w):
    q, k, v = w[:, :1024].reshape(D, 16, 64), w[:, 1024:1152], w[:, 1152:]
    cols = [k[:, :64], k[:, :64], k[:, 64:], k[:, 64:], v, v, q[:, SW_ORDER].reshape(D, 1024)]
    return f_chunks(np.concatenate(cols, axis=1))


def layer_rest_chunks(wo, up, down, gate, ple):
    parts = [t_chunks(wo)]
    for q in range(4):
        parts += [f_chunks(up[:, 1024 * q:1024 * (q + 1)]), t_chunks(down[1024 * q:1024 * (q + 1)])]
    parts += [t_chunks(gate), ple.reshape(2, P, D).transpose(1, 0, 2).reshape(1, P, CHUNK)]
    return np.concatenate(parts)


def pack_weights(i):
    g = lambda n: np.asarray(i[n])
    parts = []
    if "attn" in STAGES:
        parts += [attn_chunks(g("attn_w_in")[0]), t_chunks(g("attn_w_out")[0])]
    if "ssm" in STAGES:
        parts += [f_chunks(g("ssm_w_in")[0]), f_chunks(g("ssm_w_glu")[0]), t_chunks(g("ssm_w_out")[0])]
    for layer in range(N_LAYERS):
        if f"layer{layer}" not in STAGES:
            continue
        kind, j = layer % 3, layer // 3
        if kind == 0:
            parts.append(da_chunks(g("da_w_in_2")[j]))
            wo = g("da_w_out_2")[j]
        elif kind == 1:
            w = g("hg_w_in_2")[j]
            parts += [f_chunks(w[:, :2048]), t_chunks(w[:, 2048:])]
            wo = g("hg_w_out_2")[j]
        else:
            parts.append(sw_chunks(g("sw_w_in_2")[j]))
            wo = g("sw_w_out_2")[j].reshape(16, 64, D)[SW_ORDER].reshape(D, D)
        parts.append(layer_rest_chunks(wo, g("w_up_2")[layer], g("w_down_2")[layer], g("w_ple_gate_2")[layer], g("w_ple_2")[layer]))
    return np.ascontiguousarray(np.concatenate(parts))


def bucket(dist, max_dist):
    n = max(dist, 1)
    if dist < 16:
        return dist
    return min(16 + int(math.log(n / 16) / math.log(max_dist / 16) * 16), 31)


def one_hot(width, back_of, valid, max_dist):
    m = np.zeros((33, width), np.float32)
    for y in range(width):
        back = back_of(y)
        if valid(back):
            m[bucket(back, max_dist), y] = 1.0
        else:
            m[32, y] = NEG
    return m


W1, W2 = 256, 128
L1, L2 = W1 + P - 1, W2 + P - 1
LA = L1 + 2 * L2
WD, WS = 512, 256
LD_, LS = WD + P - 1, WS + P - 1
LB = LD_ + LS


def bias_constants():
    a = [one_hot(L1, lambda y: P + P - 1 - y, lambda b: 0 <= b <= P, 2048),
         one_hot(L2, lambda y: 4 * (P - 1 - y), lambda b: b >= 0, 2048),
         one_hot(L2, lambda y: 4 * (P - 1 - y), lambda b: b >= 0 and b % 16 == 0, 2048)]
    b = [one_hot(LD_, lambda y: 3 * P + P - 1 - y, lambda b: b >= 0, 128),
         one_hot(LS, lambda y: P + P - 1 - y, lambda b: 0 <= b < P, 128)]
    return np.concatenate(a, axis=1), np.concatenate(b, axis=1)


def hg_masks():
    m = np.zeros((P, HG_LEVELS + 1, P), np.int32)
    for lev in range(HG_LEVELS):
        c = P >> (lev + 1)
        for s in range(P):
            if (s // c) % 2 == 0:
                t0 = (s // c + 1) * c
                m[s, lev, t0:t0 + c] = 1
    m[np.arange(P), HG_LEVELS, np.arange(P)] = 1
    return m


def head_select():
    m = np.zeros((HEADS, 8, P), np.float32)
    for h in range(HEADS):
        m[h, h // 2, 64 * (h % 2):64 * (h % 2) + 64] = 1.0
    return m


class Signal:

    def __init__(self, handle, base=0):
        self.h, self.base = handle, base


class InOrder:

    def __init__(self, eng, sig):
        self.eng, self.sig, self.start, self.k, self.per = eng, sig, 0, 0, None

    def __call__(self, ins):
        self.k += 1
        ins.then_inc(self.sig.h, 1)
        self.eng.wait_ge(self.sig.h, self.sig.base + self.start + self.k)

    def enter(self, i, per):
        self.before, self.per, self.k0 = self.start + self.k, per, self.k
        self.start, self.k = self.before + i * per, 0

    def leave(self, n):
        assert self.k == self.per, f"links per pass: {self.k}, not {self.per}"
        self.start, self.k = self.before + n * self.per, 0

    def done(self):
        self.sig.base += self.start + self.k


def build(nc, t, out):
    ctx = ExitStack()
    with ctx:
        taken = {}

        def sb(name, shape, dt=F32, c=ctx):
            taken[name] = taken.get(name, 0) + 1
            return c.enter_context(nc.sbuf_tensor(name if taken[name] == 1 else f"{name}_{taken[name]}", shape, dt))

        def signal(name, base=0):
            s = Signal(ctx.enter_context(nc.semaphore(name)), base)
            if base:
                credited.append(s)
            return s

        credited = []
        NCH = t["weights"].shape[0]
        X = sb("X", [P, TT, D])
        XTh = sb("XTh", [P, KT, S], F32R)
        XTl = sb("XTl", [P, KT, S], F32R)
        Y = sb("Y", [P, TT, D])
        YF = Y[:, :, :].rearrange("p a b -> p (a b)").rearrange("p (k s) -> p k s", k=KT)
        raw = [sb(f"raw{i}", [P, CHUNK]) for i in range(RAW)]
        wh = [sb(f"wh{i}", [P, CHUNK], F32R) for i in range(SPLIT)]
        wl = [sb(f"wl{i}", [P, CHUNK], F32R) for i in range(SPLIT)]
        ident = sb("ident", [P, P])
        zero = sb("zero", [P, 1])
        mhalf = sb("mhalf", [P, 1])
        col = sb("col", [P, 64])
        st = sb("st", [P, 96])
        PS = [ctx.enter_context(nc.psum_tensor(f"bank{i}", [P, 512], F32)) for i in range(8)]

        raw_in = [signal(f"raw_in{i}") for i in range(RAW)]
        w_split = signal("w_split")
        w_high = signal("w_high")
        w_used = signal("w_used", CREDIT)
        tile_done = signal("tile_done")
        tile_free = signal("tile_free", CREDIT)
        tile2_done = signal("tile2_done")
        tile2_free = signal("tile2_free", CREDIT)
        a_b = signal("act_to_dve")
        b_a = signal("dve_to_act")
        b_p = signal("dve_to_pe")
        b_g = signal("dve_to_pool")
        g_b = signal("pool_to_dve")
        a_p = signal("act_to_pe")
        p_a = signal("pe_to_act")
        p_b = signal("pe_to_dve")
        loaded = signal("loaded")
        stored = signal("stored")
        dve_order, act_order, pool_order = signal("dve_order"), signal("act_order"), signal("pool_order")
        split_free = signal("split_free", CREDIT)
        sigs = dict(sc_done=signal("scores_done"), sc_free=signal("scores_free", CREDIT), sbias=signal("biased"),
                    pexp=signal("exp_done"), pnorm=signal("probs_done"), tr=signal("probs_transposed", CREDIT),
                    pt=signal("probsT_copied", CREDIT), pv=signal("pv_done", CREDIT), oev=signal("pv_free", CREDIT),
                    bias_in=signal("bias_in"), bias_used=signal("bias_used", CREDIT), proj=signal("proj_done"),
                    pev=signal("proj_free", CREDIT))

        bias_a = nc.dram_tensor("bias_a", (HEADS, P, 512), F32, kind="Internal").ap()
        bias_d = nc.dram_tensor("bias_d", (HEADS, P, WD), F32, kind="Internal").ap()
        bias_s = nc.dram_tensor("bias_s", (HEADS, P, WS), F32, kind="Internal").ap()

        pos = [0]

        def load_chunk(sp, c, slot):
            sp.wait_ge(w_split.h, c - RAW + 1)
            sp.dma_start(raw[slot][:, :], t["weights"][bass.ds(c, 1)].rearrange("a p n -> p (a n)")).then_inc(raw_in[slot].h, 16)

        def split_chunk(pool, c, r, s):
            pool.wait_ge(w_used.h, CREDIT + c - SPLIT + 1)
            pool.wait_ge(raw_in[r].h, 16 * ((c - r) // RAW + 1) if isinstance(c, int) else (c - r) * (16 // RAW) + 16)
            pool.tensor_tensor(wh[s][:, :], raw[r][:, :], zero[:, :].to_broadcast([P, CHUNK]), ALU.add).then_inc(w_high.h, 1)
            pool.wait_ge(w_high.h, c + 1)
            pool.tensor_tensor(wl[s][:, :], raw[r][:, :], wh[s][:, :].bitcast(F32), ALU.subtract).then_inc(w_split.h, 1)

        def stream(eng, first, last, unit, one):
            last = min(last, NCH)
            n = (last - first) // unit
            if n >= 2:
                with eng.Fori(0, n) as i:
                    for j in range(unit):
                        one(i * unit + (first + j), first + j)
                first += n * unit
            for c in range(first, last):
                one(c, c)

        def sp_stream(sp, n):
            a = pos[0] + SPLIT + RAW
            stream(sp, a, a + n, RAW, lambda c, k: load_chunk(sp, c, k % RAW))

        def pool_stream(pool, n):
            a = pos[0] + SPLIT
            stream(pool, a, a + n, 2, lambda c, k: split_chunk(pool, c, k % RAW, k % SPLIT))

        def arrived(pe, c):
            pe.wait_ge(w_split.h, c + 1)

        def three(psum, hi_pairs, first, last):
            (sh, sl), (mh, ml) = hi_pairs
            nc.tensor.matmul(psum, sh, mh, start=first, stop=False)
            nc.tensor.matmul(psum, sl, mh, start=False, stop=False)
            return nc.tensor.matmul(psum, sh, ml, start=False, stop=last)

        def f_tile(psum, slot, m, xh=XTh, xl=XTl):
            for k in range(KT):
                c = slice(256 * k + P * m, 256 * k + P * m + P)
                last = three(psum, ((wh[slot][:, c], wl[slot][:, c]), (xh[:, k, :], xl[:, k, :])), k == 0, k == KT - 1)
            return last

        def v_tile(psum, slot, c0, n, tok):
            for k in range(KT):
                c = slice(256 * k + c0, 256 * k + c0 + n)
                last = three(psum, ((tok(XTh, k), tok(XTl, k)), (wh[slot][:, c], wl[slot][:, c])), k == 0, k == KT - 1)
            return last

        def t_tile(psum, slot, kks, xs, tok, first, last, width=512, c0=0, step=512):
            xh, xl = xs
            for n, (kk, k) in enumerate(kks):
                c = slice(step * kk + c0, step * kk + c0 + width)
                r = three(psum, ((tok(xh, k), tok(xl, k)), (wh[slot][:, c], wl[slot][:, c])),
                          first and n == 0, last and n == len(kks) - 1)
            return r

        def natural(tt):
            return lambda x, k: x[:, k, P * tt:P * tt + P]

        bias_a_stored = signal("bias_a_stored")
        bias_ds_stored = signal("bias_ds_stored")

        def wait_bias_stored(eng):
            wait_bias_a_stored(eng)
            eng.wait_ge(bias_ds_stored.h, 16 * 2)

        def wait_bias_a_stored(eng):
            eng.wait_ge(bias_a_stored.h, 16 * 3)

        def setup(a_scope, b_scope):
            with ExitStack() as c:
                tb = sb("tb", [HEADS, LB], F32, b_scope)
                ta = sb("ta", [HEADS, LA], F32, a_scope)
                oh_a = sb("oh_a", [33, LA], F32, c)
                oh_b = sb("oh_b", [33, LB], F32, c)
                rb = sb("rb", [33, 2 * HEADS], F32, c)
                made = signal("made")
                tables = signal("tables")
                with nc.Block() as block:
                    @block.sync
                    def _(sp):
                        for k in range(min(RAW, NCH)):
                            sp.dma_start(raw[k][:, :], t["weights"][k]).then_inc(raw_in[k].h, 16)
                        for k in range(RAW, min(RAW + SPLIT, NCH)):
                            load_chunk(sp, k, k % RAW)

                    @block.gpsimd
                    def _(pool):
                        link = InOrder(pool, pool_order)
                        link(pool.memset(zero[:, :], 0.0))
                        link(pool.memset(mhalf[:, :], -0.5))
                        link(pool.memset(ident[:, :], 0.0))
                        pool.memset(rb[32:33, :], 1.0).then_inc(made.h, 1)
                        pool.wait_ge(made.h, 1)
                        pool.affine_select(out=ident[:, :], in_=ident[:, :], compare_op=ALU.not_equal, fill=1.0,
                                           base=0, pattern=[[-1, P]], channel_multiplier=1).then_inc(made.h, 1)
                        pool.wait_ge(made.h, 2)
                        link.done()
                        for s in credited:
                            pool.sem_inc(s.h, CREDIT)
                        for k in range(min(SPLIT, NCH)):
                            pool.wait_ge(raw_in[k % RAW].h, 16 * (k // RAW + 1))
                            pool.tensor_tensor(wh[k][:, :], raw[k % RAW][:, :], zero[:, :].to_broadcast([P, CHUNK]), ALU.add).then_inc(w_high.h, 1)
                            pool.wait_ge(w_high.h, k + 1)
                            pool.tensor_tensor(wl[k][:, :], raw[k % RAW][:, :], wh[k][:, :].bitcast(F32), ALU.subtract).then_inc(w_split.h, 1)

                    @block.scalar
                    def _(act):
                        for d, s in ((oh_a[:, :], t["onehot_a"]), (oh_b[:, :], t["onehot_b"]),
                                     (rb[0:32, 0:HEADS], t["rel_bias"]), (rb[0:32, HEADS:], t["rel_bias_2"]),
                                     (X[:, :, :], t["x"].rearrange("b (t p) d -> p (b t) d", p=P)),
                                     (col[:, 0:KT], t["attn_pre_norm"]), (col[:, KT:2 * KT], t["ssm_pre_norm"]),
                                     (col[:, 16:18], t["da_subln_2"]), (col[:, 18:19], t["hg_gnorm_2"])):
                            act.dma_start(d, s).then_inc(loaded.h, 16)
                        act.wait_ge(tables.h, 4)

                        def toeplitz(dst, table, off, w, sig=bias_a_stored):
                            x = table[:, off:off + w]
                            src = bass.AP(x.tensor, x.offset + P - 1, [list(x.ap[0]), [-1, P], [1, w]])
                            act.dma_start(dst, src).then_inc(sig.h, 16)
                        toeplitz(bias_a[:, :, 0:W1], ta, 0, W1)
                        toeplitz(bias_a[:, :, W1:384], ta, L1, W2)
                        toeplitz(bias_a[:, :, 384:512], ta, L1 + L2, W2)
                        toeplitz(bias_d, tb, 0, WD, bias_ds_stored)
                        toeplitz(bias_s, tb, LD_, WS, bias_ds_stored)
                        act.wait_ge(loaded.h, 16 * 9)

                    @block.tensor
                    def _(pe):
                        pe.wait_ge(loaded.h, 16 * 9)
                        pe.wait_ge(made.h, 2)
                        for n, (o, lo, hi, r) in enumerate(((oh_a, 0, 512, 0), (oh_a, 512, LA, 0), (oh_b, 0, 512, 1), (oh_b, 512, LB, 1))):
                            nc.tensor.matmul(PS[n][0:HEADS, 0:hi - lo], rb[:, HEADS * r:HEADS * r + HEADS], o[:, lo:hi],
                                             start=True, stop=True).then_inc(p_b.h, 1)

                    @block.vector
                    def _(dve):
                        for n, (o, lo, hi) in enumerate(((ta, 0, 512), (ta, 512, LA), (tb, 0, 512), (tb, 512, LB))):
                            dve.wait_ge(p_b.h, n + 1)
                            nc.vector.tensor_copy(o[:, lo:hi], PS[n][0:HEADS, 0:hi - lo]).then_inc(tables.h, 1)
                loaded.base += 16 * 9
                p_b.base += 4

        BN = [st[:, 16 + 12 * tt:28 + 12 * tt] for tt in range(TT)]
        MEANVAR = [st[:, 64 + 2 * tt:66 + 2 * tt] for tt in range(TT)]
        VAR = st[:, 64:72].rearrange("p (t a) -> p t a", a=2)[:, :, 1]
        SQ = st[:, 72:80].rearrange("p (h t) -> p h t", h=2)

        def load_vectors(eng, bc, vecs):
            for n, v in enumerate(vecs):
                eng.dma_start(bc[n][:, :], v.partition_broadcast(P)).then_inc(loaded.h, 16)

        def norm_phase(kind, gain=None, bc=(), extra=None, transposed=True, before_end=None):
            with ExitStack() as c:
                N = sb("N", [P, TT, D], F32, c) if kind in ("pre", "heads", "rms_add") else None
                tmp = [sb(f"tmp{i}", [P, 512], F32, c) for i in range(2)]
                src = {"pre": N, "plain": X, "ln": X, "rms_add": X, "heads": N}[kind]
                ready, sums = b_p, a_b
                with nc.Block() as block:
                    if before_end is not None:
                        @block.sync
                        def _(sp):
                            before_end(sp)

                    @block.gpsimd
                    def _(pool):
                        p = nc.gpsimd
                        link = InOrder(pool, pool_order)

                        def rsqrt(x, scale, eps):
                            link(p.tensor_scalar(x, x, scale, eps, ALU.mult, ALU.add))
                            return p.tensor_tensor(x, x, mhalf[:, :].to_broadcast([P, x.shape[1]]), ALU.pow)
                        if kind == "ln":
                            rsqrt(VAR, 1.0, LN_EPS).then_inc(g_b.h, 1)
                        elif kind == "rms_add":
                            link(p.tensor_tensor(st[:, 0:TT], SQ[:, 0, :], SQ[:, 1, :], ALU.add))
                            rsqrt(st[:, 0:TT], 1.0, RMS_EPS).then_inc(g_b.h, 1)
                        for tt in range(TT if kind in ("pre", "heads") else 0):
                            if kind == "pre":
                                pool.wait_ge(sums.h, sums.base + tt + 1)
                                rsqrt(st[:, tt:tt + 1], 1.0, RMS_EPS).then_inc(g_b.h, 1)
                            else:
                                pool.wait_ge(b_g.h, b_g.base + tt + 1)
                                link(rsqrt(st[:, 40:48], 1.0 / P, RMS_EPS))
                                p.tensor_scalar(st[:, 40:48], st[:, 40:48], extra["post"], None, ALU.mult).then_inc(g_b.h, 1)
                        link.done()

                    @block.scalar
                    def _(act):
                        if kind == "pre":
                            for tt in range(TT):
                                nc.scalar.activation(N[:, tt, :], X[:, tt, :], ACT.Square, scale=D ** -0.5,
                                                     accum_out=st[:, tt:tt + 1]).then_inc(sums.h, 1)
                        elif kind == "heads":
                            for tt in range(TT):
                                nc.scalar.activation(N[:, tt, :], Y[:, tt, :], ACT.Square).then_inc(sums.h, 1)
                        if transposed:
                            for n in range(2 * TT):
                                tt, half = n // 2, n % 2
                                if gain is None:
                                    act.wait_ge(p_a.h, p_a.base + n + 1)
                                    s = PS[n % 4][:, :]
                                else:
                                    act.wait_ge(b_a.h, b_a.base + n + 1)
                                    s = tmp[n % 2][:, :]
                                nc.scalar.activation(XTh[:, 4 * half:4 * half + 4, P * tt:P * tt + P],
                                                     s.rearrange("p (k c) -> p k c", k=4), ACT.Copy).then_inc(a_p.h, 1)

                    @block.vector
                    def _(dve):
                        link = InOrder(dve, dve_order)
                        v = nc.vector

                        def low(n):
                            tt, half = n // 2, n % 2
                            if gain is None:
                                s = PS[n % 4][:, :]
                            else:
                                dve.wait_ge(p_a.h, p_a.base + n + 1)
                                s = tmp[n % 2][:, :]
                                g = gain[:, 4 * half:4 * half + 4] if gain.shape[1] > 1 else gain
                                g = g.unsqueeze(2).to_broadcast([P, 4, P])
                                v.tensor_tensor(s.rearrange("p (k c) -> p k c", k=4),
                                                PS[n % 4][:, :].rearrange("p (k c) -> p k c", k=4), g, ALU.mult).then_inc(b_a.h, 1)
                            dve.wait_ge(a_p.h, a_p.base + n + 1)
                            v.tensor_tensor(XTl[:, 4 * half:4 * half + 4, P * tt:P * tt + P],
                                            s.rearrange("p (k c) -> p k c", k=4),
                                            XTh[:, 4 * half:4 * half + 4, P * tt:P * tt + P].bitcast(F32),
                                            ALU.subtract).then_inc(tile2_free.h, 1)

                        if bc:
                            dve.wait_ge(loaded.h, loaded.base)
                        for tt in range(TT):
                            if kind == "pre":
                                dve.wait_ge(g_b.h, g_b.base + tt + 1)
                                r = st[:, tt:tt + 1]
                                v.tensor_scalar(N[:, tt, :], X[:, tt, :], r, None, ALU.mult).then_inc(ready.h, 1)
                            elif kind == "plain":
                                dve.sem_inc(ready.h, 1)
                            elif kind == "rms_add":
                                dve.wait_ge(g_b.h, g_b.base + 1)
                                r = st[:, tt:tt + 1]
                                link(v.scalar_tensor_tensor(N[:, tt, :], Y[:, tt, :], r, bc[0][:, :], ALU.mult, ALU.mult))
                                v.tensor_tensor(X[:, tt, :], X[:, tt, :], N[:, tt, :], ALU.add).then_inc(ready.h, 1)
                            elif kind == "ln":
                                m, r = MEANVAR[tt][:, 0:1], MEANVAR[tt][:, 1:2]
                                link(v.scalar_tensor_tensor(Y[:, tt, :], Y[:, tt, :], m, bc[0][:, :], ALU.subtract, ALU.mult))
                                dve.wait_ge(g_b.h, g_b.base + 1)
                                v.scalar_tensor_tensor(X[:, tt, :], Y[:, tt, :], r, bc[1][:, :], ALU.mult, ALU.add).then_inc(ready.h, 1)
                            else:
                                dve.wait_ge(sums.h, sums.base + tt + 1)
                                sq = N[:, tt, :].rearrange("p (h e) -> p h e", h=8)
                                v.tensor_reduce(st[:, 40:48], sq, AX.X, ALU.add).then_inc(b_g.h, 1)
                                dve.wait_ge(g_b.h, g_b.base + tt + 1)
                                link(v.tensor_tensor(sq, Y[:, tt, :].rearrange("p (h e) -> p h e", h=8),
                                                     st[:, 40:48].unsqueeze(2).to_broadcast([P, 8, P]), ALU.mult))
                                if "gate" in extra:
                                    link(v.tensor_tensor(N[:, tt, :], N[:, tt, :], extra["gate"][:, tt, :], ALU.mult))
                                dve.sem_inc(ready.h, 1)
                            if transposed and tt >= 1:
                                low(2 * tt - 2)
                                low(2 * tt - 1)
                        if transposed:
                            low(2 * TT - 2)
                            low(2 * TT - 1)
                        link.done()

                    if transposed:
                        @block.tensor
                        def _(pe):
                            for n in range(2 * TT):
                                tt, half = n // 2, n % 2
                                pe.wait_ge(ready.h, ready.base + tt + 1)
                                if n >= 4:
                                    pe.wait_ge(tile2_free.h, tile2_free.base + n - 3)
                                for k in range(4):
                                    r = nc.tensor.transpose(PS[n % 4][:, P * k:P * k + P],
                                                            src[:, tt, 512 * half + P * k:512 * half + P * k + P], ident[:, :])
                                r.then_inc(p_a.h, 1)
                ready.base += TT
                if kind != "plain":
                    g_b.base += TT if kind in ("pre", "heads") else 1
                if kind == "heads":
                    b_g.base += TT
                if kind in ("pre", "heads"):
                    sums.base += TT
                if transposed:
                    p_a.base += 2 * TT
                    a_p.base += 2 * TT
                    tile2_free.base += 2 * TT
                    if gain is not None:
                        b_a.base += 2 * TT

        def t_linear(pe, c0, xs, tok):
            for j in range(4):
                half, kh = j // 2, j % 2
                arrived(pe, c0 + j)
                for tt in range(TT):
                    r = t_tile(PS[4 * half + tt][:, :], (c0 + j) % SPLIT, [(kk, 4 * kh + kk) for kk in range(4)],
                               xs, tok(tt), kh == 0, kh == 1)
                    if tt == TT - 1:
                        r.then_inc(w_used.h, 1)
                    elif kh == 1:
                        r.then_inc(tile_done.h, 1)

        def wait_t(eng, c0, half, tt):
            if tt == TT - 1:
                eng.wait_ge(w_used.h, CREDIT + c0 + 2 * half + 2)
            else:
                eng.wait_ge(tile_done.h, tile_done.base + 3 * half + tt + 1)

        def out_phase(alpha, vecs, transposed=True):
            with ExitStack() as c:
                bc = [sb(f"bc{i}", [P, D], F32, c) for i in range(len(vecs))]
                squares = sb("squares", [P, 512], F32, c)
                out_product(alpha, bc, vecs, squares)
                norm_phase("rms_add" if alpha is None else "ln", bc=bc, transposed=transposed)

        def out_product(alpha, bc, vecs, squares):
            c0 = pos[0]
            with nc.Block() as block:
                @block.sync
                def _(sp):
                    sp_stream(sp, 4)

                @block.gpsimd
                def _(pool):
                    pool_stream(pool, 4)

                @block.tensor
                def _(pe):
                    t_linear(pe, c0, (XTh, XTl), natural)

                @block.scalar
                def _(act):
                    load_vectors(act, bc, vecs)
                    if alpha is None:
                        link = InOrder(act, act_order)
                        for half in range(2):
                            for tt in range(TT):
                                act.wait_ge(b_a.h, b_a.base + 4 * half + tt + 1)
                                link(nc.scalar.activation(squares[:, :], Y[:, tt, 512 * half:512 * half + 512], ACT.Square,
                                                          scale=D ** -0.5, accum_out=SQ[:, half, tt:tt + 1]))
                        link.done()

                @block.vector
                def _(dve):
                    v = nc.vector
                    link = InOrder(dve, dve_order)
                    for half in range(2):
                        for tt in range(TT):
                            wait_t(dve, c0, half, tt)
                            y, x = (z[:, tt, 512 * half:512 * half + 512] for z in (Y, X))
                            if alpha is None:
                                v.tensor_copy(y, PS[4 * half + tt][:, :]).then_inc(b_a.h, 1)
                            else:
                                link(v.scalar_tensor_tensor(y, x, alpha, PS[4 * half + tt][:, :], ALU.mult, ALU.add))
                                link(v.bn_stats(BN[tt][:, 6 * half:6 * half + 6], y))
                                if half:
                                    v.bn_aggr(MEANVAR[tt], BN[tt])
                    link.done()
            if alpha is None:
                b_a.base += 8
            loaded.base += 16 * len(vecs)
            tile_done.base += 6
            pos[0] += 4

        def ffn_phase(vecs):
            with ExitStack() as c:
                bc = [sb(f"bc{i}", [P, D], F32, c) for i in range(2)]
                ffn_products(bc, vecs)
                norm_phase("ln", bc=bc)

        def ffn_products(bc, vecs):
            c0 = pos[0]
            with ExitStack() as c:
                HTh = sb("HTh", [P, KT, S], F32R, c)
                HTl = sb("HTl", [P, KT, S], F32R, c)
                R = [sb(f"R{i}", [P, S], F32, c) for i in range(2)]
                Q = [sb(f"Q{i}", [P, S], F32, c) for i in range(2)]
                up_free, down_free = tile_free, tile2_free
                relu_done, sq_done, high_done, low_done = up_free, b_a, a_b, b_p
                with nc.Block() as block:
                    @block.sync
                    def _(sp):
                        sp_stream(sp, 32)

                    @block.gpsimd
                    def _(pool):
                        pool_stream(pool, 32)

                    @block.tensor
                    def _(pe):
                        with pe.Fori(0, 4) as q:
                            for j in range(4):
                                arrived(pe, q * 8 + (c0 + j))
                                for m in range(2):
                                    u = 2 * j + m
                                    pe.wait_ge(up_free.h, q * 8 + (up_free.base + u - 3))
                                    r = f_tile(PS[u % 4][:, :], (c0 + j) % SPLIT, m)
                                    r.then_inc((tile_done if m == 0 else w_used).h, 1)
                            for j in range(4):
                                half, kh = j // 2, j % 2
                                arrived(pe, q * 8 + (c0 + 4 + j))
                                pe.wait_ge(low_done.h, q * 8 + (low_done.base + 4 * kh + 4))
                                for tt in range(TT):
                                    if kh == 0:
                                        pe.wait_ge(down_free.h, q * 8 + (down_free.base + 4 * half + tt - 3))
                                    r = t_tile(PS[4 + tt][:, :], (c0 + j) % SPLIT, [(kk, 4 * kh + kk) for kk in range(4)],
                                               (HTh, HTl), natural(tt), kh == 0, kh == 1)
                                    if tt == TT - 1:
                                        r.then_inc(w_used.h, 1)
                                    elif kh == 1:
                                        r.then_inc(tile2_done.h, 1)

                    @block.scalar
                    def _(act):
                        load_vectors(act, bc, vecs)
                        with act.Fori(0, 4) as q:
                            for u in range(8):
                                if u % 2 == 0:
                                    act.wait_ge(tile_done.h, q * 4 + (tile_done.base + u // 2 + 1))
                                else:
                                    act.wait_ge(w_used.h, q * 8 + (CREDIT + c0 + u // 2 + 1))
                                nc.scalar.activation(R[u % 2][:, :], PS[u % 4][:, :], ACT.Relu).then_inc(relu_done.h, 1)
                                act.wait_ge(sq_done.h, q * 8 + (sq_done.base + u + 1))
                                nc.scalar.activation(HTh[:, u, :], Q[u % 2][:, :], ACT.Copy).then_inc(high_done.h, 1)

                    @block.vector
                    def _(dve):
                        v = nc.vector
                        link = InOrder(dve, dve_order)
                        for tt in range(TT):
                            link(v.tensor_scalar(Y[:, tt, :], X[:, tt, :], ALPHA, None, ALU.mult))
                        with dve.Fori(0, 4) as q:
                            link.enter(q, 2 * TT)
                            for u in range(8):
                                dve.wait_ge(relu_done.h, q * 8 + (relu_done.base + u + 1))
                                v.tensor_tensor(Q[u % 2][:, :], R[u % 2][:, :], R[u % 2][:, :], ALU.mult).then_inc(sq_done.h, 1)
                                dve.wait_ge(high_done.h, q * 8 + (high_done.base + u + 1))
                                v.tensor_tensor(HTl[:, u, :], Q[u % 2][:, :], HTh[:, u, :].bitcast(F32), ALU.subtract).then_inc(low_done.h, 1)
                            for half in range(2):
                                for tt in range(TT):
                                    if tt == TT - 1:
                                        dve.wait_ge(w_used.h, q * 8 + (CREDIT + c0 + 4 + 2 * half + 2))
                                    else:
                                        dve.wait_ge(tile2_done.h, q * 6 + (tile2_done.base + 3 * half + tt + 1))
                                    y = Y[:, tt, 512 * half:512 * half + 512]
                                    v.tensor_tensor(y, y, PS[4 + tt][:, :], ALU.add).then_inc(down_free.h, 1)
                                    dve.wait_ge(down_free.h, q * 8 + (down_free.base + 4 * half + tt + 1))
                                    link(v.bn_stats(BN[tt][:, 6 * half:6 * half + 6], y))
                            link.leave(4)
                        for tt in range(TT):
                            v.bn_aggr(MEANVAR[tt], BN[tt])
                        link.done()
                loaded.base += 16 * len(vecs)
                up_free.base += 32
                down_free.base += 32
                tile_done.base += 16
                tile2_done.base += 24
                sq_done.base += 32
                high_done.base += 32
                low_done.base += 32
                pos[0] += 32

        def ple_phase(layer):
            c0 = pos[0]
            with ExitStack() as c:
                pT = sb("pT", [P, 2, S], F32, c)
                pTh = sb("pTh", [P, 2, S], F32R, c)
                pTl = sb("pTl", [P, 2, S], F32R, c)
                with nc.Block() as block:
                    @block.sync
                    def _(sp):
                        sp.dma_start(pT[:, :, :], t["p_2"][layer].rearrange("(k p) s -> p k s", p=P)).then_inc(loaded.h, 16)
                        sp_stream(sp, 5)

                    @block.gpsimd
                    def _(pool):
                        pool_stream(pool, 5)

                    @block.tensor
                    def _(pe):
                        t_linear(pe, c0, (XTh, XTl), natural)
                        arrived(pe, c0 + 4)
                        pe.wait_ge(b_p.h, b_p.base + 1)
                        for half in range(2):
                            for tt in range(TT):
                                n = 4 * half + tt
                                pe.wait_ge(tile2_free.h, tile2_free.base + n + 1)
                                r = t_tile(PS[n][:, :], (c0 + 4) % SPLIT, [(0, 0), (1, 1)], (pTh, pTl), natural(tt), True, True,
                                           c0=512 * half, step=1024)
                                r.then_inc((w_used if n == 7 else tile2_done).h, 1)

                    @block.scalar
                    def _(act):
                        act.wait_ge(loaded.h, loaded.base + 16)
                        nc.scalar.activation(pTh[:, :, :], pT[:, :, :], ACT.Copy).then_inc(a_b.h, 1)
                        for half in range(2):
                            for tt in range(TT):
                                wait_t(act, c0, half, tt)
                                nc.scalar.activation(Y[:, tt, 512 * half:512 * half + 512], PS[4 * half + tt][:, :],
                                                     ACT.Sigmoid).then_inc(tile2_free.h, 1)

                    @block.vector
                    def _(dve):
                        v = nc.vector
                        link = InOrder(dve, dve_order)
                        dve.wait_ge(loaded.h, loaded.base + 16)
                        dve.wait_ge(a_b.h, a_b.base + 1)
                        v.tensor_tensor(pTl[:, :, :], pT[:, :, :], pTh[:, :, :].bitcast(F32), ALU.subtract).then_inc(b_p.h, 1)
                        for half in range(2):
                            for tt in range(TT):
                                n = 4 * half + tt
                                dve.wait_ge(tile2_free.h, tile2_free.base + n + 1)
                                if n == 7:
                                    dve.wait_ge(w_used.h, CREDIT + c0 + 5)
                                else:
                                    dve.wait_ge(tile2_done.h, tile2_done.base + n + 1)
                                y, x = (z[:, tt, 512 * half:512 * half + 512] for z in (Y, X))
                                link(v.tensor_tensor(y, y, PS[n][:, :], ALU.mult))
                                v.tensor_tensor(x, x, y, ALU.add)
                        link.done()
            tile_done.base += 6
            tile2_done.base += 7
            tile2_free.base += 8
            loaded.base += 16
            a_b.base += 1
            b_p.base += 1
            pos[0] += 5

        def pe_jobs(n, depth, scores, transposes, values, fill):
            for j in range(depth):
                scores(j)
            fill(-1)
            for j in range(n):
                transposes(j)
                if j + depth < n:
                    scores(j + depth)
                fill(j)
                values(j)

        def dve_jobs(n, depth, biased, normalise):
            for j in range(n + depth - 1):
                if j >= depth - 1:
                    normalise(j - depth + 1)
                if j < n:
                    biased(j)

        def act_jobs(n, depth, exps, copy_probs, copy_out, drain):
            for j in range(n + depth):
                if depth == 2 and j < n:
                    exps(j)
                if j >= depth:
                    copy_out(j - depth)
                if depth - 1 <= j < n + depth - 1:
                    copy_probs(j - depth + 1)
                if depth > 2 and j < n:
                    exps(j)
                if j >= depth - 2:
                    drain(j - depth + 1)

        SC_DONE, SC_FREE, BIASED, EXPED, PNORM, TR, PTC, PV, OEV = (
            sigs[k] for k in ("sc_done", "sc_free", "sbias", "pexp", "pnorm", "tr", "pt", "pv", "oev"))
        BIAS_IN, BIAS_USED, PROJ, PEV = (sigs[k] for k in ("bias_in", "bias_used", "proj", "pev"))


        def diff_attention(layer, j):
            c0 = pos[0]
            lam_init = 0.8 - 0.6 * math.exp(-0.3 * layer)
            with ExitStack() as c:
                RUNS, RUN = 4, 8
                QT = sb("QT", [P, 2, 2, S], F32, c)
                KTT = sb("KTT", [P, 2, 2, S], F32, c)
                V = sb("V", [P, 2, TT, 256], F32, c)
                B = sb("B", [P, 4, WD], F32, c)
                SC = sb("SC", [P, 2, 2, 512], F32, c)
                PT = sb("PT", [P, 2, 512], F32, c)
                sa = sb("sa", [P, 2, 8], F32, c)
                lam = sb("lam", [P, 4 * 64 + 8], F32, c)
                TBANK, OBANK = 6, 7
                CH = (0, 0, 1, 1, 2, 2, 2, 2)
                STEP = (-1, 0, 1, 2, 3, 4, 5, 6)
                CHUNK_END = (1, 3, 7)
                OTHERS = tuple(n for n in range(8) if n not in CHUNK_END)
                with nc.Block() as block:
                    @block.sync
                    def _(sp):
                        sp_stream(sp, 12)

                    @block.gpsimd
                    def _(pool):
                        pool_stream(pool, 12)

                    @block.tensor
                    def _(pe):
                        def project(r, n):
                            ch = c0 + 3 * r + CH[n]
                            if n in (0, 2, 4):
                                arrived(pe, ch)
                            pe.wait_ge(PEV.h, PEV.base + RUN * r + n - 1)
                            if n < 4:
                                x = f_tile(PS[n % 2][:, :], ch % SPLIT, n % 2)
                            else:
                                x = v_tile(PS[n % 2][:, 0:256], ch % SPLIT, 0, 256, natural(n - 4))
                            x.then_inc((w_used if n in CHUNK_END else PROJ).h, 1)

                        def run(r):
                            def wait(s, k):
                                pe.wait_ge(s.h, s.base + RUN * r + k)

                            def scores(n):
                                hh, b = n // 4, n % 4
                                wait(SC_FREE, n - 1)
                                for m in range(2):
                                    x = nc.tensor.matmul(PS[2 + 2 * (n % 2) + m][:, 0:P * (b + 1)],
                                                         QT[64 * m:64 * m + 64, r % 2, hh, P * b:P * b + P],
                                                         KTT[64 * m:64 * m + 64, r % 2, hh, 0:P * (b + 1)], start=True, stop=True)
                                x.then_inc(SC_DONE.h, 1)

                            def transposes(n):
                                wait(PNORM, n + 1)
                                wait(PTC, n)
                                for k in range(n % 4 + 1):
                                    x = nc.tensor.transpose(PS[TBANK][:, P * k:P * k + P], SC[:, n % 2, 0, P * k:P * k + P], ident[:, :])
                                x.then_inc(TR.h, 1)

                            def fill(j):
                                for n in range(RUN):
                                    if STEP[n] == j and r + 1 < RUNS:
                                        project(r + 1, n)

                            def values(n):
                                wait(PTC, n + 1)
                                wait(OEV, n)
                                hh, b = n // 4, n % 4
                                for k in range(b + 1):
                                    x = nc.tensor.matmul(PS[OBANK][:, 0:P], PT[:, n % 2, P * k:P * k + P],
                                                         V[:, r % 2, k, P * hh:P * hh + P], start=(k == 0), stop=(k == b))
                                x.then_inc(PV.h, 1)
                            wait(PEV, RUN)
                            pe_jobs(RUN, 2, scores, transposes, values, fill)
                        for n in range(RUN):
                            project(0, n)
                        for r in range(RUNS):
                            run(r)

                    @block.scalar
                    def _(act):
                        a = nc.scalar

                        def load_bias(r):
                            act.dma_start(B[:, :, :], bias_d[4 * r:4 * r + 4].rearrange("h p w -> p h w")).then_inc(BIAS_IN.h, 16)

                        def take(r, n):
                            if n in CHUNK_END:
                                act.wait_ge(w_used.h, CREDIT + c0 + 3 * r + CH[n] + 1)
                            else:
                                act.wait_ge(PROJ.h, PROJ.base + len(OTHERS) * r + OTHERS.index(n) + 1)
                            if n < 4:
                                dst, scale = ((QT, 0.125), (KTT, 1.0))[n % 2]
                                a.activation(dst[:, r % 2, n // 2, :], PS[n % 2][:, :], ACT.Copy, scale=scale).then_inc(PEV.h, 1)
                            else:
                                a.activation(V[:, r % 2, n - 4, :], PS[n % 2][:, 0:256], ACT.Copy).then_inc(PEV.h, 1)

                        def run(r):
                            def wait(s, k):
                                act.wait_ge(s.h, s.base + RUN * r + k)

                            def exps(n):
                                wait(BIASED, n + 1)
                                w = P * (n % 4 + 1)
                                for m in range(2):
                                    x = a.activation(SC[:, n % 2, m, 0:w], SC[:, n % 2, m, 0:w], ACT.Exp,
                                                     bias=sa[:, n % 2, 2 + m:3 + m], accum_out=sa[:, n % 2, 4 + m:5 + m])
                                x.then_inc(EXPED.h, 1)

                            def copy_probs(n):
                                wait(TR, n + 1)
                                wait(PV, n - 1)
                                w = P * (n % 4 + 1)
                                a.activation(PT[:, n % 2, 0:w], PS[TBANK][:, 0:w], ACT.Copy).then_inc(PTC.h, 1)

                            def copy_out(n):
                                wait(PV, n + 1)
                                h = 2 * r + n // 4
                                a.activation(Y[:, n % 4, P * h:P * h + P], PS[OBANK][:, 0:P], ACT.Copy).then_inc(OEV.h, 1)

                            def drain(j):
                                if r + 1 < RUNS:
                                    if j == RUN - 2:
                                        act.wait_ge(BIAS_USED.h, BIAS_USED.base + r + 1)
                                        load_bias(r + 1)
                                    for n in range(RUN):
                                        if STEP[n] == j:
                                            take(r + 1, n)
                            act_jobs(RUN, 2, exps, copy_probs, copy_out, drain)
                        load_bias(0)
                        act.dma_start(lam[:, 0:256], t["da_lambda_2"][j].rearrange("a e -> (a e)").partition_broadcast(P)).then_inc(loaded.h, 16)
                        act.wait_ge(b_a.h, b_a.base + 1)
                        a.activation(lam[:, 258:260], lam[:, 256:258], ACT.Exp).then_inc(a_b.h, 1)
                        for n in range(RUN):
                            take(0, n)
                        for r in range(RUNS):
                            run(r)

                    @block.vector
                    def _(dve):
                        v = nc.vector
                        link = InOrder(dve, dve_order)
                        dve.wait_ge(loaded.h, loaded.base + 16)
                        l4 = lam[:, 0:256].rearrange("p (a b e) -> p a b e", a=2, b=2)
                        link(v.tensor_tensor(l4[:, :, 0, :], l4[:, :, 0, :], l4[:, :, 1, :], ALU.mult))
                        v.tensor_reduce(lam[:, 256:258], l4[:, :, 0, :], AX.X, ALU.add).then_inc(b_a.h, 1)
                        dve.wait_ge(a_b.h, a_b.base + 1)
                        link(v.tensor_tensor(lam[:, 260:261], lam[:, 259:260], lam[:, 258:259], ALU.subtract))
                        link(v.tensor_scalar(lam[:, 261:262], lam[:, 260:261], -lam_init, None, ALU.add))
                        with dve.Fori(0, 2) as i:
                            link.enter(i, 16 * 5 + 2)
                            for hp in range(2):
                                def wait(s, k, per=16):
                                    dve.wait_ge(s.h, i * per + (s.base + k))

                                def biased(n):
                                    hh, b = n // 4, n % 4
                                    w = P * (b + 1)
                                    wait(SC_DONE, 8 * hp + n + 1)
                                    wait(TR, 8 * hp + n - 1)
                                    if n == 0:
                                        wait(BIAS_IN, 16 * (hp + 1), per=32)
                                    link(v.tensor_tensor(SC[:, n % 2, 0, 0:w], PS[2 + 2 * (n % 2)][:, 0:w], B[:, 2 * hh, WD - w:WD], ALU.add))
                                    v.tensor_tensor(SC[:, n % 2, 1, 0:w], PS[3 + 2 * (n % 2)][:, 0:w], B[:, 2 * hh + 1, WD - w:WD], ALU.add).then_inc(SC_FREE.h, 1)
                                    wait(SC_FREE, 8 * hp + n + 1)
                                    link(v.tensor_reduce(sa[:, n % 2, 0:2], SC[:, n % 2, :, 0:w], AX.X, ALU.max))
                                    if n == 7:
                                        link(v.tensor_scalar(sa[:, n % 2, 2:4], sa[:, n % 2, 0:2], -1.0, None, ALU.mult))
                                        dve.sem_inc(BIAS_USED.h, 1)
                                        dve.sem_inc(BIASED.h, 1)
                                    else:
                                        v.tensor_scalar(sa[:, n % 2, 2:4], sa[:, n % 2, 0:2], -1.0, None, ALU.mult).then_inc(BIASED.h, 1)

                                def normalise(n):
                                    w = P * (n % 4 + 1)
                                    wait(EXPED, 8 * hp + n + 1)
                                    link(v.reciprocal(sa[:, n % 2, 6:8], sa[:, n % 2, 4:6]))
                                    link(v.tensor_tensor(sa[:, n % 2, 7:8], sa[:, n % 2, 7:8], lam[:, 261:262], ALU.mult))
                                    link(v.tensor_scalar(SC[:, n % 2, 1, 0:w], SC[:, n % 2, 1, 0:w], sa[:, n % 2, 7:8], None, ALU.mult))
                                    v.scalar_tensor_tensor(SC[:, n % 2, 0, 0:w], SC[:, n % 2, 0, 0:w], sa[:, n % 2, 6:7],
                                                           SC[:, n % 2, 1, 0:w], ALU.mult, ALU.add).then_inc(PNORM.h, 1)
                                dve_jobs(8, 2, biased, normalise)
                        link.leave(2)
                        link.done()
                for s in (SC_DONE, SC_FREE, BIASED, EXPED, PNORM, TR, PTC, PV, OEV, PEV):
                    s.base += 32
                PROJ.base += 20
                BIAS_IN.base += 64
                BIAS_USED.base += 4
                loaded.base += 16
                a_b.base += 1
                b_a.base += 1
                pos[0] += 12
            norm_phase("heads", gain=col[:, 16 + j:17 + j], extra={"post": 1.0 - lam_init})

        def final_store():
            with nc.Block() as block:
                @block.sync
                def _(sp):
                    sp.dma_start(out.rearrange("b (t p) d -> p (b t) d", p=P), X[:, :, :]).then_inc(stored.h, 16)
                    sp.wait_ge(stored.h, stored.base + 16)
        class Job:

            def __init__(self, e, scores, bias, rows, values, stat, ntiles):
                self.e, self.scores, self.bias, self.rows, self.values = e, scores, bias, rows, values
                self.stat, self.ntiles = stat, ntiles
                self.nstat = sum(r[1] for r in rows)

        def window_jobs(e, q, k, v, bias):
            prev_diag, diag = bias[:, 0:W1], bias[:, P:W1]
            return [Job(e, [(q(0), k(0, 1), 0, P), (q(1), k(0, 2), P, 2 * P)],
                        [(0, 1, P, diag), (P, 1, 2 * P, prev_diag)], [(0, 1, P), (P, 1, 2 * P)],
                        [[(v(0), 0)], [(v(0), 1), (v(1), 2)]], 0, 3),
                    Job(e, [(q(2), k(1, 2), 0, 2 * P), (q(3), k(2, 2), 2 * P, 2 * P)],
                        [(0, 2, 2 * P, prev_diag)], [(0, 2, 2 * P)],
                        [[(v(1), 0), (v(2), 1)], [(v(2), 2), (v(3), 3)]], 2, 4)]

        def residue_job(e, q, k, v, bias, stat):
            return Job(e, [(q(r), k(r), P * r, P) for r in range(4)], [(0, 4, P, bias)], [(0, 4, P)],
                       [[(v(r), r)] for r in range(4)], stat, 4)

        def bands(ap, first, n, w):
            return ap[:, first:first + n * w].rearrange("p (n w) -> p n w", n=n)

        DEPTH, SBANKS = 3, (2, 3, 5)

        class RowAttention:

            def __init__(self, jobs, SC, PT, stats, sink=None):
                self.jobs, self.SC, self.PT, self.stats, self.sink = jobs, SC, PT, stats, sink

            def stat(self, j, kind):
                x = self.jobs[j]
                return self.stats[:, x.e, kind, x.stat:x.stat + x.nstat]

            def pe(self, at, fill=lambda j: None):
                J, SC, PT = self.jobs, self.SC, self.PT

                def scores(n):
                    at(SC_FREE, max(n - DEPTH + 1, 0))
                    for q, k, c, w in J[n].scores:
                        r = nc.tensor.matmul(PS[SBANKS[n % DEPTH]][:, c:c + w], q, k, start=True, stop=True)
                    r.then_inc(SC_DONE.h, 1)

                def transposes(n):
                    at(PNORM, n + 1)
                    at(PTC, n)
                    for k in range(J[n].ntiles):
                        r = nc.tensor.transpose(PS[4][:, P * k:P * k + P], SC[:, n % DEPTH, P * k:P * k + P], ident[:, :])
                    r.then_inc(TR.h, 1)

                def values(n):
                    at(PTC, n + 1)
                    at(OEV, n)
                    lo = 64 * J[n].e
                    for q, terms in enumerate(J[n].values):
                        for m, (v, tile) in enumerate(terms):
                            r = nc.tensor.matmul(PS[6][lo:lo + 64, P * q:P * q + P], v, PT[:, n % 2, P * tile:P * tile + P],
                                                 start=(m == 0), stop=(m == len(terms) - 1))
                    r.then_inc(PV.h, 1)
                pe_jobs(len(J), DEPTH, scores, transposes, values, fill)

            def dve(self, at, link, bias_wait, bias_done, head_done):
                v, J, SC = nc.vector, self.jobs, self.SC

                def biased(n):
                    x = J[n]
                    at(SC_DONE, n + 1)
                    at(TR, max(n - DEPTH + 1, 0))
                    if n == 0:
                        bias_wait()
                    for i, (c, m, w, b) in enumerate(x.bias):
                        o, s = bands(SC[:, n % DEPTH, :], c, m, w), bands(PS[SBANKS[n % DEPTH]][:, :], c, m, w)
                        r = v.tensor_tensor(o, s, b.unsqueeze(1).to_broadcast([P, m, w]), ALU.add)
                        if i < len(x.bias) - 1:
                            link(r)
                    r.then_inc(SC_FREE.h, 1)
                    at(SC_FREE, n + 1)
                    if n == len(J) - 1:
                        bias_done()
                    k = 0
                    for c, m, w in x.rows:
                        link(v.tensor_reduce(self.stat(n, 0)[:, k:k + m], bands(SC[:, n % DEPTH, :], c, m, w), AX.X, ALU.max))
                        k += m
                    if self.sink is not None:
                        link(v.tensor_scalar(self.stat(n, 0), self.stat(n, 0), self.sink(x), None, ALU.max))
                    v.tensor_scalar(self.stat(n, 1), self.stat(n, 0), -1.0, None, ALU.mult).then_inc(BIASED.h, 1)

                def normalise(n):
                    x = J[n]
                    at(EXPED, n + 1)
                    link(v.reciprocal(self.stat(n, 3), self.stat(n, 2)))
                    k = 0
                    for i, (c, m, w) in enumerate(x.rows):
                        s = bands(SC[:, n % DEPTH, :], c, m, w)
                        r = v.tensor_tensor(s, s, self.stat(n, 3)[:, k:k + m].unsqueeze(2).to_broadcast([P, m, w]), ALU.mult)
                        if i < len(x.rows) - 1:
                            link(r)
                        k += m
                    r.then_inc(PNORM.h, 1)
                    head_done(n)
                dve_jobs(len(J), DEPTH, biased, normalise)

            def dve_links(self):
                return sum(len(x.bias) - 1 + len(x.rows) + (self.sink is not None) + 1 + len(x.rows) - 1 for x in self.jobs)

            def act(self, at, copy_to, link=None, drain=lambda j: None):
                a, J, SC, PT = nc.scalar, self.jobs, self.SC, self.PT

                def exps(n):
                    x = J[n]
                    at(BIASED, n + 1)
                    k = 0
                    for c, m, w in x.rows:
                        for i in range(m):
                            s = SC[:, n % DEPTH, c + i * w:c + i * w + w]
                            r = a.activation(s, s, ACT.Exp, bias=self.stat(n, 1)[:, k:k + 1], accum_out=self.stat(n, 2)[:, k:k + 1])
                            k += 1
                    if self.sink is not None:
                        link(r)
                        sk, den = sink_tmp[:, 0:k], sink_tmp[:, 4:4 + k]
                        link(a.activation(sk, self.stat(n, 1), ACT.Exp, bias=self.sink(x)))
                        for i in range(k):
                            r = a.activation(self.stat(n, 2)[:, i:i + 1], self.stat(n, 2)[:, i:i + 1], ACT.Identity, bias=sk[:, i:i + 1])
                    r.then_inc(EXPED.h, 1)

                def copy_probs(n):
                    at(TR, n + 1)
                    at(PV, n - 1)
                    w = P * J[n].ntiles
                    a.activation(PT[:, n % 2, 0:w], PS[4][:, 0:w], ACT.Copy).then_inc(PTC.h, 1)

                def copy_out(n):
                    at(PV, n + 1)
                    lo = 64 * J[n].e
                    copy_to(n, PS[6][lo:lo + 64, 0:P * len(J[n].values)]).then_inc(OEV.h, 1)
                act_jobs(len(J), DEPTH, exps, copy_probs, copy_out, drain)

        sink_tmp = sb("sink_tmp", [P, 8])

        def dilated_attention():
            c0 = pos[0]
            with ExitStack() as c:
                O3 = sb("O3", [P, 3, 8, S], F32, c)
                MX = sb("MX", [P, HEADS, 12], F32, c)
                SM = sb("SM", [P, HEADS, 12], F32, c)
                with ExitStack() as c2:
                    QK = sb("QK", [P, 6, S], F32, c2)
                    V = sb("V", [P, TT, 2, 3, P], F32, c2)
                    V2 = sb("V2", [P, TT, P], F32, c2)
                    B = sb("B", [P, 2, 512], F32, c2)
                    SC = sb("SC", [P, DEPTH, 512], F32, c2)
                    PT = sb("PT", [P, 2, 512], F32, c2)
                    stats = sb("stats", [P, 2, 4, 12], F32, c2)

                    def g0(ap, t0):
                        return ap[:, P * t0:P * t0 + P]

                    def g1(ap, r):
                        return ap[:, r::4]

                    def jobs(half):
                        by_group = [[], [], []]
                        for e in range(2):
                            lo = 64 * e
                            qk = lambda n: QK[lo:lo + 64, n, :]
                            vv = lambda g: (lambda r: V[:, r, half, g, lo:lo + 64])
                            by_group[0] += window_jobs(e, (lambda b, q=qk(0): g0(q, b)),
                                                       (lambda b, n, k=qk(1): k[:, P * b:P * b + n * P]), vv(0), B[:, e, 0:W1])
                            by_group[1].append(residue_job(e, (lambda r, q=qk(2): g1(q, r)), (lambda r, k=qk(3): g1(k, r)), vv(1), B[:, e, W1:384], 4))
                            by_group[2].append(residue_job(e, (lambda r, q=qk(4): g1(q, r)), (lambda r, k=qk(5): g1(k, r)), vv(2), B[:, e, 384:512], 8))
                        for g in range(3):
                            for n, x in enumerate(by_group[g]):
                                x.group, x.part = g, n % 2
                        return by_group[0] + by_group[1] + by_group[2]

                    att = [RowAttention(jobs(h), SC, PT, stats) for h in range(2)]
                    def qk_pair(g, ch, steps):
                        return [("qk", 2 * g, ch, 0, steps[0]), ("qk", 2 * g + 1, ch, 1, steps[1])]

                    def v_tiles(kind, ch, steps):
                        return [(kind, tt, ch, 0, steps[tt]) for tt in range(TT)]
                    first = (v_tiles("v01", 0, (-1, -1, 0, 0)) + qk_pair(0, 1, (1, 1)) + [("z", 0, 2, 0, 2), ("z", 1, 2, 1, 3)]
                             + qk_pair(1, 3, (3, 4)) + v_tiles("v2", 4, (4, 5, 5, 6)) + qk_pair(2, 5, (6, 7)))
                    second = (v_tiles("v01", 6, (-1, -1, -1, 0)) + qk_pair(0, 7, (1, 2)) + qk_pair(1, 8, (3, 4)) + qk_pair(2, 9, (5, 6)))
                    tiles = [first, second]
                    PASSES, RUN = 4, 8
                    n_tiles = len(first) + len(second)

                    def ends(half, n):
                        return n == len(tiles[half]) - 1 or tiles[half][n + 1][2] != tiles[half][n][2]
                    n_proj = sum(not ends(h, n) for h in range(2) for n in range(len(tiles[h])))

                    def proj_before(half, n):
                        return sum(not ends(h, m) for h in range(half + 1) for m in range(len(tiles[h])) if h < half or m <= n)

                    def project(pe, i, di, half, n):
                        kind, x, ch, m, _ = tiles[half][n]
                        k = n + len(first) * half
                        if n == 0 or tiles[half][n - 1][2] != ch:
                            pe.wait_ge(w_split.h, i * 10 + (10 * di + c0 + ch + 1))
                        pe.wait_ge(PEV.h, i * n_tiles + (n_tiles * di + PEV.base + k - 1))
                        bank, slot = PS[k % 2], (c0 + ch) % SPLIT
                        if kind in ("qk", "z"):
                            r = f_tile(bank[:, :], slot, m)
                        elif kind == "v01":
                            v_tile(bank[:, 0:P], slot, 0, P, lambda X_, kk: g0(X_[:, kk, :], x))
                            r = v_tile(bank[:, P:2 * P], slot, P, P, lambda X_, kk: g1(X_[:, kk, :], x))
                        else:
                            r = v_tile(bank[:, 0:256], slot, 0, 256, lambda X_, kk: g1(X_[:, kk, :], x))
                        r.then_inc((w_used if ends(half, n) else PROJ).h, 1)

                    def take(act, i, di, half, n, at=None):
                        a = nc.scalar
                        kind, x, ch, _, _ = tiles[half][n]
                        if ends(half, n):
                            act.wait_ge(w_used.h, i * 10 + (10 * di + CREDIT + c0 + ch + 1))
                        else:
                            act.wait_ge(PROJ.h, i * n_proj + (n_proj * di + PROJ.base + proj_before(half, n)))
                        bank = PS[(n + len(first) * half) % 2]
                        if kind == "qk":
                            if at is not None:
                                at(SC_DONE, 4 + 2 * (x // 2))
                            a.activation(QK[:, x, :], bank[:, :], ACT.Copy, scale=(0.125, 1.0)[x % 2]).then_inc(PEV.h, 1)
                        elif kind == "z":
                            a.activation(YF[:, bass.ds(i * 2 + (2 * di + x), 1), :].rearrange("p a s -> p (a s)"), bank[:, :], ACT.Copy).then_inc(PEV.h, 1)
                        elif kind == "v01":
                            a.activation(V[:, x, half, 0:2, :], bank[:, 0:256].rearrange("p (g e) -> p g e", g=2), ACT.Copy).then_inc(PEV.h, 1)
                        else:
                            a.activation(V[:, x, 0, 2, :], bank[:, 0:P], ACT.Copy)
                            a.activation(V2[:, x, :], bank[:, P:2 * P], ACT.Copy).then_inc(PEV.h, 1)

                    def next_half(half, last):
                        return None if last and half == 1 else (half, 1 - half)

                    def at_step(half, j):
                        return [n for n, x in enumerate(tiles[half]) if x[4] == j]
                    with nc.Block() as block:
                        @block.sync
                        def _(sp):
                            sp_stream(sp, 40)
                            wait_bias_stored(sp)

                        @block.gpsimd
                        def _(pool):
                            pool_stream(pool, 40)

                        @block.tensor
                        def _(pe):
                            def one_pass(i, last):
                                for half in range(2):
                                    def at(s, k):
                                        pe.wait_ge(s.h, i * (2 * RUN) + (s.base + RUN * half + k))

                                    def fill(j):
                                        to = next_half(half, last)
                                        for n in (at_step(to[1], j) if to else ()):
                                            project(pe, i, to[0], to[1], n)
                                    pe.wait_ge(PEV.h, i * n_tiles + (PEV.base + len(first) + len(second) * half))
                                    att[half].pe(at, fill)
                            for n in range(len(first)):
                                project(pe, 0, 0, 0, n)
                            with pe.Fori(0, PASSES - 1) as i:
                                one_pass(i, False)
                            one_pass(PASSES - 1, True)

                        @block.scalar
                        def _(act):
                            a = nc.scalar

                            def load_bias(i, di, half):
                                act.dma_start(B[:, :, :], bias_a[bass.ds(i * 4 + (4 * di + 2 * half), 2)].rearrange("h p w -> p h w")).then_inc(BIAS_IN.h, 16)

                            def one_pass(i, last):
                                for half in range(2):
                                    def at(s, k):
                                        act.wait_ge(s.h, i * (2 * RUN) + (s.base + RUN * half + k))

                                    def copy_to(n, psum):
                                        j = att[half].jobs[n]
                                        lo = 64 * j.e
                                        o = O3[lo:lo + 64, j.group, bass.ds(i * 2 + half, 1), :].rearrange("p a s -> p (a s)")
                                        if j.group == 0:
                                            return a.activation(o[:, 256 * j.part:256 * j.part + 256], psum, ACT.Copy)
                                        return a.activation(o.rearrange("p (l r) -> p r l", r=4), psum.rearrange("p (r l) -> p r l", r=4), ACT.Copy)

                                    def drain(j):
                                        to = next_half(half, last)
                                        if to and j == RUN - 2:
                                            act.wait_ge(BIAS_USED.h, i * 2 + (BIAS_USED.base + half + 1))
                                            load_bias(i, to[0], to[1])
                                        for n in (at_step(to[1], j) if to else ()):
                                            take(act, i, to[0], to[1], n, at)
                                    if half == 1:
                                        act.wait_ge(PEV.h, i * n_tiles + (PEV.base + len(first)))
                                        a.activation(V[:, :, 1, 2, :], V2[:, :, :], ACT.Copy)
                                    att[half].act(at, copy_to, drain=drain)
                            load_bias(0, 0, 0)
                            for n in range(len(first)):
                                take(act, 0, 0, 0, n)
                            with act.Fori(0, PASSES - 1) as i:
                                one_pass(i, False)
                            one_pass(PASSES - 1, True)

                        @block.vector
                        def _(dve):
                            link = InOrder(dve, dve_order)
                            with dve.Fori(0, PASSES) as i:
                                link.enter(i, sum(x.dve_links() for x in att))
                                for half in range(2):
                                    def at(s, k):
                                        dve.wait_ge(s.h, i * (2 * RUN) + (s.base + RUN * half + k))

                                    def head_done(n):
                                        if n >= RUN - 2:
                                            e = n - (RUN - 2)
                                            for dst, kind in ((MX, 0), (SM, 2)):
                                                nc.vector.tensor_copy(dst[:, bass.ds(i * 4 + (2 * half + e), 1), :].rearrange("p a s -> p (a s)"),
                                                                      stats[:, e, kind, :])
                                    att[half].dve(at, link, lambda: dve.wait_ge(BIAS_IN.h, i * 32 + (BIAS_IN.base + 16 * (half + 1))),
                                                  lambda: dve.sem_inc(BIAS_USED.h, 1), head_done)
                                link.leave(PASSES)
                            link.done()
                    for s in (SC_DONE, SC_FREE, BIASED, EXPED, PNORM, TR, PTC, PV, OEV):
                        s.base += 64
                    PEV.base += 4 * n_tiles
                    PROJ.base += 4 * n_proj
                    BIAS_IN.base += 128
                    BIAS_USED.base += 8
                    pos[0] += 40
                combine_groups(O3, MX, SM)

        def combine_groups(O3, MX, SM):
            with ExitStack() as c:
                LR = sb("LR", [HEADS, 3, S], F32, c)
                M = sb("M", [HEADS, S], F32, c)
                sel = sb("sel", [HEADS, 8, P], F32, c)
                acc = sb("acc", [P, 2, S], F32, c)
                sg = sb("sg", [P, 2, S], F32, c)
                with nc.Block() as block:
                    @block.sync
                    def _(sp):
                        sp.dma_start(sel[:, :, :], t["head_select"]).then_inc(loaded.h, 16)

                    @block.scalar
                    def _(act):
                        a = nc.scalar
                        a.activation(SM[:, :, :], SM[:, :, :], ACT.Ln).then_inc(a_b.h, 1)
                        act.wait_ge(b_a.h, b_a.base + 1)
                        a.activation(LR[:, :, :], LR[:, :, :], ACT.Exp).then_inc(a_b.h, 1)
                        for p in range(8):
                            if p >= 2:
                                act.wait_ge(tile2_free.h, tile2_free.base + p - 1)
                            a.activation(sg[:, p % 2, :], YF[:, p, :], ACT.Sigmoid).then_inc(a_b.h, 1)
                            act.wait_ge(b_a.h, b_a.base + 2 + p)
                            a.activation(XTh[:, p, :], acc[:, 0, :], ACT.Copy).then_inc(a_p.h, 1)

                    @block.tensor
                    def _(pe):
                        pe.wait_ge(b_p.h, b_p.base + 1)
                        for s in range(12):
                            r = nc.tensor.transpose(PS[s // 4][0:HEADS, P * (s % 4):P * (s % 4) + P], SM[:, :, s], ident[:, :])
                        r.then_inc(p_b.h, 1)
                        pe.wait_ge(b_p.h, b_p.base + 2)
                        pe.wait_ge(loaded.h, loaded.base + 16)
                        for p in range(8):
                            if p >= 2:
                                pe.wait_ge(tile2_free.h, tile2_free.base + p - 1)
                            for g in range(3):
                                r = nc.tensor.matmul(PS[4 * (p % 2) + g][:, :], sel[:, p, :], LR[:, g, :], start=True, stop=True)
                            r.then_inc(p_b.h, 1)

                    @block.vector
                    def _(dve):
                        v = nc.vector
                        link = InOrder(dve, dve_order)
                        dve.wait_ge(a_b.h, a_b.base + 1)
                        v.tensor_tensor(SM[:, :, :], SM[:, :, :], MX[:, :, :], ALU.add).then_inc(b_p.h, 1)
                        dve.wait_ge(p_b.h, p_b.base + 1)
                        link(v.tensor_copy(LR[:, 0, :], PS[0][0:HEADS, :]))
                        for g, r in ((1, 4), (2, 4)):
                            link(v.tensor_copy(LR[:, g, :].rearrange("p (l r) -> p r l", r=r),
                                               PS[g][0:HEADS, :].rearrange("p (r l) -> p r l", r=r)))
                        link(v.tensor_tensor(M[:, :], LR[:, 0, :], LR[:, 1, :], ALU.max))
                        link(v.tensor_tensor(M[:, :], M[:, :], LR[:, 2, :], ALU.max))
                        v.tensor_tensor(LR[:, :, :], LR[:, :, :], M[:, :].unsqueeze(1).to_broadcast([HEADS, 3, S]), ALU.subtract).then_inc(b_a.h, 1)
                        dve.wait_ge(a_b.h, a_b.base + 2)
                        link(v.tensor_tensor(M[:, :], LR[:, 0, :], LR[:, 1, :], ALU.add))
                        link(v.tensor_tensor(M[:, :], M[:, :], LR[:, 2, :], ALU.add))
                        link(v.reciprocal(M[:, :], M[:, :]))
                        v.tensor_tensor(LR[:, :, :], LR[:, :, :], M[:, :].unsqueeze(1).to_broadcast([HEADS, 3, S]), ALU.mult).then_inc(b_p.h, 1)
                        for p in range(8):
                            dve.wait_ge(p_b.h, p_b.base + 2 + p)
                            if p >= 1:
                                dve.wait_ge(a_p.h, a_p.base + p)
                            link(v.tensor_tensor(acc[:, 0, :], O3[:, 0, p, :], PS[4 * (p % 2)][:, :], ALU.mult))
                            for g in (1, 2):
                                link(v.tensor_tensor(acc[:, 1, :], O3[:, g, p, :], PS[4 * (p % 2) + g][:, :], ALU.mult))
                                link(v.tensor_tensor(acc[:, 0, :], acc[:, 0, :], acc[:, 1, :], ALU.add))
                            link(v.tensor_tensor(acc[:, 0, :], acc[:, 0, :], YF[:, p, :], ALU.mult))
                            dve.wait_ge(a_b.h, a_b.base + 3 + p)
                            v.tensor_tensor(acc[:, 0, :], acc[:, 0, :], sg[:, p % 2, :], ALU.mult).then_inc(b_a.h, 1)
                            dve.wait_ge(a_p.h, a_p.base + p + 1)
                            v.tensor_tensor(XTl[:, p, :], acc[:, 0, :], XTh[:, p, :].bitcast(F32), ALU.subtract).then_inc(tile2_free.h, 1)
                            dve.wait_ge(tile2_free.h, tile2_free.base + p + 1)
                        link.done()
                loaded.base += 16
                a_b.base += 10
                b_a.base += 9
                p_b.base += 9
                b_p.base += 2
                a_p.base += 8
                tile2_free.base += 8

        def sliding_attention():
            c0 = pos[0]
            with ExitStack() as c:
                Q = sb("Q", [P, 2, S], F32, c)
                KK = sb("KK", [P, 2, S], F32, c)
                V = sb("V", [P, TT, P], F32, c)
                B = sb("B", [P, 4, WS], F32, c)
                SC = sb("SC", [P, DEPTH, 512], F32, c)
                PT = sb("PT", [P, 2, 512], F32, c)
                stats = sb("stats", [P, 2, 4, 12], F32, c)
                sinks = sb("sinks", [P, HEADS], F32, c)
                sk = sb("sk", [P, 4], F32, c)

                js = []
                for kv in range(2):
                    for e in range(2):
                        lo = 64 * e
                        w = window_jobs(e, (lambda b, q=Q[lo:lo + 64, kv, :]: q[:, P * b:P * b + P]),
                                        (lambda b, n, k=KK[lo:lo + 64, kv, :]: k[:, P * b:P * b + n * P]),
                                        (lambda r, kv=kv: V[:, r, 64 * kv:64 * kv + 64]), B[:, 2 * kv + e, :])
                        for x in w:
                            x.head = 2 * kv + e
                        js += w
                att = RowAttention(js, SC, PT, stats, sink=lambda x: sk[:, x.head:x.head + 1])
                RUNS, RUN = 4, 8
                STEP = (1, 5)
                with nc.Block() as block:
                    @block.sync
                    def _(sp):
                        sp_stream(sp, 6)

                    @block.gpsimd
                    def _(pool):
                        pool_stream(pool, 6)

                    @block.tensor
                    def _(pe):
                        for n in range(6):
                            if n in (0, 2):
                                arrived(pe, c0 + n // 2)
                            pe.wait_ge(PEV.h, PEV.base + n - 1)
                            if n < 2:
                                r = f_tile(PS[n % 2][:, :], c0 % SPLIT, n)
                            else:
                                r = v_tile(PS[n % 2][:, 0:P], (c0 + 1) % SPLIT, 0, P, natural(n - 2))
                            r.then_inc((w_used if n in (1, 5) else PROJ).h, 1)

                        def project(r, m):
                            if m == 0:
                                arrived(pe, c0 + 2 + r)
                            pe.wait_ge(PEV.h, PEV.base + 6 + 2 * r + m - 1)
                            x = f_tile(PS[m][:, :], (c0 + r) % SPLIT, m)
                            x.then_inc((w_used if m else PROJ).h, 1)
                        project(0, 0)
                        project(0, 1)
                        for r in range(RUNS):
                            def at(s, k):
                                pe.wait_ge(s.h, s.base + RUN * r + k)

                            def fill(j):
                                if j in STEP and r + 1 < RUNS:
                                    project(r + 1, STEP.index(j))
                            pe.wait_ge(PEV.h, PEV.base + 6 + 2 * r + 2)
                            att.pe(at, fill)

                    @block.scalar
                    def _(act):
                        a = nc.scalar
                        link = InOrder(act, act_order)

                        def load_bias(r):
                            for kv in range(2):
                                h = 2 * r + 8 * kv
                                act.dma_start(B[:, 2 * kv:2 * kv + 2, :], bias_s[h:h + 2].rearrange("h p w -> p h w")).then_inc(BIAS_IN.h, 16)

                        def take(r, m):
                            if m:
                                act.wait_ge(w_used.h, CREDIT + c0 + 2 + r + 1)
                            else:
                                act.wait_ge(PROJ.h, PROJ.base + 4 + r + 1)
                            if r:
                                act.wait_ge(SC_DONE.h, SC_DONE.base + RUN * (r - 1) + 4 + 4 * m)
                            a.activation(Q[:, m, :], PS[m][:, :], ACT.Copy, scale=0.125).then_inc(PEV.h, 1)
                        act.dma_start(sinks[:, :], t["sw_sinks_2"][0].partition_broadcast(P)).then_inc(loaded.h, 16)
                        load_bias(0)
                        for n in range(6):
                            if n in (1, 5):
                                act.wait_ge(w_used.h, CREDIT + c0 + (1 if n == 1 else 2))
                            else:
                                act.wait_ge(PROJ.h, PROJ.base + {0: 1, 2: 2, 3: 3, 4: 4}[n])
                            if n < 2:
                                a.activation(KK[:, n, :], PS[n % 2][:, :], ACT.Copy).then_inc(PEV.h, 1)
                            else:
                                a.activation(V[:, n - 2, :], PS[n % 2][:, 0:P], ACT.Copy).then_inc(PEV.h, 1)
                        take(0, 0)
                        take(0, 1)
                        for r in range(RUNS):
                            def at(s, k):
                                act.wait_ge(s.h, s.base + RUN * r + k)

                            def copy_to(n, psum):
                                x = att.jobs[n]
                                lo = 64 * x.e
                                return a.activation(YF[lo:lo + 64, 2 * r + x.head // 2, 256 * (n % 2):256 * (n % 2) + 256], psum, ACT.Copy)

                            def drain(j):
                                if r + 1 < RUNS:
                                    if j == RUN - 2:
                                        act.wait_ge(BIAS_USED.h, BIAS_USED.base + r + 1)
                                        load_bias(r + 1)
                                    if j in STEP:
                                        take(r + 1, STEP.index(j))
                            att.act(at, copy_to, link, drain)
                        link.done()

                    @block.vector
                    def _(dve):
                        link = InOrder(dve, dve_order)
                        dve.wait_ge(loaded.h, loaded.base + 16)
                        with dve.Fori(0, RUNS) as i:
                            link.enter(i, att.dve_links() + 1)

                            def at(s, k):
                                dve.wait_ge(s.h, i * RUN + (s.base + k))

                            def bias_wait():
                                dve.wait_ge(BIAS_IN.h, i * 32 + (BIAS_IN.base + 32))
                            at(SC_DONE, 1)
                            link(nc.vector.tensor_copy(sk[:, :], sinks[:, bass.ds(i * 4, 4)]))
                            att.dve(at, link, bias_wait, lambda: dve.sem_inc(BIAS_USED.h, 1), lambda n: None)
                            link.leave(RUNS)
                        link.done()
                for s in (SC_DONE, SC_FREE, BIASED, EXPED, PNORM, TR, PTC, PV, OEV):
                    s.base += 32
                PEV.base += 14
                PROJ.base += 8
                BIAS_IN.base += 128
                BIAS_USED.base += 4
                loaded.base += 16
                pos[0] += 6
            split_features(lambda k: YF[:, k, :])

        def split_features(src, gate=None):
            with nc.Block() as block:
                @block.scalar
                def _(act):
                    for k in range(KT):
                        nc.scalar.activation(XTh[:, k, :], src(k), ACT.Copy).then_inc(a_b.h, 1)

                @block.vector
                def _(dve):
                    for k in range(KT):
                        dve.wait_ge(a_b.h, a_b.base + k + 1)
                        nc.vector.tensor_tensor(XTl[:, k, :], src(k), XTh[:, k, :].bitcast(F32), ALU.subtract)
            a_b.base += KT
        U8 = mybir.dt.uint8
        hg_lv = dict(pd=signal("hg_diff"), ae=signal("hg_exp"), dw=signal("hg_weighted"), wf=signal("hg_slot_free", CREDIT),
                     lf=signal("hg_level_free", CREDIT), kht=signal("hg_khat_copied", CREDIT), tk=signal("hg_khat_transposed"),
                     ud=signal("hg_update_done"), sr=signal("hg_states_ready", CREDIT), oe=signal("hg_out_free", CREDIT), dt=signal("dve_tick"), pt=signal("pool_tick"))

        def hgrn(layer, j):
            c0 = pos[0]
            with ExitStack() as c:
                G = sb("G", [P, TT, D], F32, c)
                with ExitStack() as c2:
                    QF = sb("QF", [P, KT, S], F32, c2)
                    KIN = sb("KIN", [P, KT, S], F32, c2)
                    LF = sb("LF", [P, KT, S], F32, c2)
                    IV = sb("IV", [P, TT, D], F32, c2)
                    masks = sb("masks", [P, HG_LEVELS + 1, P], U8, c2)
                    with ExitStack() as c3:
                        masks32 = sb("masks32", [P, HG_LEVELS + 1, P], I32, c3)
                        lbt = sb("lbt", [P, 4, 8], F32, c3)
                        lb = sb("lb", [P, 3, 8], F32, c3)
                        ones = sb("ones", [P, S], F32, c3)
                        SG = sb("SG", [P, 2, S], F32, c3)
                        with nc.Block() as block:
                            @block.sync
                            def _(sp):
                                sp.dma_start(lbt[:, :, :], t["hg_lower_bound_2"]).then_inc(loaded.h, 16)
                                sp.dma_start(masks32[:, :, :], t["hg_masks"]).then_inc(loaded.h, 16)
                                sp_stream(sp, 16)

                            @block.gpsimd
                            def _(pool):
                                pool_stream(pool, 16)

                            @block.tensor
                            def _(pe):
                                with pe.Fori(0, 4) as i:
                                    for n in range(4):
                                        if n % 2 == 0:
                                            pe.wait_ge(w_split.h, i * 2 + (c0 + n // 2 + 1))
                                        pe.wait_ge(tile_free.h, i * 4 + (tile_free.base + n - 3))
                                        r = f_tile(PS[n][:, :], (c0 + n // 2) % SPLIT, n % 2)
                                        r.then_inc((w_used if n % 2 else tile_done).h, 1)
                                with pe.Fori(0, 4) as i:
                                    for kh in range(2):
                                        pe.wait_ge(w_split.h, i * 2 + (c0 + 8 + kh + 1))
                                        for tt in range(TT):
                                            if kh == 0:
                                                pe.wait_ge(tile2_free.h, i * 4 + (tile2_free.base + tt - 3))
                                            r = t_tile(PS[4 + tt][:, :], (c0 + kh) % SPLIT, [(kk, 4 * kh + kk) for kk in range(4)],
                                                       (XTh, XTl), natural(tt), kh == 0, kh == 1)
                                            if tt == TT - 1:
                                                r.then_inc(w_used.h, 1)
                                            elif kh == 1:
                                                r.then_inc(tile2_done.h, 1)

                            def wait_f(eng, n):
                                if n % 2:
                                    eng.wait_ge(w_used.h, CREDIT + c0 + n // 2 + 1)
                                else:
                                    eng.wait_ge(tile_done.h, tile_done.base + n // 2 + 1)

                            def wait_g(eng, n):
                                if n % 4 == 3:
                                    eng.wait_ge(w_used.h, CREDIT + c0 + 8 + 2 * (n // 4) + 2)
                                else:
                                    eng.wait_ge(tile2_done.h, tile2_done.base + 3 * (n // 4) + n % 4 + 1)

                            @block.scalar
                            def _(act):
                                a = nc.scalar
                                act.wait_ge(b_a.h, b_a.base + 1)
                                a.activation(lbt[:, :, :], lbt[:, :, :], ACT.Exp).then_inc(a_b.h, 1)
                                for n in range(16):
                                    wait_f(act, n)
                                    if n >= 2:
                                        act.wait_ge(tile_free.h, tile_free.base + n - 1)
                                    a.activation(SG[:, n % 2, :], PS[n % 4][:, :], ACT.Sigmoid).then_inc(a_b.h, 1)
                                for n in range(8, 16):
                                    wait_g(act, n)
                                    a.activation(G[:, n % 4, 512 * (n // 4 - 2):512 * (n // 4 - 1)], PS[4 + n % 4][:, :], ACT.Sigmoid).then_inc(a_b.h, 1)
                                act.wait_ge(tile2_free.h, tile2_free.base + 16)
                                for h in range(8):
                                    a.activation(LF[:, h, :], LF[:, h, :], ACT.Ln).then_inc(a_b.h, 1)

                            @block.vector
                            def _(dve):
                                v = nc.vector
                                link = InOrder(dve, dve_order)
                                link(v.memset(ones[:, :], 1.0))
                                link(v.memset(ones[:, 0:S:P], 0.0))
                                dve.wait_ge(loaded.h, loaded.base + 32)
                                link(v.tensor_copy(masks[:, :, :], masks32[:, :, :]))
                                m, s, one_less = (lb[:, k, :] for k in range(3))
                                link(v.tensor_tensor(m, lbt[:, 0, :], lbt[:, 1, :], ALU.max))
                                link(v.tensor_tensor(m, m, lbt[:, 2, :], ALU.max))
                                link(v.tensor_tensor(m, m, lbt[:, 3, :], ALU.max))
                                v.tensor_tensor(lbt[:, :, :], lbt[:, :, :], m.unsqueeze(1).to_broadcast([P, 4, 8]), ALU.subtract).then_inc(b_a.h, 1)
                                dve.wait_ge(a_b.h, a_b.base + 1)
                                link(v.tensor_tensor(s, lbt[:, 0, :], lbt[:, 1, :], ALU.add))
                                link(v.tensor_tensor(s, s, lbt[:, 2, :], ALU.add))
                                link(v.tensor_tensor(s, s, lbt[:, 3, :], ALU.add))
                                link(v.reciprocal(s, s))
                                link(v.tensor_tensor(lbt[:, :, :], lbt[:, :, :], s.unsqueeze(1).to_broadcast([P, 4, 8]), ALU.mult))
                                link(v.tensor_copy(m, lbt[:, 0, :]))
                                for k in range(1, layer + 1):
                                    link(v.tensor_tensor(m, m, lbt[:, k, :], ALU.add))
                                link(v.tensor_tensor(m, m, lbt[:, 0, :], ALU.subtract))
                                link(v.tensor_scalar(one_less, m, -1.0, 1.0, ALU.mult, ALU.add))
                                for n in range(16):
                                    wait_f(dve, n)
                                    dve.wait_ge(a_b.h, a_b.base + 2 + n)
                                    if n < 8:
                                        v.tensor_tensor(QF[:, n, :], PS[n % 4][:, :], SG[:, n % 2, :], ALU.mult).then_inc(tile_free.h, 1)
                                    else:
                                        h = n - 8
                                        link(v.tensor_scalar(LF[:, h, :], SG[:, n % 2, :], one_less[:, h:h + 1], m[:, h:h + 1], ALU.mult, ALU.add))
                                        v.tensor_scalar(KIN[:, h, :], LF[:, h, :], -1.0, 1.0, ALU.mult, ALU.add).then_inc(tile_free.h, 1)
                                for n in range(16):
                                    wait_g(dve, n)
                                    tt, half = n % 4, n // 4
                                    if n < 8:
                                        v.tensor_copy(IV[:, tt, 512 * half:512 * half + 512], PS[4 + tt][:, :]).then_inc(tile2_free.h, 1)
                                    else:
                                        dve.wait_ge(a_b.h, a_b.base + 10 + n)
                                        g = G[:, tt, 512 * (half - 2):512 * (half - 1)]
                                        v.tensor_tensor(g, g, PS[4 + tt][:, :], ALU.mult).then_inc(tile2_free.h, 1)
                                for h in range(8):
                                    dve.wait_ge(a_b.h, a_b.base + 26 + h)
                                    v.tensor_tensor_scan(LF[:, h, :], ones[:, :], LF[:, h, :], 0.0, ALU.mult, ALU.add)
                                link.done()
                        loaded.base += 32
                        b_a.base += 1
                        a_b.base += 33
                        tile_free.base += 16
                        tile2_free.base += 16
                        tile_done.base += 8
                        tile2_done.base += 12
                        pos[0] += 16
                    hgrn_heads(QF, KIN, LF, IV, masks)
                norm_phase("heads", gain=col[:, 18:19], extra={"post": 1.0, "gate": G})

        def hgrn_heads(QF, KIN, LF, IV, masks):
            PD, AE, DW, WF, LVF, KHC, TK, UD, SR, OE, DVE_TICK, POOL_TICK = (
                hg_lv[k] for k in ("pd", "ae", "dw", "wf", "lf", "kht", "tk", "ud", "sr", "oe", "dt", "pt"))
            with ExitStack() as c:
                W = sb("W", [P, 4, S], F32, c)
                AT = sb("AT", [P, TT, P], F32, c)
                KHT = sb("KHT", [P, 3, P], F32, c)
                ST = sb("ST", [P, 3, P], F32, c)
                EL = sb("EL", [P, 4], F32, c)
                SL = 10

                def head(ap, i, b):
                    return ap[:, bass.ds(i * 2 + b, 1), :].rearrange("p a s -> p (a s)")

                def w(b, n):
                    return W[:, (SL * b + n) % 4, :]

                def blocks(ap, lev):
                    return ap.rearrange("p (n c) -> p n c", c=P >> lev)

                def at(eng, s, i, per, k):
                    eng.wait_ge(s.h, i * (2 * per) + (s.base + k))
                with nc.Block() as block:
                    @block.gpsimd
                    def _(pool):
                        with pool.Fori(0, 4) as i:
                            for b in range(2):
                                g = head(LF, i, b)
                                for n in [0] + list(range(2, 9)):
                                    at(pool, WF, i, SL, SL * b + n - 3)
                                    pool.sem_inc(POOL_TICK.h, 1)
                                    if n == 0:
                                        g3 = g.rearrange("p (n c) -> p n c", c=P)
                                        x, y = g3[:, :, P - 1:P].to_broadcast([P, TT, P]), g3
                                        o = w(b, n).rearrange("p (n c) -> p n c", c=P)
                                    else:
                                        lev = n - 2
                                        g3, half = blocks(g, lev), P >> (lev + 1)
                                        x, y = g3, g3[:, :, half - 1:half].to_broadcast([P, S // (2 * half), 2 * half])
                                        o = blocks(w(b, n), lev)
                                    pool.tensor_tensor(o, x, y, ALU.subtract).then_inc(PD.h, 1)

                    @block.scalar
                    def _(act):
                        a = nc.scalar

                        def out(i, b):
                            at(act, WF, i, SL, SL * (b + 1))
                            a.activation(Y[:, :, bass.ds(i * 256 + P * b, P)], PS[6 + b][:, :].rearrange("p (n v) -> p n v", n=TT),
                                         ACT.Copy).then_inc(OE.h, 1)
                        with act.Fori(0, 4) as i:
                            for b in range(2):
                                for n in range(SL):
                                    if n in (1, 9):
                                        at(act, WF, i, SL, SL * b + n - 3)
                                    else:
                                        at(act, PD, i, 8, 8 * b + (1 if n == 0 else n))
                                    x = w(b, n)
                                    if n == 1:
                                        r = a.activation(x, head(KIN, i, b), ACT.Copy)
                                    elif n == 9:
                                        r = a.activation(x, head(LF, i, b), ACT.Exp)
                                    elif n == 0:
                                        r = a.activation(x, x, ACT.Exp)
                                    else:
                                        x3, half = blocks(x, n - 2), P >> (n - 1)
                                        a.activation(x3[:, :, 0:half], x3[:, :, 0:half], ACT.Exp, scale=-1.0)
                                        r = a.activation(x3[:, :, half:], x3[:, :, half:], ACT.Exp)
                                    r.then_inc(AE.h, 1)
                                    if n == 3:
                                        at(act, TK, i, 1, b + 1)
                                        a.activation(KHT[:, :, :], PS[4][:, 0:3 * P].rearrange("p (n k) -> p n k", n=3), ACT.Copy).then_inc(KHC.h, 1)
                                    if n == 5 and b == 1:
                                        out(i, 0)
                            out(i, 1)

                    @block.tensor
                    def _(pe):
                        with pe.Fori(0, 4) as i:
                            for b in range(2):
                                iv = lambda cc: IV[:, cc, bass.ds(i * 256 + P * b, P)]
                                for n in range(SL):
                                    x = w(b, n)
                                    if n == 0:
                                        at(pe, DW, i, 9, 9 * b + 1)
                                        at(pe, KHC, i, 1, b)
                                        for cc in range(3):
                                            r = nc.tensor.transpose(PS[4][:, P * cc:P * cc + P], x[:, P * cc:P * cc + P], ident[:, :])
                                        r.then_inc(TK.h, 1)
                                        continue
                                    if n < 9:
                                        if n == 1:
                                            at(pe, AE, i, SL, SL * b + 2)
                                        else:
                                            at(pe, DW, i, 9, 9 * b + n)
                                        k = n - 1
                                        at(pe, LVF, i, 8, 8 * b + k - 3)
                                        for cc in range(TT):
                                            cs = slice(P * cc, P * cc + P)
                                            rhs = QF[:, bass.ds(i * 2 + b, 1), cs].rearrange("p a s -> p (a s)") if n == 1 else x[:, cs]
                                            r = nc.tensor.matmul(PS[k % 4][:, cs], x[:, cs], rhs, start=True, stop=True)
                                        r.then_inc(WF.h, 2 if n == 1 else 1)
                                    if n == 5:
                                        at(pe, KHC, i, 1, b + 1)
                                        at(pe, SR, i, 1, b)
                                        for cc in range(3):
                                            r = nc.tensor.matmul(PS[5][:, P * cc:P * cc + P], KHT[:, cc, :], iv(cc), start=True, stop=True)
                                        r.then_inc(UD.h, 1)
                                    if n == 9:
                                        at(pe, DW, i, 9, 9 * b + 9)
                                        at(pe, SR, i, 1, b + 1)
                                        at(pe, OE, i, 1, b - 1)
                                        for cc in range(TT):
                                            cs = slice(P * cc, P * cc + P)
                                            r = nc.tensor.matmul(PS[6 + b][:, cs], AT[:, cc, :], iv(cc), start=True, stop=cc == 0)
                                            if cc:
                                                r = nc.tensor.matmul(PS[6 + b][:, cs], x[:, cs], ST[:, cc - 1, :], start=False, stop=True)
                                        r.then_inc(WF.h, 1)

                    @block.vector
                    def _(dve):
                        v = nc.vector
                        link = InOrder(dve, dve_order)
                        link(v.memset(AT[:, :, :], 0.0))
                        with dve.Fori(0, 4) as i:
                            link.enter(i, 2 * (1 + 7 + 2))
                            for b in range(2):
                                def merge(k):
                                    at(dve, WF, i, SL, SL * b + k + 2)
                                    dve.sem_inc(DVE_TICK.h, 1)
                                    lev = HG_LEVELS if k == 0 else k - 1
                                    v.copy_predicated(AT[:, :, :], masks[:, lev:lev + 1, :].to_broadcast([P, TT, P]),
                                                      PS[k % 4][:, :].rearrange("p (n t) -> p n t", n=TT)).then_inc(LVF.h, 1)
                                    at(dve, LVF, i, 8, 8 * b + k + 1)
                                for n in range(SL):
                                    x = w(b, n)
                                    if n != 1:
                                        at(dve, AE, i, SL, SL * b + n + 1)
                                    if n == 0:
                                        v.tensor_tensor(x, x, head(KIN, i, b), ALU.mult).then_inc(DW.h, 1)
                                    elif n == 9:
                                        link(v.tensor_copy(EL[:, :], x[:, P - 1::P]))
                                        v.tensor_tensor(x, x, head(QF, i, b), ALU.mult).then_inc(DW.h, 1)
                                    elif n >= 2:
                                        x3, half = blocks(x, n - 2), P >> (n - 1)
                                        kin, q = blocks(head(KIN, i, b), n - 2), blocks(head(QF, i, b), n - 2)
                                        link(v.tensor_tensor(x3[:, :, 0:half], x3[:, :, 0:half], kin[:, :, 0:half], ALU.mult))
                                        v.tensor_tensor(x3[:, :, half:], x3[:, :, half:], q[:, :, half:], ALU.mult).then_inc(DW.h, 1)
                                        merge(n - 2)
                                merge(7)
                                at(dve, UD, i, 1, b + 1)
                                link(v.tensor_copy(ST[:, 0, :], PS[5][:, 0:P]))
                                for cc in (1, 2):
                                    r = v.scalar_tensor_tensor(ST[:, cc, :], ST[:, cc - 1, :], EL[:, cc:cc + 1], PS[5][:, P * cc:P * cc + P], ALU.mult, ALU.add)
                                    if cc == 1:
                                        link(r)
                                r.then_inc(SR.h, 1)
                            link.leave(4)
                        link.done()
                for s, n in ((PD, 64), (AE, 80), (DW, 72), (WF, 80), (LVF, 64), (KHC, 8), (TK, 8), (UD, 8), (SR, 8), (OE, 8)):
                    s.base += n
        ssm_in = nc.dram_tensor("ssm_in", (P, SSM_PAIRS, 2, P), F32, kind="Internal").ap()
        ssm_out = nc.dram_tensor("ssm_out", (P, SSM_PAIRS, 4, P), F32, kind="Internal").ap()
        lag_kernel = nc.dram_tensor("lag_kernel", (SSM_C, 2 * SSM_PAIRS, 15 * SSM_C), F32, kind="Internal").ap()
        u_dram = nc.dram_tensor("u_dram", (D, S), F32, kind="Internal").ap()
        y_dram = nc.dram_tensor("y_dram", (D, S), F32, kind="Internal").ap()
        QP = 4
        ssm_sig = dict(ready=signal("ssm_ready"), w2t=signal("ssm_transposed"), w2c=signal("ssm_transposed_copied", CREDIT),
                        hd=signal("ssm_lags_done", CREDIT), hc=signal("ssm_lags_copied", CREDIT), st_=[signal(f"ssm_stored_{n}", CREDIT) for n in ("even", "odd")],
                        st2=signal("ssm_stored_lags", CREDIT), st3=signal("ssm_stored_out", CREDIT),
                        vin=signal("ssm_inputs_done"), vfree=signal("ssm_inputs_free", CREDIT), sprev=signal("ssm_states"),
                        yd=signal("ssm_y_done", CREDIT), yf=signal("ssm_y_free", CREDIT),
                        tick=signal("pe_tick"), uin=signal("ssm_u_in"), ld0=signal("ssm_loaded_even"), ld1=signal("ssm_loaded_odd"),
                        lo0=signal("ssm_out_loaded_even"), lo1=signal("ssm_out_loaded_odd"), uout=signal("ssm_u_for_out"))

        def ssm_mixer():
            with ExitStack() as c:
                E = sb("E", [P, 2, SSM_PAIRS, SSM_N], F32, c)
                RD = sb("RD", [P, SSM_PAIRS, SSM_N], F32, c)
                norm_phase("pre", gain=col[:, KT:2 * KT])
                ssm_prepare_and_project(E, RD)
                with ExitStack() as c2:
                    ssm_core(E, RD, c2)
            ssm_gate()
            split_features(lambda k: YF[:, k, :])

        def ssm_prepare_and_project(E, RD):
            c0 = pos[0]
            PASSES = SSM_PAIRS // QP
            PI2 = 2 * math.pi
            C1 = 6.28125
            C2 = float(np.float32(PI2 - C1))
            C3 = PI2 - C1 - C2
            MAGIC = 1.5 * 2 ** 23
            R, W2T_, W2C, HD, HC, ST1, ST2, ST3 = (ssm_sig[k] for k in ("ready", "w2t", "w2c", "hd", "hc", "st_", "st2", "st3"))
            with ExitStack() as c:
                A = sb("A", [P, 3, SSM_PAIRS], F32, c)
                BB = sb("BB", [P, 2, SSM_PAIRS, SSM_C], F32, c)
                CC = sb("CC", [P, 2, SSM_PAIRS, SSM_C], F32, c)
                s_ = sb("s_", [P, 16, SSM_PAIRS], F32, c)
                PW = sb("PW", [P, 2, 9, SSM_PAIRS], F32, c)
                PR = sb("PR", [P, 2, 8, SSM_PAIRS], F32, c)
                BQ = sb("BQ", [P, 2, 2, QP, SSM_C], F32, c)
                CA = sb("CA", [P, 2, 2, QP, 9, SSM_C], F32, c)
                UF = sb("UF", [P, KT, SSM_T, SSM_N], F32, c)
                W2 = sb("W2", [P, 2, QP, 8, SSM_C], F32, c)
                W2T = sb("W2T", [P, QP, 2, P], F32, c)
                T = sb("T", [P, 2, SSM_PAIRS * SSM_N // 2], F32, c)
                HS = sb("HS", [SSM_C, 2 * QP, 15 * SSM_C], F32, c)
                dcol = sb("dcol", [SSM_C, 2 * SSM_PAIRS], F32, c)
                eye = sb("eye", [SSM_C, SSM_C], F32, c)
                skip = sb("skip", [SSM_C, 2 * SSM_PAIRS, SSM_C], F32, c)
                n_loads = 9
                with nc.Block() as block:
                    @block.sync
                    def _(sp):
                        for d, x in ((A[:, 0, :], "ssm_a_re"), (A[:, 1, :], "ssm_a_im"), (A[:, 2, :], "ssm_log_dt"),
                                     (BB[:, 0], "ssm_b_re"), (BB[:, 1], "ssm_b_im"), (CC[:, 0], "ssm_c_re"), (CC[:, 1], "ssm_c_im"),
                                     (dcol[:, :], "ssm_d_rows"), (eye[:, :], "eye16")):
                            sp.dma_start(d, t[x]).then_inc(loaded.h, 16)

                        def lag_store(p, first):
                            sp.wait_ge(HC.h, p + (HC.base + 1))
                            sp.dma_start(lag_kernel[:, bass.ds(first, 2 * QP), :], HS[:, :, :]).then_inc(ST2.h, 16)

                        def one_pass(i, b):
                            load_chunk(sp, i * 2 + (c0 + SPLIT + RAW + b), (c0 + b) % RAW)
                            sp.wait_ge(R.h, i * 2 + (R.base + b + 1))
                            for x in range(2):
                                sp.dma_start(ssm_out[:, bass.ds(i * (2 * QP) + QP * b, QP), 2 + x, :].rearrange("p a (n c) -> p a n c", c=SSM_C),
                                             CA[:, b, x, :, 1:9, :]).then_inc(ST1[b].h, 16)
                            sp.wait_ge(W2C.h, i * 4 + (W2C.base + 2 * b + 2))
                            sp.dma_start(ssm_in[:, bass.ds(i * (2 * QP) + QP * b, QP)], W2T[:, :, :, :]).then_inc(ST3.h, 16)
                        one_pass(0, 0)
                        with sp.Fori(0, PASSES // 2 - 1) as i:
                            one_pass(i, 1)
                            lag_store(i * 2, i * (4 * QP))
                            load_chunk(sp, i * 2 + (c0 + SPLIT + RAW + 2), c0 % RAW)
                            sp.wait_ge(R.h, i * 2 + (R.base + 3))
                            for x in range(2):
                                sp.dma_start(ssm_out[:, bass.ds(i * (2 * QP) + 2 * QP, QP), 2 + x, :].rearrange("p a (n c) -> p a n c", c=SSM_C),
                                             CA[:, 0, x, :, 1:9, :]).then_inc(ST1[0].h, 16)
                            sp.wait_ge(W2C.h, i * 4 + (W2C.base + 6))
                            sp.dma_start(ssm_in[:, bass.ds(i * (2 * QP) + 2 * QP, QP)], W2T[:, :, :, :]).then_inc(ST3.h, 16)
                            lag_store(i * 2 + 1, i * (4 * QP) + 2 * QP)
                        one_pass(PASSES // 2 - 1, 1)
                        lag_store(PASSES - 2, (PASSES - 2) * 2 * QP)
                        lag_store(PASSES - 1, (PASSES - 1) * 2 * QP)
                        sp.wait_ge(ST2.h, ST2.base + 16 * PASSES)
                        for st_ in range(SSM_T):
                            src = lag_kernel[:, :, SSM_C * (7 - st_):SSM_C * (7 - st_) + P].rearrange("c (a g) n -> c a g n", g=2)
                            for g in range(2):
                                sp.dma_start(ssm_out[SSM_C * st_:SSM_C * st_ + SSM_C, :, g, :], src[:, :, g, :]).then_inc(stored.h, 16)
                        sp.wait_ge(stored.h, stored.base + 16 * 17)
                        for s1 in ST1:
                            sp.wait_ge(s1.h, s1.base + 16 * PASSES)
                        sp.wait_ge(ST3.h, ST3.base + 16 * PASSES)

                    @block.gpsimd
                    def _(pool):
                        pool_stream(pool, 8)

                    @block.scalar
                    def _(act):
                        a = nc.scalar
                        act.wait_ge(loaded.h, loaded.base + 16 * n_loads)
                        a.activation(s_[:, 0, :], A[:, 2, :], ACT.Exp).then_inc(a_b.h, 1)
                        act.wait_ge(b_a.h, b_a.base + 1)
                        a.activation(s_[:, 3, :], s_[:, 1, :], ACT.Exp)
                        a.activation(s_[:, 4, :], s_[:, 1, :], ACT.Exp, scale=float(SSM_T)).then_inc(a_b.h, 1)
                        act.wait_ge(b_a.h, b_a.base + 2)
                        a.activation(s_[:, 6, :], s_[:, 5, :], ACT.Sin)
                        a.activation(s_[:, 7, :], s_[:, 5, :], ACT.Sin, scale=0.5).then_inc(a_b.h, 1)

                        def take(i, b, d, z):
                            for m in range(2):
                                if m:
                                    act.wait_ge(w_used.h, i * 2 + (CREDIT + c0 + 2 * d + b + 1))
                                else:
                                    act.wait_ge(tile_done.h, i * 2 + (tile_done.base + 2 * d + b + 1))
                                if z:
                                    o = YF[:, bass.ds(i * 4 + (4 * d - 8 + 2 * b + m), 1), :].rearrange("p a s -> p (a s)")
                                    a.activation(o, PS[m][:, :], ACT.Copy).then_inc(tile_free.h, 1)
                                else:
                                    a.activation(UF[:, 4 * d + 2 * b + m], PS[m][:, :].rearrange("p (n s) -> p s n", s=SSM_T), ACT.Copy).then_inc(tile_free.h, 1)

                        def copy_v(i, b, d=0):
                            for n in range(2):
                                act.wait_ge(W2T_.h, i * 4 + (W2T_.base + 4 * d + 2 * b + n + 1))
                                if n == 0:
                                    act.wait_ge(ST3.h, i * 32 + (ST3.base + 32 * d + 16 * b))
                                a.activation(W2T[:, 2 * n:2 * n + 2, :, :].rearrange("p a b c -> p (a b c)"), PS[2 + n][:, :], ACT.Copy).then_inc(W2C.h, 1)
                        take(0, 0, 0, False)
                        take(0, 1, 0, False)
                        for b in range(2):
                            copy_v(0, b)
                            take(0, b, 1, False)
                        act.wait_ge(tile_free.h, tile_free.base + 8)
                        act.dma_start(u_dram.rearrange("(k p) s -> p k s", p=P), UF[:, :, :, :].rearrange("p k s n -> p k (s n)")).then_inc(stored.h, 16)
                        with act.Fori(0, 2) as i:
                            for b in range(2):
                                copy_v(i, b, 1)
                                take(i, b, 2, True)
                        for b in range(2):
                            copy_v(3, b)

                    @block.tensor
                    def _(pe):
                        def project(i, b, d):
                            pe.wait_ge(w_split.h, i * 2 + (c0 + 2 * d + b + 1))
                            for m in range(2):
                                pe.wait_ge(tile_free.h, i * 4 + (tile_free.base + 4 * d + 2 * b + m - 1))
                                r = f_tile(PS[m][:, :], (c0 + b) % SPLIT, m)
                                r.then_inc((w_used if m else tile_done).h, 1)

                        def products(i, b):
                            pe.wait_ge(R.h, i * 2 + (R.base + b + 1))
                            pe.wait_ge(W2C.h, i * 4 + (W2C.base + 2 * b))
                            for n in range(2):
                                for x in range(4):
                                    r = nc.tensor.transpose(PS[2 + n][:, P * x:P * x + P], W2[:, x % 2, 2 * n + x // 2].rearrange("p n c -> p (n c)"), ident[:, :])
                                r.then_inc(W2T_.h, 1)
                            pe.wait_ge(HC.h, i * 2 + (HC.base + b - 1))
                            pe.sem_inc(ssm_sig["tick"].h, 1)
                            for g in range(2 * QP):
                                lo, pr = 64 * (g % 2), g // 2
                                for x in range(2):
                                    r = nc.tensor.matmul(PS[4 + 2 * b + g % 2][0:SSM_C, P * pr:P * pr + P], BQ[lo:lo + 64, b, x, pr, :],
                                                         CA[lo:lo + 64, b, x, pr, 0:8, :].rearrange("p n c -> p (n c)"), start=x == 0, stop=x == 1)
                            r.then_inc(HD.h, 1)
                        project(0, 0, 0)
                        project(0, 1, 0)
                        with pe.Fori(0, PASSES // 2 - 1) as i:
                            for b in range(2):
                                products(i, b)
                                project(i, b, 1)
                        for b in range(2):
                            products(PASSES // 2 - 1, b)

                    @block.vector
                    def _(dve):
                        v = nc.vector
                        link = InOrder(dve, dve_order)

                        def mul(o, x, y):
                            link(v.tensor_tensor(o, x, y, ALU.mult))

                        def cmul(o, x, y, t1, t2, negate_im=False):
                            mul(t1, x[0], y[0])
                            mul(t2, x[1], y[1])
                            link(v.tensor_tensor(o[0], t1, t2, ALU.subtract))
                            mul(t1, x[0], y[1])
                            mul(t2, x[1], y[0])
                            if negate_im:
                                link(v.tensor_scalar(t1, t1, -1.0, None, ALU.mult))
                            link(v.tensor_tensor(o[1], t1, t2, ALU.subtract if negate_im else ALU.add))
                        sm = lambda k: s_[:, k, :]
                        dve.wait_ge(loaded.h, loaded.base + 16 * n_loads)
                        link(v.memset(HS[:, :, 0:7 * SSM_C], 0.0))
                        link(v.tensor_tensor(skip[:, :, :], eye[:, :].unsqueeze(1).to_broadcast([SSM_C, 2 * SSM_PAIRS, SSM_C]),
                                             dcol[:, :].unsqueeze(2).to_broadcast([SSM_C, 2 * SSM_PAIRS, SSM_C]), ALU.mult))
                        dve.wait_ge(a_b.h, a_b.base + 1)
                        v.tensor_tensor(sm(1), A[:, 0, :], sm(0), ALU.mult).then_inc(b_a.h, 1)
                        mul(sm(2), A[:, 1, :], sm(0))
                        link(v.tensor_scalar(sm(8), sm(2), 1.0 / PI2, None, ALU.mult))
                        link(v.tensor_scalar(sm(8), sm(8), MAGIC, None, ALU.add))
                        link(v.tensor_scalar(sm(8), sm(8), -MAGIC, None, ALU.add))
                        link(v.scalar_tensor_tensor(sm(2), sm(8), -C1, sm(2), ALU.mult, ALU.add))
                        link(v.scalar_tensor_tensor(sm(2), sm(8), -C2, sm(2), ALU.mult, ALU.add))
                        link(v.scalar_tensor_tensor(sm(2), sm(8), -C3, sm(2), ALU.mult, ALU.add))
                        v.tensor_scalar(sm(5), sm(2), math.pi, -math.pi, ALU.min, ALU.max).then_inc(b_a.h, 1)
                        dve.wait_ge(a_b.h, a_b.base + 3)
                        mul(sm(8), sm(7), sm(7))
                        link(v.tensor_scalar(sm(9), sm(8), -2.0, 1.0, ALU.mult, ALU.add))
                        pw = lambda n, m=1: (PW[:, 0, n:n + m, :], PW[:, 1, n:n + m, :])
                        link(v.memset(PW[:, 0, 0:1, :], 1.0))
                        link(v.memset(PW[:, 1, 0:1, :], 0.0))
                        mul(PW[:, 0, 1, :], sm(3), sm(9))
                        mul(PW[:, 1, 1, :], sm(3), sm(6))
                        tw = lambda m: tuple(T[:, x, 0:m * SSM_PAIRS].rearrange("p (n a) -> p n a", n=m) for x in range(2))
                        for m in (1, 2, 4):
                            top = tuple(x.to_broadcast([P, m, SSM_PAIRS]) for x in pw(m))
                            cmul(pw(m + 1, m), pw(1, m), top, *tw(m))
                        for n in range(8):
                            link(v.tensor_copy(PR[:, :, n, :], PW[:, :, 7 - n, :]))
                        link(v.tensor_scalar(sm(10), PW[:, 0, 1, :], -1.0, None, ALU.add))
                        mul(sm(11), A[:, 0, :], A[:, 0, :])
                        mul(sm(12), A[:, 1, :], A[:, 1, :])
                        link(v.tensor_tensor(sm(11), sm(11), sm(12), ALU.add))
                        link(v.reciprocal(sm(11), sm(11)))
                        mul(sm(12), sm(10), A[:, 0, :])
                        mul(sm(13), PW[:, 1, 1, :], A[:, 1, :])
                        link(v.tensor_tensor(sm(12), sm(12), sm(13), ALU.add))
                        mul(sm(12), sm(12), sm(11))
                        mul(sm(13), PW[:, 1, 1, :], A[:, 0, :])
                        mul(sm(14), sm(10), A[:, 1, :])
                        link(v.tensor_tensor(sm(13), sm(13), sm(14), ALU.subtract))
                        mul(sm(13), sm(13), sm(11))

                        def operands(i, d, b, waits):
                            pr = bass.ds(i * (2 * QP) + QP * (2 * d + b), QP)
                            if waits:
                                dve.wait_ge(ST1[b].h, i * 32 + (ST1[b].base + 32 * d))
                                dve.wait_ge(HD.h, i * 2 + (HD.base + 2 * d + b - 1))
                                dve.wait_ge(W2T_.h, i * 4 + (W2T_.base + 2 * (2 * d + b)))
                            bb = [BB[:, x, pr, :] for x in range(2)]
                            ff = [s_[:, 12 + x, pr].unsqueeze(2).to_broadcast([P, QP, SSM_C]) for x in range(2)]
                            tb = [T[:, x, 0:QP * SSM_C].rearrange("p (a c) -> p a c", c=SSM_C) for x in range(2)]
                            cmul((BQ[:, b, 0], BQ[:, b, 1]), ff, bb, *tb)
                            sh = [P, QP, 9, SSM_C]
                            aa = [PW[:, x, :, pr].rearrange("p n a -> p a n").unsqueeze(3).to_broadcast(sh) for x in range(2)]
                            cc = [CC[:, x, pr, :].unsqueeze(2).to_broadcast(sh) for x in range(2)]
                            t9 = [T[:, x, 0:QP * 9 * SSM_C].rearrange("p (a n c) -> p a n c", n=9, c=SSM_C) for x in range(2)]
                            cmul((CA[:, b, 0], CA[:, b, 1]), aa, cc, *t9, negate_im=True)
                            sh = [P, QP, 8, SSM_C]
                            aa = [PR[:, x, :, pr].rearrange("p n a -> p a n").unsqueeze(3).to_broadcast(sh) for x in range(2)]
                            cc = [BQ[:, b, x].unsqueeze(2).to_broadcast(sh) for x in range(2)]
                            t8 = [T[:, x, 0:QP * P].rearrange("p (a n c) -> p a n c", n=8, c=SSM_C) for x in range(2)]
                            cmul((W2[:, 0], W2[:, 1]), aa, cc, *t8)
                            dve.sem_inc(R.h, 1)

                        def kernels(i, b):
                            dve.wait_ge(HD.h, i * 2 + (HD.base + b + 1))
                            dve.wait_ge(ST2.h, i * 32 + (ST2.base + 16 * b))
                            for n in range(2):
                                link(v.tensor_copy(HS[:, n:n + 2 * QP - 1:2, 7 * SSM_C:], PS[4 + 2 * b + n][0:SSM_C, :].rearrange("p (g n) -> p g n", g=QP)))
                            lag0 = HS[:, :, 7 * SSM_C:8 * SSM_C]
                            link(v.tensor_tensor(lag0, lag0, skip[:, bass.ds(i * (4 * QP) + 2 * QP * b, 2 * QP), :], ALU.add))
                            dve.sem_inc(HC.h, 1)
                        operands(0, 0, 0, False)
                        with dve.Fori(0, PASSES // 2 - 1) as i:
                            link.enter(i, 2 * (6 + 7 + 6 + 3))
                            operands(i, 0, 1, True)
                            kernels(i, 0)
                            operands(i, 1, 0, True)
                            kernels(i, 1)
                            link.leave(PASSES // 2 - 1)
                        operands(PASSES // 2 - 1, 0, 1, True)
                        for b in range(2):
                            kernels(PASSES // 2 - 1, b)
                        u = [(sm(9), sm(6)), (sm(10), sm(11)), (sm(12), sm(13))]
                        t2 = (sm(14), sm(15))
                        cur = u[0]
                        for k in range(3):
                            nxt = u[1 + k % 2]
                            cmul(nxt, cur, cur, *t2)
                            cur = nxt
                        link(v.memset(E[:, 0, :, 0:1], 1.0))
                        link(v.memset(E[:, 1, :, 0:1], 0.0))
                        for k in range(6):
                            m = 1 << k
                            cu = tuple(x.unsqueeze(2).to_broadcast([P, SSM_PAIRS, m]) for x in cur)
                            tt_ = tuple(T[:, x, 0:SSM_PAIRS * m].rearrange("p (a n) -> p a n", n=m) for x in range(2)) if m <= 32 else None
                            cmul(tuple(E[:, x, :, m:2 * m] for x in range(2)), tuple(E[:, x, :, 0:m] for x in range(2)), cu, *tt_)
                            nxt = u[1 + (k + 1) % 2]
                            cmul(nxt, cur, cur, *t2)
                            cur = nxt
                        link(v.tensor_copy(RD[:, :, :], sm(4).unsqueeze(2).to_broadcast([P, SSM_PAIRS, SSM_N])))
                        link(v.memset(RD[:, :, 0:1], 0.0))
                        link.done()
                loaded.base += 16 * n_loads
                a_b.base += 3
                b_a.base += 2
                R.base += PASSES
                for s1 in ST1:
                    s1.base += 16 * PASSES
                ST2.base += 16 * PASSES
                ST3.base += 16 * PASSES
                W2C.base += 2 * PASSES
                W2T_.base += 2 * PASSES
                HD.base += PASSES
                HC.base += PASSES
                tile_free.base += 16
                tile_done.base += 8
                pos[0] += 8
                stored.base += 16
                stored.base += 256

        def ssm_core(E, RD, c):
            VIN, VFREE, SPREV, YD, YFR = (ssm_sig[k] for k in ("vin", "vfree", "sprev", "yd", "yf"))
            LD = [ssm_sig["ld0"], ssm_sig["ld1"]]
            LO = [ssm_sig["lo0"], ssm_sig["lo1"]]
            UIN, UOUT = ssm_sig["uin"], ssm_sig["uout"]
            FP = 4
            U = sb("U", [P, 2 * SSM_PAIRS, SSM_N], F32, c)
            UI = sb("UI", [P, 2, 2 * FP, SSM_N], F32, c)
            UO = sb("UO", [P, 2, 2 * FP, SSM_N], F32, c)
            YG = U
            MI = sb("MI", [P, 2, FP, 2, P], F32, c)
            MO = sb("MO", [P, 2, FP, 4, P], F32, c)
            SP_ = sb("SP_", [P, 2, 2, FP, SSM_N], F32, c)
            Z = sb("Z", [P, 2, FP, SSM_N], F32, c)
            T = sb("T2", [P, 2, FP, SSM_N], F32, c)
            with nc.Block() as block:
                @block.sync
                def _(sp):
                    for s in range(SSM_T):
                        sp.dma_start(U[SSM_C * s:SSM_C * s + SSM_C, :, :],
                                     u_dram.rearrange("(g c) (s n) -> s c g n", c=SSM_C, s=SSM_T)[s]).then_inc(loaded.h, 16)

                    def load_in(p, b):
                        sp.dma_start(MI[:, b], ssm_in[:, bass.ds(p, FP)]).then_inc(LD[b].h, 16)

                    def load_out(p, b):
                        sp.dma_start(MO[:, b], ssm_out[:, bass.ds(p, FP)]).then_inc(LO[b].h, 16)
                    for b in range(2):
                        load_in(FP * b, b)
                        load_out(FP * b, b)
                    with sp.Fori(0, 3) as i:
                        for b in range(2):
                            sp.wait_ge(VIN.h, i * 2 + (VIN.base + b + 1))
                            load_in(i * 8 + (8 + FP * b), b)
                            sp.wait_ge(YD.h, i * 2 + (YD.base + b + 1))
                            load_out(i * 8 + (8 + FP * b), b)

                @block.scalar
                def _(act):
                    a = nc.scalar
                    act.wait_ge(loaded.h, loaded.base + 16 * SSM_T)

                    def copy_u(dst, b, g, sig):
                        a.activation(dst[:, b].rearrange("p g n -> p (g n)"), U[:, bass.ds(g, 8), :].rearrange("p g n -> p (g n)"),
                                     ACT.Copy).then_inc(sig.h, 1)

                    def evacuate(i, b):
                        act.wait_ge(YD.h, i * 2 + (YD.base + b + 1))
                        yg = YG[:, :, :].rearrange("p (a g) n -> p a g n", g=2)
                        for g in range(2):
                            r = a.activation(yg[:, bass.ds(i * 8 + FP * b, FP), g, :], PS[4 + b + 2 * g][:, 0:256].rearrange("p (a n) -> p a n", a=FP), ACT.Copy)
                        r.then_inc(YFR.h, 1)
                    for b in range(2):
                        copy_u(UI, b, 8 * b, UIN)
                        copy_u(UO, b, 8 * b, UOUT)
                    with act.Fori(0, 3) as i:
                        for b in range(2):
                            act.wait_ge(VIN.h, i * 2 + (VIN.base + b + 1))
                            copy_u(UI, b, i * 16 + (16 + 8 * b), UIN)
                            evacuate(i, b)
                            copy_u(UO, b, i * 16 + (16 + 8 * b), UOUT)
                    for b in range(2):
                        evacuate(3, b)
                    act.wait_ge(YFR.h, YFR.base + 8)
                    for s in range(SSM_T):
                        act.dma_start(y_dram.rearrange("(g c) (s n) -> s c g n", c=SSM_C, s=SSM_T)[s],
                                      YG[SSM_C * s:SSM_C * s + SSM_C, :, :]).then_inc(stored.h, 16)
                    act.wait_ge(stored.h, stored.base + 16 * SSM_T)

                @block.tensor
                def _(pe):
                    def inputs(i, b, ahead):
                        pe.wait_ge(UIN.h, i * 2 + (UIN.base + 2 * ahead + b + 1))
                        pe.wait_ge(LD[b].h, i * 16 + (LD[b].base + 16 * ahead + 16))
                        pe.wait_ge(VFREE.h, i * 2 + (VFREE.base + 2 * ahead + b - 1))
                        for x in range(2):
                            for g in range(2 * FP):
                                lo = 64 * (g % 2)
                                r = nc.tensor.matmul(PS[b][lo:lo + 64, 256 * x + 64 * (g // 2):256 * x + 64 * (g // 2) + 64],
                                                     MI[:, b, g // 2, x, lo:lo + 64],
                                                     UI[:, b, g, :], start=True, stop=True)
                        r.then_inc(VIN.h, 1)

                    def outputs(i, b):
                        pe.wait_ge(UOUT.h, i * 2 + (UOUT.base + b + 1))
                        pe.wait_ge(LO[b].h, i * 16 + (LO[b].base + 16))
                        pe.wait_ge(SPREV.h, i * 2 + (SPREV.base + b + 1))
                        pe.wait_ge(YFR.h, i * 2 + (YFR.base + b - 1))
                        for g in range(2 * FP):
                            lo, o = 64 * (g % 2), PS[4 + b + 2 * (g % 2)][:, 64 * (g // 2):64 * (g // 2) + 64]
                            nc.tensor.matmul(o, MO[:, b, g // 2, g % 2, :], UO[:, b, g, :], start=True, stop=False)
                            for x in range(2):
                                r = nc.tensor.matmul(o, MO[lo:lo + 64, b, g // 2, 2 + x, :], SP_[lo:lo + 64, b, x, g // 2, :], start=False, stop=x == 1)
                        r.then_inc(YD.h, 1)
                    inputs(0, 0, 0)
                    inputs(0, 1, 0)
                    with pe.Fori(0, 3) as i:
                        for b in range(2):
                            outputs(i, b)
                            inputs(i, b, 1)
                    for b in range(2):
                        outputs(3, b)

                @block.vector
                def _(dve):
                    v = nc.vector
                    link = InOrder(dve, dve_order)
                    link(v.memset(SP_[:, :, :, :, 0:1].rearrange("p a b c d -> p (a b) (c d)"), 0.0))
                    with dve.Fori(0, 4) as i:
                        link.enter(i, 2 * 13)
                        for b in range(2):
                            pr = bass.ds(i * 8 + FP * b, FP)
                            er, ei = (E[:, x, pr, :] for x in range(2))
                            vr, vi = (PS[b][:, 256 * x:256 * x + 256].rearrange("p (a n) -> p a n", a=FP) for x in range(2))
                            t0, t1 = T[:, 0], T[:, 1]
                            dve.wait_ge(VIN.h, i * 2 + (VIN.base + b + 1))
                            link(v.tensor_tensor(t0, vr, er, ALU.mult))
                            link(v.tensor_tensor(t1, vi, ei, ALU.mult))
                            link(v.tensor_tensor(Z[:, 0], t0, t1, ALU.add))
                            link(v.tensor_tensor(t0, vi, er, ALU.mult))
                            v.tensor_tensor(t1, vr, ei, ALU.mult).then_inc(VFREE.h, 1)
                            dve.wait_ge(VFREE.h, i * 2 + (VFREE.base + b + 1))
                            link(v.tensor_tensor(Z[:, 1], t0, t1, ALU.subtract))
                            rd = RD[:, pr, :].rearrange("p a n -> p (a n)")
                            for x in range(2):
                                z = Z[:, x].rearrange("p a n -> p (a n)")
                                link(v.tensor_tensor_scan(z, rd, z, 0.0, ALU.mult, ALU.add))
                            n1 = slice(0, SSM_N - 1)
                            er, ei = (E[:, x, pr, n1] for x in range(2))
                            z0, z1, t0, t1 = Z[:, 0, :, n1], Z[:, 1, :, n1], T[:, 0, :, n1], T[:, 1, :, n1]
                            link(v.tensor_tensor(t0, z0, er, ALU.mult))
                            link(v.tensor_tensor(t1, z1, ei, ALU.mult))
                            dve.wait_ge(YD.h, i * 2 + (YD.base + b - 1))
                            link(v.tensor_tensor(SP_[:, b, 0, :, 1:], t0, t1, ALU.subtract))
                            link(v.tensor_tensor(t0, z0, ei, ALU.mult))
                            link(v.tensor_tensor(t1, z1, er, ALU.mult))
                            link(v.tensor_tensor(SP_[:, b, 1, :, 1:], t0, t1, ALU.add))
                            dve.sem_inc(SPREV.h, 1)
                        link.leave(4)
                    link.done()
            loaded.base += 16 * SSM_T
            stored.base += 16 * SSM_T
            for s in (VIN, VFREE, SPREV, YD, YFR, UIN, UOUT):
                s.base += 8
            for s in LD + LO:
                s.base += 64

        def ssm_gate():
            c0 = pos[0]
            with ExitStack() as c:
                GF = sb("GF", [P, KT, S], F32, c)
                SG = sb("SG", [P, 2, S], F32, c)
                bcol = sb("bcol", [P, KT], F32, c)
                with nc.Block() as block:
                    @block.sync
                    def _(sp):
                        sp.dma_start(GF[:, :, :], y_dram.rearrange("(k p) s -> p k s", p=P)).then_inc(loaded.h, 16)
                        sp.dma_start(bcol[:, :], t["ssm_b_glu"]).then_inc(loaded.h, 16)
                        sp_stream(sp, 4)

                    @block.gpsimd
                    def _(pool):
                        pool_stream(pool, 4)

                    @block.tensor
                    def _(pe):
                        for n in range(8):
                            if n % 2 == 0:
                                arrived(pe, c0 + n // 2)
                            if n == 0:
                                pe.wait_ge(b_p.h, b_p.base + 8)
                            pe.wait_ge(tile_free.h, tile_free.base + n - 3)
                            r = f_tile(PS[n % 4][:, :], (c0 + n // 2) % SPLIT, n % 2)
                            r.then_inc((w_used if n % 2 else tile_done).h, 1)

                    @block.scalar
                    def _(act):
                        a = nc.scalar
                        for n in range(8):
                            if n >= 2:
                                act.wait_ge(b_a.h, b_a.base + n - 1)
                            a.activation(SG[:, n % 2, :], YF[:, n, :], ACT.Sigmoid).then_inc(a_b.h, 1)
                        act.wait_ge(loaded.h, loaded.base + 32)
                        for n in range(8):
                            a.activation(GF[:, n, :], GF[:, n, :], ACT.Gelu_apprx_tanh).then_inc(a_b.h, 1)
                            act.wait_ge(a_b.h, a_b.base + 8 + 2 * n + 1)
                            a.activation(XTh[:, n, :], GF[:, n, :], ACT.Copy).then_inc(a_b.h, 1)
                        for n in range(8):
                            if n % 2:
                                act.wait_ge(w_used.h, CREDIT + c0 + n // 2 + 1)
                            else:
                                act.wait_ge(tile_done.h, tile_done.base + n // 2 + 1)
                            act.wait_ge(b_a.h, b_a.base + 8 + n - 1)
                            a.activation(SG[:, n % 2, :], PS[n % 4][:, :], ACT.Sigmoid, bias=bcol[:, n:n + 1]).then_inc(tile_free.h, 1)

                    @block.vector
                    def _(dve):
                        v = nc.vector
                        link = InOrder(dve, dve_order)
                        for n in range(8):
                            dve.wait_ge(a_b.h, a_b.base + n + 1)
                            v.tensor_tensor(YF[:, n, :], YF[:, n, :], SG[:, n % 2, :], ALU.mult).then_inc(b_a.h, 1)
                        dve.wait_ge(b_a.h, b_a.base + 8)
                        for n in range(8):
                            dve.wait_ge(a_b.h, a_b.base + 8 + 2 * n + 2)
                            v.tensor_tensor(XTl[:, n, :], GF[:, n, :], XTh[:, n, :].bitcast(F32), ALU.subtract).then_inc(b_p.h, 1)
                        for n in range(8):
                            dve.wait_ge(tile_free.h, tile_free.base + n + 1)
                            link(v.tensor_tensor(SG[:, n % 2, :], SG[:, n % 2, :], GF[:, n, :], ALU.mult))
                            y = YF[:, n, :].rearrange("p (n s) -> p n s", s=SSM_T)
                            v.tensor_tensor(y, y, SG[:, n % 2, :].rearrange("p (s n) -> p n s", s=SSM_T), ALU.mult).then_inc(b_a.h, 1)
                        link.done()
            loaded.base += 32
            a_b.base += 24
            b_a.base += 16
            b_p.base += 8
            tile_free.base += 8
            tile_done.base += 4
            pos[0] += 4

        with ExitStack() as b_scope:
            with ExitStack() as a_scope:
                setup(a_scope, b_scope)
                if "attn" in STAGES:
                    norm_phase("pre", gain=col[:, 0:KT], before_end=wait_bias_a_stored)
                else:
                    norm_phase("plain", before_end=wait_bias_stored)
            if "attn" in STAGES:
                dilated_attention()
        if "attn" in STAGES:
            out_phase(None, (t["attn_post_norm"][0],), False)
        if "ssm" in STAGES:
            ssm_mixer()
            out_phase(None, (t["ssm_post_norm"][0],), "layer0" in STAGES)
        for layer in range(N_LAYERS):
            if f"layer{layer}" not in STAGES:
                continue
            if layer or "ssm" not in STAGES:
                norm_phase("plain")
            kind, j = layer % 3, layer // 3
            if kind == 0:
                diff_attention(layer, j)
            elif kind == 1:
                hgrn(layer, j)
            else:
                sliding_attention()
            out_phase(ALPHA, (t["ln_g_2"][layer, 0], t["ln_b_2"][layer, 0]))
            ffn_phase((t["ln_g_2"][layer, 1], t["ln_b_2"][layer, 1]))
            ple_phase(layer)
        assert pos[0] == NCH, (pos[0], NCH)
        final_store()


def column(v):
    return np.ascontiguousarray(np.asarray(v).reshape(-1, P).T)


def kernel(**inputs):
    import concourse.bacc as bacc
    from concourse.bass_utils import run_bass_kernel_spmd

    i = {k: np.asarray(v) for k, v in inputs.items()}
    onehot_a, onehot_b = bias_constants()
    arrays = {
        "x": i["x"], "weights": pack_weights(i), "onehot_a": onehot_a, "onehot_b": onehot_b,
        "rel_bias": i["rel_bias"], "rel_bias_2": i["rel_bias_2"],
        "attn_pre_norm": column(i["attn_pre_norm"]), "ssm_pre_norm": column(i["ssm_pre_norm"]),
        "da_subln_2": column(i["da_subln_2"]), "hg_gnorm_2": column(i["hg_gnorm_2"]),
        "attn_post_norm": i["attn_post_norm"], "ssm_post_norm": i["ssm_post_norm"],
        "ln_g_2": i["ln_g_2"], "ln_b_2": i["ln_b_2"],
        "head_select": head_select(),
        "p_2": np.ascontiguousarray(i["p_2"][:, 0].transpose(0, 2, 1)),
        "da_lambda_2": i["da_lambda_2"],
        "sw_sinks_2": np.ascontiguousarray(i["sw_sinks_2"][:, SW_ORDER]),
        "hg_lower_bound_2": np.ascontiguousarray(i["hg_lower_bound_2"].reshape(N_LAYERS, 8, P).transpose(2, 0, 1)),
        "hg_masks": hg_masks(),
        "ssm_a_re": np.ascontiguousarray(i["ssm_a_re"][0].reshape(32, 2, 64).transpose(1, 2, 0).reshape(P, 32)),
        "ssm_a_im": np.ascontiguousarray(i["ssm_a_im"][0].reshape(32, 2, 64).transpose(1, 2, 0).reshape(P, 32)),
        "ssm_log_dt": np.ascontiguousarray(np.repeat(i["ssm_log_dt"][0].reshape(32, 2).T, 64, axis=0)),
        "ssm_b_re": np.ascontiguousarray(i["ssm_b_re"][0].reshape(32, 2, 64, 16).transpose(1, 2, 0, 3).reshape(P, 32, 16)),
        "ssm_b_im": np.ascontiguousarray(i["ssm_b_im"][0].reshape(32, 2, 64, 16).transpose(1, 2, 0, 3).reshape(P, 32, 16)),
        "ssm_c_re": np.ascontiguousarray(i["ssm_c_re"][0].reshape(32, 2, 16, 64).transpose(1, 3, 0, 2).reshape(P, 32, 16)),
        "ssm_c_im": np.ascontiguousarray(i["ssm_c_im"][0].reshape(32, 2, 16, 64).transpose(1, 3, 0, 2).reshape(P, 32, 16)),
        "ssm_d_rows": np.ascontiguousarray(i["ssm_d"][0].reshape(64, SSM_C).T), "eye16": np.eye(SSM_C, dtype=np.float32),
        "ssm_b_glu": column(i["ssm_b_glu"]),
    }
    nc = bacc.Bacc("TRN2", target_bir_lowering=False, num_devices=1)
    t = {k: nc.dram_tensor("in_" + k, v.shape, mybir.dt.from_np(v.dtype), kind="ExternalInput").ap() for k, v in arrays.items()}
    out = nc.dram_tensor("out_0", (1, S, D), F32, kind="ExternalOutput").ap()
    build(nc, t, out)
    r = run_bass_kernel_spmd(nc, [{"in_" + k: v for k, v in arrays.items()}], core_ids=[0])
    return r.results[0]["out_0"]
```
